# Optimizing a Trainium2 kernel written in Bass

```python
import math
import jax, jax.numpy as jnp
from jax import lax
import numpy as np
import jax
import jax.numpy as jnp

D_MODEL = 1024
BATCH = 1
SEQ = 512
DEPTH = 2

N_META = 16
MIX_WIDTH = D_MODEL
DIFF_WIDTH = MIX_WIDTH // 2
FOX_WIDTH = MIX_WIDTH - DIFF_WIDTH
DIFF_QK_DIM = 64
DIFF_V_DIM = 2 * DIFF_QK_DIM
DIFF_HEADS = DIFF_WIDTH // DIFF_V_DIM
FOX_HEAD_DIM = 64
FOX_HEADS = FOX_WIDTH // FOX_HEAD_DIM
ROPE_THETA = 10000.0
Q_BLOCK = 128
NORM_EPS = 1e-6
SPLITS = (DIFF_HEADS * 2 * DIFF_QK_DIM, DIFF_HEADS * 2 * DIFF_QK_DIM, DIFF_WIDTH, DIFF_WIDTH,
          FOX_WIDTH, FOX_WIDTH, FOX_WIDTH, FOX_WIDTH, FOX_HEADS)
PROJ_WIDTH = sum(SPLITS)


def rms_norm(x, g):
    xf = x.astype(jnp.float32)
    y = xf * lax.rsqrt(jnp.mean(xf * xf, axis=-1, keepdims=True) + NORM_EPS)
    return (y * g.astype(jnp.float32)).astype(x.dtype)

def rope(t, pos):
    half = t.shape[-1] // 2
    inv = ROPE_THETA ** (-jnp.arange(half, dtype=jnp.float32) / half)
    ang = pos.astype(jnp.float32)[:, None] * inv[None, :]
    cos, sin = jnp.cos(ang), jnp.sin(ang)
    tf = t.astype(jnp.float32)
    t1, t2 = tf[..., :half], tf[..., half:]
    return jnp.concatenate([t1 * cos - t2 * sin, t2 * cos + t1 * sin], axis=-1).astype(t.dtype)

def sweep_query_blocks(block_fn, q_parts, pos):
    meta_out = block_fn(tuple(q[:, :, :N_META] for q in q_parts), pos[:N_META])

    def to_blocks(q):
        b, h, _, d = q.shape
        return jnp.moveaxis(q[:, :, N_META:].reshape(b, h, -1, Q_BLOCK, d), 2, 0)

    blocks = tuple(to_blocks(q) for q in q_parts)
    pos_blocks = pos[N_META:].reshape(-1, Q_BLOCK)
    outs = lax.map(lambda a: block_fn(a[0], a[1]), (blocks, pos_blocks))
    nb, b, h, t, dv = outs.shape
    real = jnp.moveaxis(outs, 0, 2).reshape(b, h, nb * t, dv)
    return jnp.concatenate([meta_out, real], axis=2)

def hybrid_layer(h, pos, norm_g, w_in, b_forget, lam_q1, lam_k1, lam_q2, lam_k2,
                 subln_g, w_out, lambda_init):
    bsz, length, _ = h.shape
    u = rms_norm(h, norm_g)
    proj = jnp.einsum('bld,dp->blp', u, w_in)
    split_points = np.cumsum(SPLITS)[:-1].tolist()
    dq, dk, dv, dz, fq, fk, fv, fz, f_logit = jnp.split(proj, split_points, axis=-1)

    def diff_qk(t):
        t = t.reshape(bsz, length, DIFF_HEADS, 2, DIFF_QK_DIM).transpose(3, 0, 2, 1, 4)
        return rope(t[0], pos), rope(t[1], pos)

    q1, q2 = diff_qk(dq)
    k1, k2 = diff_qk(dk)
    v_a = dv.reshape(bsz, length, DIFF_HEADS, DIFF_V_DIM).transpose(0, 2, 1, 3)
    lam = (jnp.exp(jnp.sum(lam_q1.astype(jnp.float32) * lam_k1.astype(jnp.float32)))
           - jnp.exp(jnp.sum(lam_q2.astype(jnp.float32) * lam_k2.astype(jnp.float32)))
           + lambda_init)
    d_scale = DIFF_QK_DIM ** -0.5

    def diff_block(qs, qpos):
        qa, qc = qs
        mask = pos[None, :] <= qpos[:, None]

        def probs(q, k):
            s = jnp.einsum('bhqd,bhkd->bhqk', q, k).astype(jnp.float32) * d_scale
            return jax.nn.softmax(jnp.where(mask, s, -jnp.inf), axis=-1)

        p = probs(qa, k1) - lam * probs(qc, k2)
        return jnp.einsum('bhqk,bhkd->bhqd', p.astype(v_a.dtype), v_a)

    o_a = sweep_query_blocks(diff_block, (q1, q2), pos)
    o_a = rms_norm(o_a, subln_g.reshape(DIFF_HEADS, 1, DIFF_V_DIM)) * (1.0 - lambda_init)
    o_a = o_a.transpose(0, 2, 1, 3).reshape(bsz, length, DIFF_WIDTH)

    def fox_heads(t):
        return t.reshape(bsz, length, FOX_HEADS, FOX_HEAD_DIM).transpose(0, 2, 1, 3)

    q_f, k_f, v_f = fox_heads(fq), fox_heads(fk), fox_heads(fv)
    log_f = jax.nn.log_sigmoid(f_logit.astype(jnp.float32) + b_forget.astype(jnp.float32))
    cum = jnp.cumsum(log_f, axis=1).transpose(0, 2, 1)
    f_scale = FOX_HEAD_DIM ** -0.5

    def fox_block(qs, qpos):
        q, c_q = qs
        mask = pos[None, :] <= qpos[:, None]
        s = (jnp.einsum('bhqd,bhkd->bhqk', q, k_f).astype(jnp.float32) * f_scale
             + c_q - cum[:, :, None, :])
        p = jax.nn.softmax(jnp.where(mask, s, -jnp.inf), axis=-1)
        return jnp.einsum('bhqk,bhkd->bhqd', p.astype(v_f.dtype), v_f)

    o_b = sweep_query_blocks(fox_block, (q_f, cum[..., None]), pos)
    o_b = o_b.transpose(0, 2, 1, 3).reshape(bsz, length, FOX_WIDTH)

    mixed = jnp.concatenate([o_a * jax.nn.silu(dz), o_b * jax.nn.silu(fz)], axis=-1)
    return h + jnp.einsum('blm,md->bld', mixed, w_out)

def first_inputs(seed: int = 0) -> dict:
    key = jax.random.key(seed)
    ks = jax.random.split(key, 14)
    f32 = jnp.float32
    x = jax.random.normal(ks[0], (BATCH, SEQ, D_MODEL), f32)
    meta_tokens = jax.random.normal(ks[1], (N_META, D_MODEL), f32)
    norm_g = 1.0 + 0.02 * jax.random.normal(ks[2], (DEPTH, D_MODEL), f32)
    w_in = jax.random.normal(ks[3], (DEPTH, D_MODEL, PROJ_WIDTH), f32) * D_MODEL ** -0.5
    b_forget = (jnp.linspace(1.0, 6.0, FOX_HEADS, dtype=f32)[None, :]
                + 0.1 * jax.random.normal(ks[4], (DEPTH, FOX_HEADS), f32))
    lam_q1 = 0.1 * jax.random.normal(ks[5], (DEPTH, DIFF_QK_DIM), f32)
    lam_k1 = 0.1 * jax.random.normal(ks[6], (DEPTH, DIFF_QK_DIM), f32)
    lam_q2 = 0.1 * jax.random.normal(ks[7], (DEPTH, DIFF_QK_DIM), f32)
    lam_k2 = 0.1 * jax.random.normal(ks[8], (DEPTH, DIFF_QK_DIM), f32)
    subln_g = 1.0 + 0.02 * jax.random.normal(ks[9], (DEPTH, DIFF_WIDTH), f32)
    w_out = jax.random.normal(ks[10], (DEPTH, MIX_WIDTH, D_MODEL), f32) * MIX_WIDTH ** -0.5
    final_g = 1.0 + 0.02 * jax.random.normal(ks[11], (D_MODEL,), f32)
    return {'x': x, 'meta_tokens': meta_tokens, 'norm_g': norm_g, 'w_in': w_in,
            'b_forget': b_forget, 'lam_q1': lam_q1, 'lam_k1': lam_k1, 'lam_q2': lam_q2,
            'lam_k2': lam_k2, 'subln_g': subln_g, 'w_out': w_out, 'final_g': final_g}

def first_block(x, meta_tokens, norm_g, w_in, b_forget, lam_q1, lam_k1, lam_q2, lam_k2,
              subln_g, w_out, final_g):
    bsz, _, dm = x.shape
    meta = jnp.broadcast_to(meta_tokens.astype(x.dtype)[None], (bsz, N_META, dm))
    h = jnp.concatenate([meta, x], axis=1)
    pos = jnp.arange(h.shape[1], dtype=jnp.int32)
    for layer in range(DEPTH):
        lambda_init = 0.8 - 0.6 * math.exp(-0.3 * layer)
        h = hybrid_layer(h, pos, norm_g[layer], w_in[layer], b_forget[layer],
                         lam_q1[layer], lam_k1[layer], lam_q2[layer], lam_k2[layer],
                         subln_g[layer], w_out[layer], lambda_init)
    return rms_norm(h, final_g)[:, N_META:]


GRID_W = 64
CTX_LEN = 256
N_MIXERS = 4
ROPE_BASE = 10000.0
NEG_INF = -1e30

NA_HEADS = 16
NA_HEAD_DIM = D_MODEL // NA_HEADS
NA_WIN_ROWS = 8
NA_WIN_COLS = 16

RW_HEAD = 64
RW_HEADS = D_MODEL // RW_HEAD
RW_DECAY_LORA = 64
RW_ICLR_LORA = 64
RW_GATE_LORA = 128
RW_GN_EPS = 64e-5

MLA_HEADS = 16
MLA_Q_RANK = 384
MLA_KV_RANK = 256
MLA_NOPE = 64
MLA_ROPE = 32
MLA_V = 64

SWA_Q_HEADS = 16
SWA_KV_HEADS = 4
SWA_GROUP = SWA_Q_HEADS // SWA_KV_HEADS
SWA_HEAD_DIM = 64
SWA_WINDOW = 128

N_EXPERTS = 16
EC_CAPACITY = 2
D_FF_EXPERT = 1024


def rms_norm_2(x, g):
    xf = x.astype(jnp.float32)
    y = xf * lax.rsqrt(jnp.mean(xf * xf, axis=-1, keepdims=True) + NORM_EPS)
    return (y * g.astype(jnp.float32)).astype(x.dtype)

def modulate(h, shift, scale):
    return h * (1 + scale) + shift

def ada_modulation(cond, w, b):
    m = jax.nn.silu(cond) @ w + b
    return jnp.split(m, 6, axis=-1)

def axial_rope(n, d_rot):
    t = jnp.arange(n)
    row = (t // GRID_W).astype(jnp.float32)
    col = (t % GRID_W).astype(jnp.float32)
    d_axis = d_rot // 2
    inv = ROPE_BASE ** (-jnp.arange(0, d_axis, 2, dtype=jnp.float32) / d_axis)
    ang = jnp.concatenate([row[:, None] * inv, col[:, None] * inv], axis=-1)
    return jnp.cos(ang), jnp.sin(ang)

def apply_rope(x, cos, sin):
    half = x.shape[-1] // 2
    xf = x.astype(jnp.float32)
    x1, x2 = xf[..., :half], xf[..., half:]
    return jnp.concatenate([x1 * cos - x2 * sin, x2 * cos + x1 * sin], axis=-1).astype(x.dtype)

def context_attention(q, k, v, scale, sink=None):
    L = k.shape[1]
    s = jnp.einsum('bqhgd,bkhd->bhgqk', q, k).astype(jnp.float32) * scale
    if sink is not None:
        snk = jnp.broadcast_to(sink.astype(jnp.float32)[None, :, :, None, None], s.shape[:-1] + (1,))
        s = jnp.concatenate([s, snk], axis=-1)
    p = jax.nn.softmax(s, axis=-1)[..., :L]
    return jnp.einsum('bhgqk,bkhd->bqhgd', p.astype(v.dtype), v)

def neighbourhood_attention(hc, hl, w_qkv, q_g, k_g, rpb, w_o, ctx_out):
    B, n, D = hl.shape
    L = hc.shape[1]
    rows = n // GRID_W
    H, dh = NA_HEADS, NA_HEAD_DIM
    scale = dh ** -0.5

    def project(h):
        qkv = (h @ w_qkv).reshape(h.shape[0], h.shape[1], 3, H, dh)
        return rms_norm_2(qkv[:, :, 0], q_g), rms_norm_2(qkv[:, :, 1], k_g), qkv[:, :, 2]

    qc, kc, vc = project(hc)
    ql, kl, vl = project(hl)

    kr = min(NA_WIN_ROWS, rows)
    n_cb = GRID_W // NA_WIN_COLS
    strip = 2 * NA_WIN_COLS
    qcol = np.arange(GRID_W).reshape(n_cb, NA_WIN_COLS)
    strip0 = np.clip(np.arange(n_cb) * NA_WIN_COLS - NA_WIN_COLS // 2, 0, GRID_W - strip)
    kcol = strip0[:, None] + np.arange(strip)
    cstart = np.clip(qcol - NA_WIN_COLS // 2, 0, GRID_W - NA_WIN_COLS)
    kc3 = kcol[:, None, :]
    col_ok = (kc3 >= cstart[:, :, None]) & (kc3 < cstart[:, :, None] + NA_WIN_COLS)
    dcol_idx = np.clip(kc3 - qcol[:, :, None] + NA_WIN_COLS - 1, 0, 2 * NA_WIN_COLS - 2)
    rpb_cols = rpb[:, :, dcol_idx]
    col_ok = jnp.asarray(col_ok)[:, :, None, :]

    qg = ql.reshape(B, rows, GRID_W, H, dh)
    kg = kl.reshape(B, rows, GRID_W, H, dh)
    vg = vl.reshape(B, rows, GRID_W, H, dh)

    def row_step(r):
        r0 = jnp.clip(r - kr // 2, 0, rows - kr)
        kw = lax.dynamic_slice_in_dim(kg, r0, kr, axis=1)[:, :, kcol]
        vw = lax.dynamic_slice_in_dim(vg, r0, kr, axis=1)[:, :, kcol]
        q = lax.dynamic_index_in_dim(qg, r, axis=1, keepdims=False)[:, qcol]
        dr_idx = r0 + jnp.arange(kr) - r + (NA_WIN_ROWS - 1)
        bias = jnp.transpose(rpb_cols[:, dr_idx], (0, 2, 3, 1, 4)).astype(jnp.float32)
        s_lat = jnp.einsum('bjqhd,brjkhd->bhjqrk', q, kw).astype(jnp.float32) * scale + bias[None]
        s_lat = jnp.where(col_ok, s_lat, NEG_INF).reshape(B, H, n_cb, NA_WIN_COLS, kr * strip)
        s_ctx = jnp.einsum('bjqhd,bkhd->bhjqk', q, kc).astype(jnp.float32) * scale
        p = jax.nn.softmax(jnp.concatenate([s_lat, s_ctx], axis=-1), axis=-1).astype(vl.dtype)
        p_lat = p[..., :kr * strip].reshape(B, H, n_cb, NA_WIN_COLS, kr, strip)
        o = (jnp.einsum('bhjqrk,brjkhd->bjqhd', p_lat, vw)
             + jnp.einsum('bhjqk,bkhd->bjqhd', p[..., kr * strip:], vc))
        return o.reshape(B, GRID_W, H, dh)

    o = lax.map(row_step, jnp.arange(rows))
    ol = jnp.moveaxis(o, 0, 1).reshape(B, n, H * dh) @ w_o
    oc = None
    if ctx_out:
        oc = context_attention(qc[:, :, :, None], kc, vc, scale).reshape(B, L, H * dh) @ w_o
    return oc, ol

def centred_shift(h):
    hp = jnp.pad(h, ((0, 0), (1, 1), (0, 0)))
    return 0.5 * (hp[:, :-2] + hp[:, 2:])

def _rwkv_step(S, inp):
    r, w, kk, kka, kt, v = inp
    sk = jnp.einsum('bhij,bhj->bhi', S, kk)
    S = S * w[:, :, None, :] - sk[..., None] * kka[:, :, None, :] + v[..., None] * kt[:, :, None, :]
    return S, jnp.einsum('bhij,bhj->bhi', S, r)

def _rwkv_scan(S0, seqs, reverse):
    xs = tuple(jnp.swapaxes(t, 0, 1) for t in seqs)
    S, y = lax.scan(_rwkv_step, S0, xs, reverse=reverse)
    return S, jnp.swapaxes(y, 0, 1)

def rwkv7_bidirectional(hc, hl, mix, w_r, w_k, w_v, w0, w1, w2, a0, a1, a2, g1, g2,
                        k_k, k_a, r_k, ln_g, ln_b, w_o, ctx_out):
    f32 = jnp.float32
    H, N = RW_HEADS, RW_HEAD

    def heads(t):
        return t.reshape(t.shape[:-1] + (H, N))

    def stream(h, S0):
        B = h.shape[0]
        xx = centred_shift(h) - h
        xr, xw, xk, xv, xa, xg = (h + xx * mix[s] for s in range(6))
        r = heads((xr @ w_r).astype(f32))
        k = (xk @ w_k).astype(f32)
        v = heads((xv @ w_v).astype(f32))
        g = jax.nn.sigmoid(xg @ g1) @ g2
        dec = w0[:, None, None, :] + jnp.einsum('zbtr,zrd->zbtd', jnp.tanh(jnp.einsum('btd,zdr->zbtr', xw, w1)), w2)
        logw = -jax.nn.softplus(-dec.astype(f32)) - 0.5
        w = heads(jnp.exp(-jnp.exp(logw)))
        a = heads(jax.nn.sigmoid((a0[:, None, None, :] + jnp.einsum(
            'zbtr,zrd->zbtd', jnp.einsum('btd,zdr->zbtr', xa, a1), a2)).astype(f32)))
        kk = heads(k * k_k.astype(f32))
        kk = kk / jnp.maximum(jnp.linalg.norm(kk, axis=-1, keepdims=True), 1e-12)
        kt = heads(k)[None] * (1 + (a - 1) * heads(k_a.astype(f32)))
        if S0 is None:
            z = jnp.zeros((B, H, N, N), f32)
            S0 = (z, z)
        S_f, y_f = _rwkv_scan(S0[0], (r, w[0], kk, kk * a[0], kt[0], v), False)
        S_b, y_b = _rwkv_scan(S0[1], (r, w[1], kk, kk * a[1], kt[1], v), True)
        return (S_f, S_b), (y_f + y_b, r, kt, v, g)

    def readout(y, r, kt, v, g, dtype):
        B, T = y.shape[:2]
        mu = jnp.mean(y, axis=-1, keepdims=True)
        var = jnp.mean(jnp.square(y - mu), axis=-1, keepdims=True)
        yn = ((y - mu) * lax.rsqrt(var + RW_GN_EPS)).reshape(B, T, -1) * ln_g.astype(f32) + ln_b.astype(f32)
        bonus = jnp.sum(jnp.sum(r[None] * kt * r_k.astype(f32), axis=-1, keepdims=True), axis=0) * v
        return ((yn + bonus.reshape(B, T, -1)).astype(dtype) * g) @ w_o

    ctx_state, ctx_feats = stream(hc, None)
    _, lat_feats = stream(hl, ctx_state)
    ol = readout(*lat_feats, hl.dtype)
    oc = readout(*ctx_feats, hc.dtype) if ctx_out else None
    return oc, ol

def multi_head_latent_attention(hc, hl, w_down, q_norm_g, kv_norm_g, w_uq, w_ukv,
                                qn_g, qr_g, kn_g, kr_g, w_o, cos, sin, ctx_out):
    f32 = jnp.float32
    H = MLA_HEADS
    scale = (MLA_NOPE + MLA_ROPE) ** -0.5

    def project(h, rope):
        B, T, _ = h.shape
        d = h @ w_down
        cq = rms_norm_2(d[..., :MLA_Q_RANK], q_norm_g)
        ckv = rms_norm_2(d[..., MLA_Q_RANK:MLA_Q_RANK + MLA_KV_RANK], kv_norm_g)
        k_r = rms_norm_2(d[..., MLA_Q_RANK + MLA_KV_RANK:], kr_g)
        q = (cq @ w_uq).reshape(B, T, H, MLA_NOPE + MLA_ROPE)
        kv = (ckv @ w_ukv).reshape(B, T, H, MLA_NOPE + MLA_V)
        q_n = rms_norm_2(q[..., :MLA_NOPE], qn_g)
        q_r = rms_norm_2(q[..., MLA_NOPE:], qr_g)
        k_n = rms_norm_2(kv[..., :MLA_NOPE], kn_g)
        v = kv[..., MLA_NOPE:]
        if rope:
            q_r = apply_rope(q_r, cos[:, None], sin[:, None])
            k_r = apply_rope(k_r, cos, sin)
        return q_n, q_r, k_n, k_r, v

    qn_l, qr_l, kn_l, kr_l, v_l = project(hl, True)
    qn_c, qr_c, kn_c, kr_c, v_c = project(hc, False)
    B, n = hl.shape[:2]
    L = hc.shape[1]

    def block(b):
        s0 = b * Q_BLOCK
        qn = lax.dynamic_slice_in_dim(qn_l, s0, Q_BLOCK, axis=1)
        qr = lax.dynamic_slice_in_dim(qr_l, s0, Q_BLOCK, axis=1)
        s_lat = jnp.einsum('bqhd,bkhd->bhqk', qn, kn_l) + jnp.einsum('bqhd,bkd->bhqk', qr, kr_l)
        s_ctx = jnp.einsum('bqhd,bkhd->bhqk', qn, kn_c) + jnp.einsum('bqhd,bkd->bhqk', qr, kr_c)
        s = jnp.concatenate([s_lat, s_ctx], axis=-1).astype(f32) * scale
        p = jax.nn.softmax(s, axis=-1).astype(v_l.dtype)
        return (jnp.einsum('bhqk,bkhd->bqhd', p[..., :n], v_l)
                + jnp.einsum('bhqk,bkhd->bqhd', p[..., n:], v_c))

    o = lax.map(block, jnp.arange(n // Q_BLOCK))
    ol = jnp.moveaxis(o, 0, 1).reshape(B, n, H * MLA_V) @ w_o
    oc = None
    if ctx_out:
        q = jnp.concatenate([qn_c, qr_c], axis=-1)
        k = jnp.concatenate([kn_c, jnp.broadcast_to(kr_c[:, :, None, :], (B, L, H, MLA_ROPE))], axis=-1)
        oc = context_attention(q[:, :, :, None], k, v_c, scale).reshape(B, L, H * MLA_V) @ w_o
    return oc, ol

def window_gqa_sink(hc, hl, w_qkv, q_g, k_g, sink, w_o, cos, sin, ctx_out):
    f32 = jnp.float32
    Hk, G, dh = SWA_KV_HEADS, SWA_GROUP, SWA_HEAD_DIM
    scale = dh ** -0.5
    sink_hg = sink.reshape(Hk, G)
    nq = Hk * G * dh

    def project(h, rope):
        B, T, _ = h.shape
        qkv = h @ w_qkv
        q = rms_norm_2(qkv[..., :nq].reshape(B, T, Hk, G, dh), q_g)
        k = rms_norm_2(qkv[..., nq:nq + Hk * dh].reshape(B, T, Hk, dh), k_g)
        v = qkv[..., nq + Hk * dh:].reshape(B, T, Hk, dh)
        if rope:
            q = apply_rope(q, cos[:, None, None], sin[:, None, None])
            k = apply_rope(k, cos[:, None], sin[:, None])
        return q, k, v

    ql, kl, vl = project(hl, True)
    qc, kc, vc = project(hc, False)
    B, n = hl.shape[:2]
    L = hc.shape[1]
    pad = ((0, 0), (Q_BLOCK, Q_BLOCK), (0, 0), (0, 0))
    kp, vp = jnp.pad(kl, pad), jnp.pad(vl, pad)
    q_off = jnp.arange(Q_BLOCK)
    k_off = jnp.arange(3 * Q_BLOCK) - Q_BLOCK

    def block(b):
        s0 = b * Q_BLOCK
        q = lax.dynamic_slice_in_dim(ql, s0, Q_BLOCK, axis=1)
        k = lax.dynamic_slice_in_dim(kp, s0, 3 * Q_BLOCK, axis=1)
        v = lax.dynamic_slice_in_dim(vp, s0, 3 * Q_BLOCK, axis=1)
        qpos, kpos = s0 + q_off, s0 + k_off
        ok = ((kpos >= 0) & (kpos < n))[None, :] & (jnp.abs(qpos[:, None] - kpos[None, :]) <= SWA_WINDOW)
        s_loc = jnp.where(ok, jnp.einsum('bqhgd,bkhd->bhgqk', q, k).astype(f32) * scale, NEG_INF)
        s_ctx = jnp.einsum('bqhgd,bkhd->bhgqk', q, kc).astype(f32) * scale
        s_snk = jnp.broadcast_to(sink_hg.astype(f32)[None, :, :, None, None], s_loc.shape[:-1] + (1,))
        p = jax.nn.softmax(jnp.concatenate([s_loc, s_ctx, s_snk], axis=-1), axis=-1).astype(vl.dtype)
        return (jnp.einsum('bhgqk,bkhd->bqhgd', p[..., :3 * Q_BLOCK], v)
                + jnp.einsum('bhgqk,bkhd->bqhgd', p[..., 3 * Q_BLOCK:-1], vc))

    o = lax.map(block, jnp.arange(n // Q_BLOCK))
    ol = jnp.moveaxis(o, 0, 1).reshape(B, n, nq) @ w_o
    oc = None
    if ctx_out:
        oc = context_attention(qc, kc, vc, scale, sink_hg).reshape(B, L, nq) @ w_o
    return oc, ol

def expert_choice_ffn(h, w_router, w1, w3, w2):
    B, T, D = h.shape
    cap = max(1, EC_CAPACITY * T // N_EXPERTS)
    aff = jax.nn.softmax((h @ w_router).astype(jnp.float32), axis=-1)
    gate, idx = lax.top_k(jnp.swapaxes(aff, 1, 2), cap)
    xin = jax.vmap(lambda hb, ib: hb[ib])(h, idx)
    hid = jax.nn.silu(jnp.einsum('becd,edf->becf', xin, w1)) * jnp.einsum('becd,edf->becf', xin, w3)
    y = jnp.einsum('becf,efd->becd', hid, w2) * gate[..., None].astype(h.dtype)
    return jax.vmap(lambda yb, ib: jax.ops.segment_sum(
        yb.reshape(-1, D), ib.reshape(-1), num_segments=T))(y, idx)

def _layers_of(mixer):
    return len(range(mixer, DEPTH, N_MIXERS))

def second_inputs(seed: int = 0) -> dict:
    key = jax.random.key(seed)
    keys = iter(jax.random.split(key, 96))
    f32 = jnp.float32
    D = D_MODEL

    def normal(shape, scale):
        return jax.random.normal(next(keys), shape, f32) * scale

    def gain(shape):
        return 1.0 + 0.1 * jax.random.normal(next(keys), shape, f32)

    def uniform(shape, lo, hi):
        return jax.random.uniform(next(keys), shape, f32, lo, hi)

    nA, nB, nC, nD = (_layers_of(m) for m in range(N_MIXERS))
    swa_cols = (SWA_Q_HEADS + 2 * SWA_KV_HEADS) * SWA_HEAD_DIM
    return {
        'x': normal((BATCH, SEQ, D), 1.0),
        'c': normal((BATCH, D), 1.0),
        'ctx': normal((BATCH, CTX_LEN, D), 1.0),
        'c_ctx': normal((D,), 1.0),
        'norm1_g': gain((DEPTH, D)),
        'norm2_g': gain((DEPTH, D)),
        'ada_w': normal((DEPTH, D, 6 * D), 0.5 * D ** -0.5),
        'ada_b': normal((DEPTH, 6 * D), 0.02),
        'na_w_qkv': normal((nA, D, 3 * D), D ** -0.5),
        'na_q_g': gain((nA, NA_HEAD_DIM)),
        'na_k_g': gain((nA, NA_HEAD_DIM)),
        'na_rpb': normal((nA, NA_HEADS, 2 * NA_WIN_ROWS - 1, 2 * NA_WIN_COLS - 1), 0.5),
        'na_w_o': normal((nA, D, D), D ** -0.5),
        'rw_mix': uniform((nB, 6, D), 0.0, 1.0),
        'rw_w_r': normal((nB, D, D), D ** -0.5),
        'rw_w_k': normal((nB, D, D), D ** -0.5),
        'rw_w_v': normal((nB, D, D), D ** -0.5),
        'rw_w0': uniform((nB, 2, D), -6.0, -1.0),
        'rw_w1': normal((nB, 2, D, RW_DECAY_LORA), D ** -0.5),
        'rw_w2': normal((nB, 2, RW_DECAY_LORA, D), 0.5 * RW_DECAY_LORA ** -0.5),
        'rw_a0': normal((nB, 2, D), 0.5),
        'rw_a1': normal((nB, 2, D, RW_ICLR_LORA), D ** -0.5),
        'rw_a2': normal((nB, 2, RW_ICLR_LORA, D), 0.5 * RW_ICLR_LORA ** -0.5),
        'rw_g1': normal((nB, D, RW_GATE_LORA), D ** -0.5),
        'rw_g2': normal((nB, RW_GATE_LORA, D), RW_GATE_LORA ** -0.5),
        'rw_k_k': uniform((nB, D), 0.7, 1.0),
        'rw_k_a': uniform((nB, D), 0.8, 1.2),
        'rw_r_k': normal((nB, RW_HEADS, RW_HEAD), 0.1),
        'rw_ln_g': gain((nB, D)),
        'rw_ln_b': normal((nB, D), 0.02),
        'rw_w_o': normal((nB, D, D), D ** -0.5),
        'mla_w_down': normal((nC, D, MLA_Q_RANK + MLA_KV_RANK + MLA_ROPE), D ** -0.5),
        'mla_q_norm_g': gain((nC, MLA_Q_RANK)),
        'mla_kv_norm_g': gain((nC, MLA_KV_RANK)),
        'mla_w_uq': normal((nC, MLA_Q_RANK, MLA_HEADS * (MLA_NOPE + MLA_ROPE)), MLA_Q_RANK ** -0.5),
        'mla_w_ukv': normal((nC, MLA_KV_RANK, MLA_HEADS * (MLA_NOPE + MLA_V)), MLA_KV_RANK ** -0.5),
        'mla_qn_g': gain((nC, MLA_NOPE)),
        'mla_qr_g': gain((nC, MLA_ROPE)),
        'mla_kn_g': gain((nC, MLA_NOPE)),
        'mla_kr_g': gain((nC, MLA_ROPE)),
        'mla_w_o': normal((nC, MLA_HEADS * MLA_V, D), (MLA_HEADS * MLA_V) ** -0.5),
        'swa_w_qkv': normal((nD, D, swa_cols), D ** -0.5),
        'swa_q_g': gain((nD, SWA_HEAD_DIM)),
        'swa_k_g': gain((nD, SWA_HEAD_DIM)),
        'swa_sink': normal((nD, SWA_Q_HEADS), 0.5),
        'swa_w_o': normal((nD, SWA_Q_HEADS * SWA_HEAD_DIM, D), (SWA_Q_HEADS * SWA_HEAD_DIM) ** -0.5),
        'moe_router': normal((DEPTH, D, N_EXPERTS), D ** -0.5),
        'moe_w1': normal((DEPTH, N_EXPERTS, D, D_FF_EXPERT), D ** -0.5),
        'moe_w3': normal((DEPTH, N_EXPERTS, D, D_FF_EXPERT), D ** -0.5),
        'moe_w2': normal((DEPTH, N_EXPERTS, D_FF_EXPERT, D), D_FF_EXPERT ** -0.5),
    }

def second_block(x, c, ctx, c_ctx, norm1_g, norm2_g, ada_w, ada_b,
              na_w_qkv, na_q_g, na_k_g, na_rpb, na_w_o,
              rw_mix, rw_w_r, rw_w_k, rw_w_v, rw_w0, rw_w1, rw_w2, rw_a0, rw_a1, rw_a2,
              rw_g1, rw_g2, rw_k_k, rw_k_a, rw_r_k, rw_ln_g, rw_ln_b, rw_w_o,
              mla_w_down, mla_q_norm_g, mla_kv_norm_g, mla_w_uq, mla_w_ukv,
              mla_qn_g, mla_qr_g, mla_kn_g, mla_kr_g, mla_w_o,
              swa_w_qkv, swa_q_g, swa_k_g, swa_sink, swa_w_o,
              moe_router, moe_w1, moe_w3, moe_w2):
    n = x.shape[1]
    cos_mla, sin_mla = axial_rope(n, MLA_ROPE)
    cos_swa, sin_swa = axial_rope(n, SWA_HEAD_DIM)
    xl, xc = x, ctx
    for i in range(DEPTH):
        mixer, j = i % N_MIXERS, i // N_MIXERS
        ctx_needed = i < DEPTH - 1
        sh1, sc1, gt1, sh2, sc2, gt2 = (t[:, None, :] for t in ada_modulation(c, ada_w[i], ada_b[i]))
        csh1, csc1, cgt1, csh2, csc2, cgt2 = ada_modulation(c_ctx, ada_w[i], ada_b[i])
        hl = modulate(rms_norm_2(xl, norm1_g[i]), sh1, sc1)
        hc = modulate(rms_norm_2(xc, norm1_g[i]), csh1, csc1)
        if mixer == 0:
            oc, ol = neighbourhood_attention(hc, hl, na_w_qkv[j], na_q_g[j], na_k_g[j], na_rpb[j],
                                             na_w_o[j], ctx_needed)
        elif mixer == 1:
            oc, ol = rwkv7_bidirectional(hc, hl, rw_mix[j], rw_w_r[j], rw_w_k[j], rw_w_v[j],
                                         rw_w0[j], rw_w1[j], rw_w2[j], rw_a0[j], rw_a1[j], rw_a2[j],
                                         rw_g1[j], rw_g2[j], rw_k_k[j], rw_k_a[j], rw_r_k[j],
                                         rw_ln_g[j], rw_ln_b[j], rw_w_o[j], ctx_needed)
        elif mixer == 2:
            oc, ol = multi_head_latent_attention(hc, hl, mla_w_down[j], mla_q_norm_g[j], mla_kv_norm_g[j],
                                                 mla_w_uq[j], mla_w_ukv[j], mla_qn_g[j], mla_qr_g[j],
                                                 mla_kn_g[j], mla_kr_g[j], mla_w_o[j],
                                                 cos_mla, sin_mla, ctx_needed)
        else:
            oc, ol = window_gqa_sink(hc, hl, swa_w_qkv[j], swa_q_g[j], swa_k_g[j], swa_sink[j],
                                     swa_w_o[j], cos_swa, sin_swa, ctx_needed)
        xl = xl + gt1 * ol
        hl = modulate(rms_norm_2(xl, norm2_g[i]), sh2, sc2)
        xl = xl + gt2 * expert_choice_ffn(hl, moe_router[i], moe_w1[i], moe_w3[i], moe_w2[i])
        if ctx_needed:
            xc = xc + cgt1 * oc
            hc = modulate(rms_norm_2(xc, norm2_g[i]), csh2, csc2)
            xc = xc + cgt2 * expert_choice_ffn(hc, moe_router[i], moe_w1[i], moe_w3[i], moe_w2[i])
    return xl


def setup_inputs(seed=0):
    out = dict(first_inputs(seed))
    for name, value in second_inputs(seed + 1).items():
        if name != "x":
            out[name + "_2"] = value
    return out


def reference(
    x, meta_tokens, norm_g, w_in, b_forget, lam_q1, lam_k1, lam_q2, lam_k2, subln_g, w_out,
    final_g, c_2, ctx_2, c_ctx_2, norm1_g_2, norm2_g_2, ada_w_2, ada_b_2, na_w_qkv_2, na_q_g_2,
    na_k_g_2, na_rpb_2, na_w_o_2, rw_mix_2, rw_w_r_2, rw_w_k_2, rw_w_v_2, rw_w0_2, rw_w1_2,
    rw_w2_2, rw_a0_2, rw_a1_2, rw_a2_2, rw_g1_2, rw_g2_2, rw_k_k_2, rw_k_a_2, rw_r_k_2,
    rw_ln_g_2, rw_ln_b_2, rw_w_o_2, mla_w_down_2, mla_q_norm_g_2, mla_kv_norm_g_2, mla_w_uq_2,
    mla_w_ukv_2, mla_qn_g_2, mla_qr_g_2, mla_kn_g_2, mla_kr_g_2, mla_w_o_2, swa_w_qkv_2,
    swa_q_g_2, swa_k_g_2, swa_sink_2, swa_w_o_2, moe_router_2, moe_w1_2, moe_w3_2, moe_w2_2,
):
    x = first_block(
        x, meta_tokens, norm_g, w_in, b_forget, lam_q1, lam_k1, lam_q2, lam_k2, subln_g, w_out,
        final_g,
    )
    return second_block(
        x, c_2, ctx_2, c_ctx_2, norm1_g_2, norm2_g_2, ada_w_2, ada_b_2, na_w_qkv_2, na_q_g_2,
        na_k_g_2, na_rpb_2, na_w_o_2, rw_mix_2, rw_w_r_2, rw_w_k_2, rw_w_v_2, rw_w0_2, rw_w1_2,
        rw_w2_2, rw_a0_2, rw_a1_2, rw_a2_2, rw_g1_2, rw_g2_2, rw_k_k_2, rw_k_a_2, rw_r_k_2,
        rw_ln_g_2, rw_ln_b_2, rw_w_o_2, mla_w_down_2, mla_q_norm_g_2, mla_kv_norm_g_2,
        mla_w_uq_2, mla_w_ukv_2, mla_qn_g_2, mla_qr_g_2, mla_kn_g_2, mla_kr_g_2, mla_w_o_2,
        swa_w_qkv_2, swa_q_g_2, swa_k_g_2, swa_sink_2, swa_w_o_2, moe_router_2, moe_w1_2,
        moe_w3_2, moe_w2_2,
    )


_drawn_inputs = setup_inputs


def setup_inputs(seed=0):
    import zlib

    import numpy as np

    out = dict(_drawn_inputs(seed))
    spreads = {}
    factors = {'subln_g': 5.066,
     'na_q_g_2': 8.0,
     'na_k_g_2': 8.0,
     'na_rpb_2': 5.027,
     'rw_w1_2': 6.646,
     'rw_w2_2': 6.873,
     'rw_ln_g_2': 3.751,
     'rw_ln_b_2': 21.844}
    for name, (base, spread) in spreads.items():
        noise = np.random.default_rng([zlib.crc32(name.encode()), seed]).standard_normal(out[name].shape)
        drawn = base * np.exp(spread * noise) if base else spread * noise
        out[name] = jnp.asarray(drawn.astype(out[name].dtype))
    for name, factor in factors.items():
        out[name] = (out[name] * factor).astype(out[name].dtype)
    return out
```

```python
from contextlib import ExitStack, contextmanager
import math

import numpy as np

import concourse.bass as bass
import concourse.mybir as mybir

F32 = mybir.dt.float32
ALU = mybir.AluOpType
ACT = mybir.ActivationFunctionType
AX = mybir.AxisListType

P = 128
BANK = 512
BANKS = 8
D = 1024
KD = D // P
SEQ = 512
LT = SEQ // P
NMETA = 16
CTX = 256
CT = CTX // P
DEPTH = 2
EPS = 1e-6
HEAD = 64
CHUNK = 512
SLOTS = 3
NEG = -1e30


class Named(dict):

    def __getattr__(self, name):
        return self[name]

    def __setattr__(self, name, value):
        self[name] = value


def bank(k, b, n=BANK, first=0):
    return k.psum[:, b * BANK + first:b * BANK + first + n]


@contextmanager
def stage(k, names):
    k.stage_no += 1
    sems = {n: k.nc.alloc_semaphore(f"{n}_{k.stage_no}") for n in names.split()}
    with k.nc.Block() as block:
        yield block, Named(sems)
    k.nc.clear_and_free_semaphores(list(sems.values()))
    k.nc.all_engine_barrier()


class Chain:

    def __init__(self, eng, sem, base=0):
        self.eng, self.sem, self.base, self.n = eng, sem, base, 0

    def __call__(self, ins):
        self.n += 1
        ins.then_inc(self.sem, 1)
        self.eng.wait_ge(self.sem, self.base + self.n)



def load_chunk(k, sp, c):
    slot = c % SLOTS
    for place, src in k.chunks[c]:
        sp.dma_start(place(k.ring[:, slot]), src).then_inc(k.chunk_loaded[slot], 16)


def feed(k, sp, c0, product, ends):
    for n, end in enumerate(ends):
        if c0 + n + SLOTS < len(k.chunks):
            sp.wait_ge(product, end)
            load_chunk(k, sp, c0 + n + SLOTS)


def chunk_here(k, pe, c):
    total = 16 * sum(len(k.chunks[x]) for x in range(c % SLOTS, c + 1, SLOTS))
    pe.wait_ge(k.chunk_loaded[c % SLOTS], total)
    return k.ring[:, c % SLOTS]


def columns(w, n):
    src = w[:, n * CHUNK:(n + 1) * CHUNK].rearrange("(a p) n -> p a n", p=P)
    return [(lambda slot: slot, src)]



def turn_count(segs):
    return len(segs) * KD


def turn_tensor(k, pe, s, src, segs):
    j = 0
    for tiles, rows, _ in segs:
        for a in range(KD):
            if j >= BANKS:
                pe.wait_ge((s.act_turned, s.dve_turned)[j % 2], (j - BANKS) // 2 + 1)
            for n, t in enumerate(tiles):
                last = k.nc.tensor.transpose(bank(k, j % BANKS, rows, n * rows),
                                             src[0:rows, t, a * P:(a + 1) * P], k.ident[0:rows, 0:rows])
            last.then_inc(s.turned, 1)
            j += 1


def turn_out(k, eng, s, dst, segs, scale, shift, mine):
    j = 0
    for g, (tiles, rows, col) in enumerate(segs):
        for a in range(KD):
            if j % 2 == mine:
                n = len(tiles) * rows
                eng.wait_ge(s.turned, j + 1)
                out, got = dst[:, a, col:col + n], bank(k, j % BANKS, n)
                sc = scale(g, a) if scale else 1.0
                sh = shift(g, a) if shift else 0.0
                if mine == 0:
                    k.nc.scalar.activation(out, got, ACT.Identity, bias=sh, scale=sc).then_inc(s.act_turned, 1)
                else:
                    k.nc.vector.tensor_scalar(out, got, sc, sh, ALU.mult, ALU.add).then_inc(s.dve_turned, 1)
            j += 1


def turn(k, src, dst, segs, scale=None, shift=None):
    with stage(k, "turned act_turned dve_turned") as (block, s):
        @block.tensor
        def _(pe):
            turn_tensor(k, pe, s, src, segs)

        @block.scalar
        def _(act):
            turn_out(k, act, s, dst, segs, scale, shift, 0)

        @block.vector
        def _(dve):
            turn_out(k, dve, s, dst, segs, scale, shift, 1)


def norm_turn(k, src, xn, dst, segs, scale, shift=None):
    nc = k.nc
    tiles = [(t, rows) for ts, rows, _ in segs for t in ts]
    with ExitStack() as mem, stage(k, "cleared summed rooted inverted normed turned act_turned dve_turned") as (block, s):
        junk = mem.enter_context(nc.sbuf_tensor(f"junk{k.stage_no}", [P, D], F32))
        stat = mem.enter_context(nc.sbuf_tensor(f"stat{k.stage_no}", [P, 3, 8], F32))

        @block.gpsimd
        def _(pool):
            nc.gpsimd.memset(stat[:, 0, :], 1.0).then_inc(s.cleared, 1)

        @block.scalar
        def _(act):
            act.wait_ge(s.cleared, 1)
            for n, (t, rows) in enumerate(tiles):
                if n:
                    act.wait_ge(s.summed, n)
                nc.scalar.activation(junk[0:rows, :], src[0:rows, t, :], ACT.Square,
                                     accum_out=stat[0:rows, 0, n:n + 1]).then_inc(s.summed, 1)
            act.wait_ge(s.summed, len(tiles))
            nc.scalar.activation(stat[:, 1, :], stat[:, 0, :], ACT.Sqrt, bias=EPS, scale=1.0 / D).then_inc(s.rooted, 1)
            turn_out(k, act, s, dst, segs, scale, shift, 0)

        @block.vector
        def _(dve):
            dve.wait_ge(s.rooted, 1)
            nc.vector.reciprocal(stat[:, 2, :], stat[:, 1, :]).then_inc(s.inverted, 1)
            dve.wait_ge(s.inverted, 1)
            for n, (t, rows) in enumerate(tiles):
                nc.vector.tensor_scalar(xn[0:rows, t, :], src[0:rows, t, :], stat[0:rows, 2, n:n + 1], None,
                                        ALU.mult).then_inc(s.normed, 1)
            turn_out(k, dve, s, dst, segs, scale, shift, 1)

        @block.tensor
        def _(pe):
            pe.wait_ge(s.normed, len(tiles))
            turn_tensor(k, pe, s, xn, segs)



TOK = SEQ + NMETA
HSEGS = [(list(range(LT)), P, 0), ([LT], NMETA, SEQ)]
HTILES = [(t, P) for t in range(LT)] + [(LT, NMETA)]
DIFF_HEADS = 4
FOX_HEADS = 8


def hybrid_project(k, l, uT, qkT, V, Z, zf):
    nc = k.nc
    c0 = k.c
    jobs = 16
    rows_jobs = 4 * len(HTILES)
    with stage(k, "wf_here product act_out dve_out") as (block, s):
        @block.sync
        def _(sp):
            feed(k, sp, c0, s.product, [4 * (n + 1) for n in range(4)]
                 + [jobs + 1 + len(HTILES) * (n + 1) for n in range(4)])

        @block.tensor
        def _(pe):
            for j in range(jobs):
                c, f = c0 + j // 4, j % 4
                w = chunk_here(k, pe, c)
                big, small = 2 * (j % 4), 2 * (j % 4) + 1
                if j >= 4:
                    pe.wait_ge(s.act_out, j - 3)
                    pe.wait_ge(s.dve_out, j - 3)
                for a in range(KD):
                    st = dict(start=a == 0, stop=a == KD - 1)
                    nc.tensor.matmul(bank(k, big), w[:, a, f * P:(f + 1) * P], uT[:, a, 0:SEQ], **st)
                    last = nc.tensor.matmul(bank(k, small, NMETA), w[:, a, f * P:(f + 1) * P], uT[:, a, SEQ:TOK], **st)
                last.then_inc(s.product, 1)
            pe.wait_ge(s.act_out, jobs)
            pe.wait_ge(s.dve_out, jobs)
            wf = k.w_forget[:, l]
            for a in range(KD):
                st = dict(start=a == 0, stop=a == KD - 1)
                nc.tensor.matmul(bank(k, 0)[0:FOX_HEADS, :], wf[:, a, :], uT[:, a, 0:SEQ], **st)
                last = nc.tensor.matmul(bank(k, 1, NMETA)[0:FOX_HEADS, :], wf[:, a, :], uT[:, a, SEQ:TOK], **st)
            last.then_inc(s.product, 1)
            for j in range(rows_jobs):
                c, (t, rows) = c0 + 4 + j // len(HTILES), HTILES[j % len(HTILES)]
                w = chunk_here(k, pe, c)
                b = 2 + j % 6
                if j >= 6:
                    pe.wait_ge((s.act_out, s.dve_out)[j % 2], jobs + 1 + (j - 6) // 2 + 1)
                for a in range(KD):
                    last = nc.tensor.matmul(bank(k, b)[0:rows, :], uT[:, a, t * P:t * P + rows], w[:, a, :],
                                            start=a == 0, stop=a == KD - 1)
                last.then_inc(s.product, 1)

        def rows_out(eng, mine):
            for j in range(rows_jobs):
                if j % 2 != mine:
                    continue
                n, (t, rows) = j // len(HTILES), HTILES[j % len(HTILES)]
                eng.wait_ge(s.product, jobs + 1 + j + 1)
                got = bank(k, 2 + j % 6)[0:rows, :]
                out = (V, V, Z, Z)[n][0:rows, t, (n % 2) * CHUNK:(n % 2 + 1) * CHUNK]
                if mine == 0:
                    nc.scalar.activation(out, got, ACT.Copy).then_inc(s.act_out, 1)
                else:
                    nc.vector.tensor_copy(out, got).then_inc(s.dve_out, 1)

        @block.scalar
        def _(act):
            for j in range(jobs):
                act.wait_ge(s.product, j + 1)
                nc.scalar.mul(qkT[:, j, 0:SEQ], bank(k, 2 * (j % 4)), (0.125, 1.0)[j // 4 % 2]).then_inc(s.act_out, 1)
            act.wait_ge(s.product, jobs + 1)
            nc.scalar.activation(zf[:, 0:SEQ], bank(k, 0)[0:FOX_HEADS, :], ACT.Identity,
                                 bias=k.b_forget[:, l:l + 1]).then_inc(s.act_out, 1)
            rows_out(act, 0)

        @block.vector
        def _(dve):
            for j in range(jobs):
                dve.wait_ge(s.product, j + 1)
                nc.vector.tensor_scalar(qkT[:, j, SEQ:TOK], bank(k, 2 * (j % 4) + 1, NMETA), (0.125, 1.0)[j // 4 % 2], None,
                                        ALU.mult).then_inc(s.dve_out, 1)
            dve.wait_ge(s.product, jobs + 1)
            nc.vector.tensor_scalar(zf[:, SEQ:TOK], bank(k, 1, NMETA)[0:FOX_HEADS, :], k.b_forget[:, l:l + 1], None,
                                    ALU.add).then_inc(s.dve_out, 1)
            rows_out(dve, 1)
    k.c += 8


def hybrid_prepare(k, l, qkT, Z, zf, ncum, lam, spare):
    nc = k.nc
    lam_init = 0.8 - 0.6 * math.exp(-0.3 * l)
    with ExitStack() as mem, stage(k, "mirrored rotated act_step dve_step pool_step gated lam_exp") as (block, s):
        room = spare[:, :, :].rearrange("p a b -> p (a b)")
        spun = room[:, 0:2 * TOK].rearrange("p (a b) -> p a b", a=2)
        work = room[0:FOX_HEADS, 2 * TOK:6 * TOK].rearrange("p (a b) -> p a b", a=4)
        lam_junk = room[:, 6 * TOK:6 * TOK + 2 * HEAD].rearrange("p (a b) -> p a b", a=2)

        @block.tensor
        def _(pe):
            for j in range(8):
                if j >= 4:
                    pe.wait_ge(s.rotated, j - 3)
                nc.tensor.matmul(bank(k, 2 * (j % 4)), k.rope_mirror[:, :], qkT[:, j, 0:SEQ], start=True, stop=True)
                nc.tensor.matmul(bank(k, 2 * (j % 4) + 1, NMETA), k.rope_mirror[:, :], qkT[:, j, SEQ:TOK],
                                 start=True, stop=True).then_inc(s.mirrored, 1)

        @block.scalar
        def _(act):
            act.wait_ge(s.dve_step, 2)
            nc.scalar.activation(lam[:, 2:4], lam[:, 0:2], ACT.Exp).then_inc(s.lam_exp, 1)
            chain = Chain(act, s.act_step)
            chain(nc.scalar.activation(work[:, 0, :], zf[:, :], ACT.Abs))
            chain(nc.scalar.activation(work[:, 1, :], work[:, 0, :], ACT.Exp, scale=-1.0))
            chain(nc.scalar.activation(work[:, 0, :], work[:, 1, :], ACT.Ln, bias=1.0))
            for t, rows in HTILES:
                nc.scalar.activation(Z[0:rows, t, :], Z[0:rows, t, :], ACT.Silu).then_inc(s.gated, 1)

        @block.vector
        def _(dve):
            for m in range(2):
                nc.vector.tensor_tensor_reduce(lam_junk[:, m, :], k.lam_vec[:, l, 2 * m, :], k.lam_vec[:, l, 2 * m + 1, :],
                                               1.0, 0.0, ALU.mult, ALU.add, lam[:, m:m + 1]).then_inc(s.dve_step, 1)
            chain = Chain(dve, s.dve_step, 2)
            dve.wait_ge(s.lam_exp, 1)
            chain(nc.vector.scalar_tensor_tensor(lam[:, 4:5], lam[:, 3:4], -lam_init, lam[:, 2:3], ALU.add, ALU.subtract))
            chain(nc.vector.tensor_scalar(work[:, 2, :], zf[:, :], 0.0, None, ALU.min))
            chain(nc.vector.memset(work[:, 3, :], 1.0))
            dve.wait_ge(s.act_step, 3)
            chain(nc.vector.tensor_tensor(zf[:, :], work[:, 0, :], work[:, 2, :], ALU.subtract))
            chain(nc.vector.tensor_tensor_scan(ncum[:, SEQ:TOK], work[:, 3, 0:NMETA], zf[:, SEQ:TOK], 0.0, ALU.mult, ALU.add))
            chain(nc.vector.tensor_tensor_scan(ncum[:, 0:SEQ], work[:, 3, 0:SEQ], zf[:, 0:SEQ], ncum[:, TOK - 1:TOK],
                                               ALU.mult, ALU.add))
            for j in range(8):
                b = spun[:, j % 2, :]
                dve.wait_ge(s.mirrored, j + 1)
                nc.vector.tensor_tensor(b[:, 0:SEQ], bank(k, 2 * (j % 4)), k.rope_sin[:, 0:SEQ], ALU.mult)
                chain(nc.vector.tensor_tensor(b[:, SEQ:TOK], bank(k, 2 * (j % 4) + 1, NMETA), k.rope_sin[:, SEQ:TOK], ALU.mult))
                chain(nc.vector.tensor_tensor(qkT[:, j, :], qkT[:, j, :], k.rope_cos[:, :], ALU.mult))
                nc.vector.tensor_tensor(qkT[:, j, :], qkT[:, j, :], b, ALU.add).then_inc(s.rotated, 1)


def hybrid_units(last):
    units = []
    for i, rows in HTILES[:LT] if last else HTILES:
        nk = i + 1 if i < LT else 0
        for h in range(DIFF_HEADS):
            units.append((i, rows, nk, h, [(h, 4 + h, 0), (h, 4 + h, 1)]))
        for h in range(FOX_HEADS):
            units.append((i, rows, nk, DIFF_HEADS + h, [(8 + h // 2, 12 + h // 2, h % 2)]))
    return units


def hybrid_attend(k, qkT, V, Z, O, ncum, lam, spare, last_layer):
    nc = k.nc
    units = hybrid_units(last_layer)
    maps, first = [], []
    for u, unit in enumerate(units):
        first.append(len(maps))
        maps += [(u, m) for m in unit[4]]
    diff_before = lambda u: sum(len(x[4]) == 2 for x in units[:u])
    with ExitStack() as mem, stage(k, "scored masked peaked exped mixed flipped copied valued stored scaled") as (block, s):
        sb = lambda n, shape: mem.enter_context(nc.sbuf_tensor(f"{n}{k.stage_no}", shape, F32))
        room = spare[:, :, :].rearrange("p a b -> p (a b)")
        prob = room[:, 0:2 * TOK].rearrange("p (a b) -> p a b", a=2)
        probT = room[:, 2 * TOK:2 * TOK + 10 * P].rearrange("p (a b) -> p a b", a=2)
        stat = sb("stat", [P, 2, 4])

        def extent(nk):
            return nk * P + NMETA

        @block.tensor
        def _(pe):
            def scores(u):
                i, rows, nk, head, ms = units[u]
                for x, (qt, kt, half) in enumerate(ms):
                    m = first[u] + x
                    ps = bank(k, 2 * (m % 2), 2 * BANK)
                    if m >= 2:
                        pe.wait_ge(s.exped, m - 1)
                    lo = half * HEAD
                    parts = ([(0, nk * P, 0)] if nk else []) + [(nk * P, NMETA, SEQ)]
                    q = qkT[lo:lo + HEAD, qt, i * P:i * P + rows]
                    fox = head >= DIFF_HEADS
                    for at, n, key in parts:
                        last = nc.tensor.matmul(ps[0:rows, at:at + n], q, qkT[lo:lo + HEAD, kt, key:key + n],
                                                start=True, stop=not fox)
                        if fox:
                            last = nc.tensor.matmul(ps[0:rows, at:at + n], k.pick_head[:, head - DIFF_HEADS, 0:rows],
                                                    ncum[:, key:key + n], start=False, stop=True)
                    last.then_inc(s.scored, 1)

            def flip_over(u):
                i, rows, nk, head, ms = units[u]
                p = prob[:, first[u] % 2, :]
                flip = bank(k, 4, 2 * BANK)
                if len(ms) == 2:
                    pe.wait_ge(s.mixed, diff_before(u) + 1)
                else:
                    pe.wait_ge(s.exped, first[u] + 1)
                if u >= 1:
                    pe.wait_ge(s.copied, u)
                for j in range(nk):
                    nc.tensor.transpose(flip[:, j * P:j * P + rows], p[0:rows, j * P:(j + 1) * P], k.ident[0:rows, 0:rows])
                nc.tensor.transpose(flip[0:NMETA, nk * P:nk * P + rows], p[0:rows, nk * P:nk * P + NMETA],
                                    k.ident[0:rows, 0:rows]).then_inc(s.flipped, 1)

            def values(u):
                i, rows, nk, head, ms = units[u]
                pe.wait_ge(s.copied, u + 1)
                if u >= 2:
                    pe.wait_ge(s.stored, u - 1)
                pt = probT[:, u % 2, :]
                if head < DIFF_HEADS:
                    cols = slice(head * P, (head + 1) * P)
                else:
                    cols = slice(512 + (head - DIFF_HEADS) * HEAD, 512 + (head - DIFF_HEADS + 1) * HEAD)
                n = cols.stop - cols.start
                out = bank(k, 6 + u % 2, n)[0:rows, :]
                for j in range(nk):
                    nc.tensor.matmul(out, pt[:, j * P:j * P + rows], V[:, j, cols], start=j == 0, stop=False)
                nc.tensor.matmul(out, pt[0:NMETA, nk * P:nk * P + rows], V[0:NMETA, LT, cols], start=nk == 0,
                                 stop=True).then_inc(s.valued, 1)

            scores(0)
            for u in range(len(units)):
                early = u + 1 < len(units) and len(units[u][4]) == len(units[u + 1][4]) == 1
                if early:
                    scores(u + 1)
                if u >= 1:
                    values(u - 1)
                if u + 1 < len(units) and not early:
                    scores(u + 1)
                flip_over(u)
            values(len(units) - 1)

        @block.vector
        def _(dve):
            def peak(m):
                u, _ = maps[m]
                i, rows, nk, head, ms = units[u]
                ps = bank(k, 2 * (m % 2), 2 * BANK)
                at = (nk - 1) * P if nk else 0
                n = P if nk else NMETA
                dve.wait_ge(s.scored, m + 1)
                if m >= 2:
                    dve.wait_ge(s.exped, m - 1)
                nc.vector.tensor_tensor(ps[0:rows, at:at + n], ps[0:rows, at:at + n], k.causal[0:rows, 0:n],
                                        ALU.add).then_inc(s.masked, 1)
                dve.wait_ge(s.masked, m + 1)
                nc.vector.tensor_reduce(stat[0:rows, m % 2, 0:1], ps[0:rows, 0:extent(nk)], AX.X, ALU.max,
                                        negate=True).then_inc(s.peaked, 1)

            scaled = [0]

            def scale(ins):
                scaled[0] += 1
                ins.then_inc(s.scaled, 1)
                dve.wait_ge(s.scaled, scaled[0])

            def finish(u):
                i, rows, nk, head, ms = units[u]
                m = first[u]
                e = extent(nk)
                for x in range(len(ms)):
                    dve.wait_ge(s.exped, m + x + 1)
                    scale(nc.vector.reciprocal(stat[0:rows, (m + x) % 2, 2:3], stat[0:rows, (m + x) % 2, 1:2]))
                if len(ms) == 2:
                    a, b = m % 2, (m + 1) % 2
                    scale(nc.vector.tensor_scalar(prob[0:rows, a, 0:e], prob[0:rows, a, 0:e], stat[0:rows, a, 2:3], None,
                                                  ALU.mult))
                    scale(nc.vector.tensor_scalar(prob[0:rows, b, 0:e], prob[0:rows, b, 0:e], stat[0:rows, b, 2:3],
                                                  lam[0:rows, 4:5], ALU.mult, ALU.mult))
                    nc.vector.tensor_tensor(prob[0:rows, a, 0:e], prob[0:rows, a, 0:e], prob[0:rows, b, 0:e],
                                            ALU.add).then_inc(s.mixed, 1)
                else:
                    scale(nc.vector.tensor_copy(keep[0:rows, u % 2, :], stat[0:rows, m % 2, 2:3]))

            def store(u):
                i, rows, nk, head, ms = units[u]
                dve.wait_ge(s.valued, u + 1)
                if head < DIFF_HEADS:
                    nc.vector.tensor_copy(O[0:rows, i, head * P:(head + 1) * P],
                                          bank(k, 6 + u % 2, P)[0:rows, :]).then_inc(s.stored, 1)
                else:
                    c = 512 + (head - DIFF_HEADS) * HEAD
                    nc.vector.scalar_tensor_tensor(O[0:rows, i, c:c + HEAD], bank(k, 6 + u % 2, HEAD)[0:rows, :],
                                                   keep[0:rows, u % 2, :], Z[0:rows, i, c:c + HEAD],
                                                   ALU.mult, ALU.mult).then_inc(s.stored, 1)

            keep = sb("keep", [P, 2, 1])
            for x in range(len(units[0][4])):
                peak(x)
            for u in range(len(units)):
                early = u + 1 < len(units) and len(units[u][4]) == len(units[u + 1][4]) == 1
                if early:
                    peak(first[u + 1])
                finish(u)
                if u + 1 < len(units) and not early:
                    for x in range(len(units[u + 1][4])):
                        peak(first[u + 1] + x)
                if u >= 1:
                    store(u - 1)
            store(len(units) - 1)

        @block.scalar
        def _(act):
            def exponent(m):
                u, _ = maps[m]
                i, rows, nk, head, ms = units[u]
                e = extent(nk)
                act.wait_ge(s.peaked, m + 1)
                before = [v for v in range(u) if any((first[v] + x) % 2 == m % 2 for x in range(len(units[v][4])))]
                if before:
                    act.wait_ge(s.flipped, before[-1] + 1)
                    d = diff_before(before[-1] + 1)
                    if d:
                        act.wait_ge(s.mixed, d)
                nc.scalar.activation(prob[0:rows, m % 2, 0:e], bank(k, 2 * (m % 2), 2 * BANK)[0:rows, 0:e], ACT.Exp,
                                     bias=stat[0:rows, m % 2, 0:1], accum_out=stat[0:rows, m % 2, 1:2]).then_inc(s.exped, 1)

            def copy(u):
                i, rows, nk, head, ms = units[u]
                act.wait_ge(s.flipped, u + 1)
                if u >= 2:
                    act.wait_ge(s.valued, u - 1)
                flip = bank(k, 4, 2 * BANK)
                if nk:
                    nc.scalar.activation(probT[:, u % 2, 0:nk * P], flip[:, 0:nk * P], ACT.Copy)
                nc.scalar.activation(probT[0:NMETA, u % 2, nk * P:nk * P + rows], flip[0:NMETA, nk * P:nk * P + rows],
                                     ACT.Copy).then_inc(s.copied, 1)

            for x in range(len(units[0][4])):
                exponent(x)
            for u in range(len(units)):
                copy_next = u
                if u + 1 < len(units) and len(units[u + 1][4]) == 1 and len(units[u][4]) == 1:
                    exponent(first[u + 1])
                    copy(u)
                else:
                    copy(u)
                    if u + 1 < len(units):
                        for x in range(len(units[u + 1][4])):
                            exponent(first[u + 1] + x)


def hybrid_gate(k, O, Z, tiles):
    nc = k.nc
    with ExitStack() as mem, stage(k, "cleared summed rooted step") as (block, s):
        sb = lambda n, shape: mem.enter_context(nc.sbuf_tensor(f"{n}{k.stage_no}", shape, F32))
        sq = sb("sq", [P, 2, 512])
        stat = sb("stat", [P, 2, 5 * DIFF_HEADS])

        @block.gpsimd
        def _(pool):
            nc.gpsimd.memset(stat[:, 0, :], 1.0).then_inc(s.cleared, 1)

        @block.vector
        def _(dve):
            chain = Chain(dve, s.step)
            dve.wait_ge(s.cleared, 1)
            for t, rows in tiles:
                o = O[0:rows, t, 0:512]
                chain(nc.vector.tensor_tensor(sq[0:rows, t % 2, :], o, o, ALU.mult))
                nc.vector.tensor_reduce(stat[0:rows, 0, t * 4:t * 4 + 4],
                                        sq[0:rows, t % 2, :].rearrange("p (h d) -> p h d", h=4), AX.X,
                                        ALU.add).then_inc(s.summed, 1)
            dve.wait_ge(s.rooted, 1)
            chain(nc.vector.reciprocal(stat[:, 0, :], stat[:, 1, :]))
            for t, rows in tiles:
                o = O[0:rows, t, 0:512]
                chain(nc.vector.tensor_tensor(o.rearrange("p (h d) -> p h d", h=4), o.rearrange("p (h d) -> p h d", h=4),
                                              stat[0:rows, 0, t * 4:t * 4 + 4].unsqueeze(2).to_broadcast([rows, 4, P]),
                                              ALU.mult))
                chain(nc.vector.tensor_tensor(o, o, Z[0:rows, t, 0:512], ALU.mult))

        @block.scalar
        def _(act):
            act.wait_ge(s.summed, len(tiles))
            nc.scalar.activation(stat[:, 1, :], stat[:, 0, :], ACT.Sqrt, bias=EPS, scale=1.0 / P).then_inc(s.rooted, 1)


def add_projection(k, srcT, tiles, X, gate=None):
    nc = k.nc
    c0 = k.c
    jobs = [(n, t, rows) for n in range(2) for t, rows in tiles]
    with ExitStack() as mem, stage(k, "product added gated") as (block, s):
        if gate is not None:
            part = mem.enter_context(nc.sbuf_tensor(f"part{k.stage_no}", [P, 2, CHUNK], F32))

        @block.sync
        def _(sp):
            feed(k, sp, c0, s.product, [len(tiles) * (n + 1) for n in range(2)])

        @block.tensor
        def _(pe):
            for j, (n, t, rows) in enumerate(jobs):
                w = chunk_here(k, pe, c0 + n)
                if j >= BANKS:
                    pe.wait_ge(s.added, j - BANKS + 1)
                for a in range(KD):
                    last = nc.tensor.matmul(bank(k, j % BANKS)[0:rows, :], srcT[:, a, t * P:t * P + rows], w[:, a, :],
                                            start=a == 0, stop=a == KD - 1)
                last.then_inc(s.product, 1)

        @block.vector
        def _(dve):
            for j, (n, t, rows) in enumerate(jobs):
                dve.wait_ge(s.product, j + 1)
                x = X[0:rows, t, n * CHUNK:(n + 1) * CHUNK]
                got = bank(k, j % BANKS)[0:rows, :]
                if gate is not None:
                    nc.vector.tensor_tensor(part[0:rows, j % 2, :], got, gate(t)[:, n * CHUNK:(n + 1) * CHUNK],
                                            ALU.mult).then_inc(s.gated, 1)
                    dve.wait_ge(s.gated, j + 1)
                    got = part[0:rows, j % 2, :]
                nc.vector.tensor_tensor(x, x, got, ALU.add).then_inc(s.added, 1)
    k.c += 2


def hybrid_layer(k, l):
    nc = k.nc
    last = l == DEPTH - 1
    with ExitStack() as mem:
        sb = lambda n, shape: mem.enter_context(nc.sbuf_tensor(f"h{l}_{n}", shape, F32))
        uT = sb("uT", [P, KD, TOK])
        O = sb("O", [P, 5, D])
        norm_turn(k, k.X, O, uT, HSEGS, lambda g, a: k.norm_cols[:, l, a:a + 1])
        with ExitStack() as inner:
            sbi = lambda n, shape: inner.enter_context(nc.sbuf_tensor(f"h{l}_{n}", shape, F32))
            qkT = sbi("qkT", [P, 16, TOK])
            V = sbi("V", [P, 5, D])
            Z = sbi("Z", [P, 5, D])
            zf = sbi("zf", [FOX_HEADS, TOK])
            ncum = sbi("ncum", [FOX_HEADS, TOK])
            lam = sbi("lam", [P, 8])
            hybrid_project(k, l, uT, qkT, V, Z, zf)
            hybrid_prepare(k, l, qkT, Z, zf, ncum, lam, O)
            hybrid_attend(k, qkT, V, Z, O, ncum, lam, uT, last)
            tiles = HTILES[:LT] if last else HTILES
            hybrid_gate(k, O, Z, tiles)
        lam_init = 0.8 - 0.6 * math.exp(-0.3 * l)
        turn(k, O, uT, HSEGS[:1] if last else HSEGS,
             lambda g, a: k.subln_cols[:, l, a:a + 1] if a < 4 else 1.0)
        add_projection(k, uT, tiles, k.X)


def final_norm(k):
    nc = k.nc
    with ExitStack() as mem, stage(k, "summed rooted step gain_here") as (block, s):
        sb = lambda n, shape: mem.enter_context(nc.sbuf_tensor(f"{n}{k.stage_no}", shape, F32))
        junk, stat, gain = sb("junk", [P, D]), sb("stat", [P, 3, LT]), sb("gain", [P, D])

        @block.sync
        def _(sp):
            sp.dma_start(gain[:, :], k.d["final_g"].partition_broadcast(P)).then_inc(s.gain_here, 16)

        @block.scalar
        def _(act):
            for t in range(LT):
                if t:
                    act.wait_ge(s.summed, t)
                nc.scalar.activation(junk[:, :], k.X[:, t, :], ACT.Square,
                                     accum_out=stat[:, 0, t:t + 1]).then_inc(s.summed, 1)
            act.wait_ge(s.summed, LT)
            nc.scalar.activation(stat[:, 1, :], stat[:, 0, :], ACT.Sqrt, bias=EPS, scale=1.0 / D).then_inc(s.rooted, 1)

        @block.vector
        def _(dve):
            dve.wait_ge(s.rooted, 1)
            chain = Chain(dve, s.step)
            chain(nc.vector.reciprocal(stat[:, 2, :], stat[:, 1, :]))
            dve.wait_ge(s.gain_here, 16)
            for t in range(LT):
                chain(nc.vector.scalar_tensor_tensor(k.X[:, t, :], k.X[:, t, :], stat[:, 2, t:t + 1], gain[:, :],
                                                     ALU.mult, ALU.mult))



TOK2 = SEQ + CTX
SEGS2 = [(list(range(LT)), P, 0), (list(range(LT, LT + CT)), P, SEQ)]
TILES2 = [(t, P) for t in range(LT + CT)]
SECTIONS = 6
SHIFT, GAIN = 0, 1


def modulation(k, l):
    nc = k.nc
    c0 = k.c
    n_chunks = SECTIONS * D // CHUNK
    mods = k.big[0][0:2, :, :].rearrange("p a b -> p (a b)")
    with stage(k, "bias_here cond_ready product added turned columned gate_made gate_out step") as (block, s):
        @block.sync
        def _(sp):
            sp.dma_start(mods, k.d["ada_b_2"][l].partition_broadcast(2)).then_inc(s.bias_here, 16)
            feed(k, sp, c0, s.product, range(1, n_chunks + 1))

        @block.scalar
        def _(act):
            nc.scalar.activation(k.cond_silu[:, :, :], k.cond[:, :, :], ACT.Silu).then_inc(s.cond_ready, 1)
            for j in range(8):
                act.wait_ge(s.gate_made, j + 1)
                nc.scalar.activation(k.gates[:, j // 2, j % 2 * CHUNK:(j % 2 + 1) * CHUNK], bank(k, j % 4),
                                     ACT.Copy).then_inc(s.gate_out, 1)

        @block.tensor
        def _(pe):
            pe.wait_ge(s.cond_ready, 1)
            for n in range(n_chunks):
                w = chunk_here(k, pe, c0 + n)
                if n >= 6:
                    pe.wait_ge(s.added, n - 5)
                for a in range(KD):
                    last = nc.tensor.matmul(bank(k, n % 6)[0:2, :], k.cond_silu[:, a, :], w[:, a, :],
                                            start=a == 0, stop=a == KD - 1)
                last.then_inc(s.product, 1)
            pe.wait_ge(s.added, n_chunks)
            for x, sec in enumerate((0, 1, 3, 4)):
                for a in range(KD):
                    at = sec * D + a * P
                    last = nc.tensor.transpose(bank(k, 6, 2, (x * KD + a) * 2), mods[:, at:at + P], k.ident[0:2, 0:2])
            last.then_inc(s.turned, 1)
            for j in range(8):
                g, half = j // 2, j % 2
                at = (2, 5)[g // 2] * D + half * CHUNK
                if j >= 4:
                    pe.wait_ge(s.gate_out, j - 3)
                nc.tensor.matmul(bank(k, j % 4), k.pick_row[:, g % 2, :], mods[:, at:at + CHUNK],
                                 start=True, stop=True).then_inc(s.gate_made, 1)

        @block.vector
        def _(dve):
            dve.wait_ge(s.bias_here, 16)
            for n in range(n_chunks):
                dve.wait_ge(s.product, n + 1)
                m = mods[:, n * CHUNK:(n + 1) * CHUNK]
                nc.vector.tensor_tensor(m, m, bank(k, n % 6)[0:2, :], ALU.add).then_inc(s.added, 1)
            dve.wait_ge(s.turned, 1)
            chain = Chain(dve, s.step)
            chain(nc.vector.tensor_copy(k.mod_cols[:, :, :, :].rearrange("p s a r -> p (s a r)"), bank(k, 6, 64)))
            for x, g in ((1, k.norm1_cols), (3, k.norm2_cols)):
                chain(nc.vector.scalar_tensor_tensor(k.mod_cols[:, x, :, :], k.mod_cols[:, x, :, :], 1.0,
                                                     g[:, l, :].unsqueeze(2).to_broadcast([P, KD, 2]), ALU.add, ALU.mult))
    k.c += n_chunks


def project_rows(k, srcT, tiles, outs):
    nc = k.nc
    c0 = k.c
    jobs = [(n, t, rows) for n in range(len(outs)) for t, rows in tiles]
    with stage(k, "product act_out dve_out") as (block, s):
        @block.sync
        def _(sp):
            feed(k, sp, c0, s.product, [len(tiles) * (n + 1) for n in range(len(outs))])

        @block.tensor
        def _(pe):
            for j, (n, t, rows) in enumerate(jobs):
                w = chunk_here(k, pe, c0 + n)
                if j >= BANKS:
                    pe.wait_ge((s.act_out, s.dve_out)[j % 2], (j - BANKS) // 2 + 1)
                for a in range(KD):
                    last = nc.tensor.matmul(bank(k, j % BANKS)[0:rows, :], srcT[:, a, t * P:t * P + rows], w[:, a, :],
                                            start=a == 0, stop=a == KD - 1)
                last.then_inc(s.product, 1)

        @block.scalar
        def _(act):
            for j in range(0, len(jobs), 2):
                n, t, rows = jobs[j]
                act.wait_ge(s.product, j + 1)
                nc.scalar.activation(outs[n](t), bank(k, j % BANKS)[0:rows, :], ACT.Copy).then_inc(s.act_out, 1)

        @block.vector
        def _(dve):
            for j in range(1, len(jobs), 2):
                n, t, rows = jobs[j]
                dve.wait_ge(s.product, j + 1)
                nc.vector.tensor_copy(outs[n](t), bank(k, j % BANKS)[0:rows, :]).then_inc(s.dve_out, 1)
    k.c += len(outs)


NA_HEADS = 16
GRID = 64
WIN_ROWS, WIN_COLS = 8, 16
REL_ROWS, REL_COLS = 2 * WIN_ROWS - 1, 2 * WIN_COLS - 1
PAD = 2 * GRID


def head_norm(k, rows3, tiles, eps_width):
    nc = k.nc
    heads = NA_HEADS
    with ExitStack() as mem, stage(k, "squared summed rooted step") as (block, s):
        sb = lambda n, shape: mem.enter_context(nc.sbuf_tensor(f"{n}{k.stage_no}", shape, F32))
        sq = sb("sq", [P, 2, D])
        stat = sb("stat", [P, 2, len(tiles) * heads])

        @block.scalar
        def _(act):
            for n, (t, rows) in enumerate(tiles):
                if n >= 2:
                    act.wait_ge(s.summed, n - 1)
                nc.scalar.activation(sq[:, n % 2, :], rows3[:, t, :], ACT.Square).then_inc(s.squared, 1)
            act.wait_ge(s.summed, len(tiles))
            nc.scalar.activation(stat[:, 1, :], stat[:, 0, :], ACT.Sqrt, bias=EPS, scale=1.0 / HEAD).then_inc(s.rooted, 1)

        @block.vector
        def _(dve):
            for n, (t, rows) in enumerate(tiles):
                dve.wait_ge(s.squared, n + 1)
                nc.vector.tensor_reduce(stat[:, 0, n * heads:(n + 1) * heads],
                                        sq[:, n % 2, :].rearrange("p (h d) -> p h d", h=heads), AX.X,
                                        ALU.add).then_inc(s.summed, 1)
            dve.wait_ge(s.rooted, 1)
            chain = Chain(dve, s.step)
            chain(nc.vector.reciprocal(stat[:, 0, :], stat[:, 1, :]))
            for n, (t, rows) in enumerate(tiles):
                x = rows3[:, t, :].rearrange("p (h d) -> p h d", h=heads)
                chain(nc.vector.tensor_tensor(x, x, stat[:, 0, n * heads:(n + 1) * heads].unsqueeze(2)
                                              .to_broadcast([P, heads, HEAD]), ALU.mult))


def pad_bias(k, j):
    nc = k.nc
    rows = NA_HEADS * REL_ROWS // 2
    with ExitStack() as mem, stage(k, "cleared here stored") as (block, s):
        pad = mem.enter_context(nc.sbuf_tensor(f"pad{k.stage_no}", [rows, 2, PAD], F32))

        @block.vector
        def _(dve):
            nc.vector.memset(pad[:, :, :], 0.0).then_inc(s.cleared, 1)

        @block.sync
        def _(sp):
            sp.wait_ge(s.cleared, 1)
            first = GRID - WIN_COLS
            sp.dma_start(pad[:, :, first:first + REL_COLS],
                         k.d["na_rpb_2"][j].rearrange("h r c -> (h r) c").rearrange("(a p) c -> p a c", p=rows)).then_inc(s.here, 16)
            sp.wait_ge(s.here, 16)
            for a in range(2):
                sp.dma_start(k.bias_rows[a * rows:(a + 1) * rows], pad[:, a, :].unsqueeze(1).to_broadcast([rows, GRID, PAD])
                             ).then_inc(s.stored, 16)
            sp.wait_ge(s.stored, 32)


def neighbour_attend(k, qT, kT, V, oT):
    nc = k.nc
    tiles = LT + CT
    units = [(h, t) for h in range(NA_HEADS) for t in range(tiles)]
    lat_before = lambda u: u // tiles * LT + min(u % tiles, LT)
    with ExitStack() as mem, stage(k, "even_bias odd_bias biased scored masked peaked exped inverted scaled flipped copied valued stored") as (block, s):
        sb = lambda n, shape: mem.enter_context(nc.sbuf_tensor(f"{n}{k.stage_no}", shape, F32))
        bias = sb("bias", [P, 2, 16 * GRID])
        prob = sb("prob", [P, 2, TOK2])
        probT = sb("probT", [P, TOK2])
        stat = sb("stat", [P, 2, 3])

        def extent(t):
            return TOK2 if t < LT else CTX

        @block.sync
        def _(sp):
            for h in range(NA_HEADS):
                if h >= 2:
                    sp.wait_ge(s.masked, LT * (h - 1))
                for half in range(2):
                    src = bass.AP(tensor=k.bias_rows.tensor, offset=h * REL_ROWS * GRID * PAD + GRID - 1,
                                  ap=[[PAD - 1, GRID], [GRID * PAD, REL_ROWS], [1, GRID]])
                    dst = bias[half * GRID:(half + 1) * GRID, h % 2, half * GRID:half * GRID + REL_ROWS * GRID]
                    sp.dma_start(dst.rearrange("p (a b) -> p a b", b=GRID), src).then_inc((s.even_bias, s.odd_bias)[h % 2], 16)

        @block.tensor
        def _(pe):
            def scores(u):
                h, t = units[u]
                lo = h % 2 * HEAD
                ps = bank(k, 2 * (u % 2), 2 * BANK)
                if u >= 2:
                    pe.wait_ge(s.exped, u - 1)
                q = qT[lo:lo + HEAD, h // 2, t * P:(t + 1) * P]
                at = 0
                if t < LT:
                    nc.tensor.matmul(ps[:, 0:SEQ], q, kT[lo:lo + HEAD, h // 2, 0:SEQ], start=True, stop=True)
                    at = SEQ
                nc.tensor.matmul(ps[:, at:at + CTX], q, kT[lo:lo + HEAD, h // 2, SEQ:TOK2], start=True,
                                 stop=True).then_inc(s.scored, 1)

            def flip(u):
                flip = bank(k, 4, 2 * BANK)
                n = extent(units[u][1]) // P
                pe.wait_ge(s.scaled, u + 1)
                if u >= 1:
                    pe.wait_ge(s.copied, u)
                for j in range(n):
                    last = nc.tensor.transpose(flip[:, j * P:(j + 1) * P], prob[:, u % 2, j * P:(j + 1) * P], k.ident[:, :])
                last.then_inc(s.flipped, 1)

            def values(u):
                h, t = units[u]
                lo = h % 2 * HEAD
                n = extent(t) // P
                pe.wait_ge(s.copied, u + 1)
                if u >= 2:
                    pe.wait_ge(s.stored, u - 1)
                for j in range(n):
                    kt = j if t < LT else LT + j
                    last = nc.tensor.matmul(bank(k, 6 + u % 2, P)[lo:lo + HEAD, :], V[:, kt, h * HEAD:(h + 1) * HEAD],
                                            probT[:, j * P:(j + 1) * P], start=j == 0, stop=j == n - 1)
                last.then_inc(s.valued, 1)

            scores(0)
            for u in range(len(units)):
                if u + 1 < len(units):
                    scores(u + 1)
                if u >= 1:
                    values(u - 1)
                flip(u)
            values(len(units) - 1)

        @block.vector
        def _(dve):
            def peak(u):
                h, t = units[u]
                ps = bank(k, 2 * (u % 2), 2 * BANK)
                if t == 0:
                    dve.wait_ge((s.even_bias, s.odd_bias)[h % 2], 32 * (h // 2 + 1))
                    b = bias[:, h % 2, GRID:REL_ROWS * GRID].rearrange("p (a b) -> p a b", b=GRID)
                    nc.vector.tensor_tensor(b, b, k.col_mask[:, :].unsqueeze(1).to_broadcast([P, REL_ROWS - 1, GRID]),
                                            ALU.add).then_inc(s.biased, 1)
                    dve.wait_ge(s.biased, h + 1)
                dve.wait_ge(s.scored, u + 1)
                if t < LT:
                    first = (WIN_ROWS - 1 - 2 * t) * GRID
                    nc.vector.tensor_tensor(ps[:, 0:SEQ], ps[:, 0:SEQ], bias[:, h % 2, first:first + SEQ],
                                            ALU.add).then_inc(s.masked, 1)
                    dve.wait_ge(s.masked, lat_before(u) + 1)
                nc.vector.tensor_reduce(stat[:, u % 2, 0:1], ps[:, 0:extent(t)], AX.X, ALU.max,
                                        negate=True).then_inc(s.peaked, 1)

            def normalise(u):
                h, t = units[u]
                dve.wait_ge(s.exped, u + 1)
                nc.vector.reciprocal(stat[:, u % 2, 2:3], stat[:, u % 2, 1:2]).then_inc(s.inverted, 1)
                dve.wait_ge(s.inverted, u + 1)
                p = prob[:, u % 2, 0:extent(t)]
                nc.vector.tensor_scalar(p, p, stat[:, u % 2, 2:3], None, ALU.mult).then_inc(s.scaled, 1)

            def store(u):
                h, t = units[u]
                lo = h % 2 * HEAD
                dve.wait_ge(s.valued, u + 1)
                nc.vector.tensor_copy(oT[lo:lo + HEAD, h // 2, t * P:(t + 1) * P],
                                      bank(k, 6 + u % 2, P)[lo:lo + HEAD, :]).then_inc(s.stored, 1)

            peak(0)
            for u in range(len(units)):
                if u + 1 < len(units):
                    peak(u + 1)
                normalise(u)
                if u >= 1:
                    store(u - 1)
            store(len(units) - 1)

        @block.scalar
        def _(act):
            def exponent(u):
                h, t = units[u]
                act.wait_ge(s.peaked, u + 1)
                if u >= 2:
                    act.wait_ge(s.flipped, u - 1)
                nc.scalar.activation(prob[:, u % 2, 0:extent(t)], bank(k, 2 * (u % 2), extent(t)), ACT.Exp,
                                     bias=stat[:, u % 2, 0:1], accum_out=stat[:, u % 2, 1:2]).then_inc(s.exped, 1)

            exponent(0)
            for u in range(len(units)):
                if u + 1 < len(units):
                    exponent(u + 1)
                act.wait_ge(s.flipped, u + 1)
                if u >= 1:
                    act.wait_ge(s.valued, u)
                n = extent(units[u][1])
                nc.scalar.activation(probT[:, 0:n], bank(k, 4, n), ACT.Copy).then_inc(s.copied, 1)


def modulated_norm(k, which, xn, dst, segs):
    col = lambda x: lambda g, a: k.mod_cols[:, 2 * which + x, a, g:g + 1]
    norm_turn(k, k.X, xn, dst, segs, col(GAIN), col(SHIFT))


def neighbour_layer(k, j):
    A, B, C, V = k.big
    feat = lambda buf: buf[:, :, :].rearrange("p a b -> p (a b)").rearrange("p (a b) -> p a b", a=KD)
    modulated_norm(k, 0, B, feat(A), SEGS2)
    place = lambda buf, n: lambda t: buf[:, t, n * CHUNK:(n + 1) * CHUNK]
    project_rows(k, feat(A), TILES2, [place(buf, n) for buf in (B, C, V) for n in range(2)])
    head_norm(k, B, TILES2, HEAD)
    head_norm(k, C, TILES2, HEAD)
    turn(k, B, feat(A), SEGS2, lambda g, a: k.na_q_cols[:, j:j + 1])
    turn(k, C, feat(B), SEGS2, lambda g, a: k.na_k_cols[:, j:j + 1])
    pad_bias(k, j)
    neighbour_attend(k, feat(A), feat(B), V, feat(C))
    add_projection(k, feat(C), TILES2, k.X, lambda t: k.gates[:, 0 if t < LT else 1, :])



EXPERTS = 16
CAP_L, CAP_C = 2 * SEQ // EXPERTS, 2 * CTX // EXPERTS
ROUND = 4
EPAD = EXPERTS + ROUND
W_CHUNKS = 6


def expert_chunk(d, l, e, j):
    name = ("moe_w1_2", "moe_w3_2", "moe_w1_2", "moe_w3_2", "moe_w2_2", "moe_w2_2")[j]
    half = (0, 0, 1, 1, 0, 1)[j]
    return d[name][l, e].rearrange("(a p) n -> p a n", p=P)[:, :, half * CHUNK:(half + 1) * CHUNK]


def route(k, l, hT, aff, slot, tiles):
    nc = k.nc
    streams = [(0, SEQ, CAP_L)] + ([(SEQ, CTX, CAP_C)] if len(tiles) > LT else [])
    n_tok = sum(n for _, n, _ in streams)
    nt = len(tiles)
    with ExitStack() as mem, stage(k, "logits exped turned placed step ready") as (block, s):
        sb = lambda n, shape: mem.enter_context(nc.sbuf_tensor(f"{n}{k.stage_no}", shape, F32))
        stat = sb("stat", [P, 2, 8])
        affT, left, rank = sb("affT", [EXPERTS, TOK2]), sb("left", [EXPERTS, TOK2]), sb("rank", [EXPERTS, TOK2])
        ones = sb("ones", [EXPERTS, SEQ])
        best = sb("best", [EXPERTS, 8])
        raw = sb("raw", [P, nt, EXPERTS])

        @block.tensor
        def _(pe):
            for t in range(nt):
                for a in range(KD):
                    last = nc.tensor.matmul(bank(k, 0, EXPERTS, t * EXPERTS), hT[:, a, t * P:(t + 1) * P],
                                            k.router[:, l, a, :], start=a == 0, stop=a == KD - 1)
            last.then_inc(s.logits, 1)
            pe.wait_ge(s.ready, 1)
            for t in range(nt):
                last = nc.tensor.transpose(bank(k, 1, P, t * P)[0:EXPERTS, :], aff[:, t, 0:EXPERTS], k.ident[:, :])
            last.then_inc(s.turned, 1)
            pe.wait_ge(s.ready, 2)
            for t in range(nt):
                last = nc.tensor.transpose(bank(k, 3, EXPERTS, t * EXPERTS), rank[:, t * P:(t + 1) * P],
                                           k.ident[0:EXPERTS, 0:EXPERTS])
            last.then_inc(s.placed, 1)

        @block.scalar
        def _(act):
            act.wait_ge(s.step, 4)
            nc.scalar.activation(raw[:, :, :], raw[:, :, :], ACT.Exp).then_inc(s.exped, 1)

        @block.vector
        def _(dve):
            chain = Chain(dve, s.step)
            chain(nc.vector.memset(slot[:, :, :], -1.0))
            chain(nc.vector.memset(aff[:, :, :], 0.0))
            dve.wait_ge(s.logits, 1)
            lg = bank(k, 0, nt * EXPERTS).rearrange("p (t e) -> p t e", t=nt)
            wide = lambda x: x.unsqueeze(2).to_broadcast([P, nt, EXPERTS])
            chain(nc.vector.tensor_reduce(stat[:, 0, 0:nt], lg, AX.X, ALU.max))
            chain(nc.vector.tensor_tensor(raw[:, :, :], lg, wide(stat[:, 0, 0:nt]), ALU.subtract))
            dve.wait_ge(s.exped, 1)
            chain(nc.vector.tensor_reduce(stat[:, 0, 0:nt], raw[:, :, :], AX.X, ALU.add))
            chain(nc.vector.reciprocal(stat[:, 1, 0:nt], stat[:, 0, 0:nt]))
            nc.vector.tensor_tensor(aff[:, 0:nt, 0:EXPERTS], raw[:, :, :], wide(stat[:, 1, 0:nt]), ALU.mult).then_inc(s.ready, 1)
            chain(nc.vector.memset(ones[:, :], 1.0))
            dve.wait_ge(s.turned, 1)
            chain(nc.vector.tensor_copy(affT[:, 0:n_tok], bank(k, 1, n_tok)[0:EXPERTS, :]))
            chain(nc.vector.tensor_copy(left[:, 0:n_tok], affT[:, 0:n_tok]))
            for first, n, cap in streams:
                row = left[:, first:first + n]
                for _ in range(cap // 8):
                    chain(nc.vector.max(best[:, :], row))
                    chain(nc.vector.match_replace(row, best[:, :], row, -1.0))
            chosen = left[:, 0:n_tok]
            chain(nc.vector.tensor_scalar(chosen, chosen, 0.0, None, ALU.is_lt))
            for first, n, cap in streams:
                chain(nc.vector.tensor_tensor_scan(rank[:, first:first + n], ones[:, 0:n], left[:, first:first + n], 0.0,
                                                   ALU.mult, ALU.add))
            chain(nc.vector.tensor_tensor(rank[:, 0:n_tok], rank[:, 0:n_tok], chosen, ALU.mult))
            nc.vector.tensor_scalar(rank[:, 0:n_tok], rank[:, 0:n_tok], -1.0, None, ALU.add).then_inc(s.ready, 1)
            dve.wait_ge(s.placed, 1)
            chain(nc.vector.tensor_copy(slot[:, 0:nt, 0:EXPERTS], bank(k, 3, nt * EXPERTS)
                                        .rearrange("p (t e) -> p t e", t=nt)))


def experts(k, l, xn, aff, slot, acc, room_a, room_b, with_ctx):
    nc = k.nc
    c0 = k.c
    M = CAP_L + (CAP_C if with_ctx else 0)
    nt = LT + (CT if with_ctx else 0)
    jobs = [(t, half) for t in range(nt) for half in range(2)]
    CJ = len(jobs)
    T = M if M > HEAD else P
    flat_a = room_a[:, :, :].rearrange("p a b -> p (a b)")
    flat_b = room_b[:, :, :].rearrange("p a b -> p (a b)")

    def carve(flat, at, *dims):
        n = math.prod(dims)
        letters = "abcd"[:len(dims)]
        pat = f"p ({' '.join(letters)}) -> p {' '.join(letters)}"
        return flat[:, at:at + n].rearrange(pat, **dict(zip(letters, dims))), at + n

    onehot, at = carve(flat_a, 0, 2, LT + CT, CAP_L)
    gate_tok, at = carve(flat_a, at, 2, LT + CT)
    xinT, at = carve(flat_a, at, 2, KD, M)
    hidT, at = carve(flat_a, at, KD, M)
    backT, at = carve(flat_a, at, 2, SEQ)
    y2, at = carve(flat_b, 0, 2, CHUNK)
    yc, at = carve(flat_b, at, 2, CHUNK)
    hid, at = carve(flat_b, at, 2, CHUNK)
    silu, at = carve(flat_b, at, 2, CHUNK)
    backC, at = carve(flat_b, at, 2, CTX)
    gate_row, at = carve(flat_b, at, 2)
    assert at <= (LT + CT) * D

    with stage(k, "cleared onehot gathered xin_ready back_copied up silued hid_ready flipped hid_copied down y_ready "
                  "combined added weighted") as (block, s):
        loaded0 = [16 * sum(len(k.chunks[x]) for x in range(n, c0, SLOTS)) for n in range(SLOTS)]

        @block.gpsimd
        def _(pool):
            for x in (y2, yc, backT[:, 1, :], backC[:, 1, :], hid):
                nc.gpsimd.memset(x, 0.0).then_inc(s.cleared, 1)
            for t in range(nt):
                nc.gpsimd.memset(acc[:, t, :], 0.0).then_inc(s.cleared, 1)

        @block.sync
        def _(sp):
            for e in range(EXPERTS):
                for j in range(W_CHUNKS):
                    c = c0 + e * W_CHUNKS + j + SLOTS
                    if c < len(k.chunks):
                        if j < 4:
                            sp.wait_ge(s.up, e * 4 + j + 1)
                        else:
                            sp.wait_ge(s.down, e * 2 + j - 3)
                        load_chunk(k, sp, c)

        @block.tensor
        def _(pe):
            def weights(e, j):
                n = (c0 + j) % SLOTS
                pe.wait_ge(k.chunk_loaded[n], e * (16 * W_CHUNKS // SLOTS) + loaded0[n] + 16 * (j // SLOTS + 1))
                return k.ring[:, n]

            def gather(e, b, combos):
                pe.wait_ge(s.onehot, e + 1)
                pe.wait_ge(s.xin_ready, e)
                pe.wait_ge(s.back_copied, e)
                pe.wait_ge(s.added, combos)
                for a in range(KD):
                    for t in range(LT):
                        nc.tensor.matmul(bank(k, 4, CAP_L, a * CAP_L), xn[:, t, a * P:(a + 1) * P], onehot[:, b, t, :],
                                         start=t == 0, stop=t == LT - 1)
                    for t in range(LT, nt):
                        nc.tensor.matmul(bank(k, 5, CAP_C, a * CAP_C), xn[:, t, a * P:(a + 1) * P], onehot[:, b, t, 0:CAP_C],
                                         start=t == LT, stop=t == nt - 1)
                for t in range(LT):
                    nc.tensor.transpose(bank(k, 6, P, t * P)[0:CAP_L, :], onehot[:, b, t, :], k.ident[:, :])
                for t in range(LT, nt):
                    nc.tensor.transpose(bank(k, 7, P, (t - LT) * P)[0:CAP_C, :], onehot[:, b, t, 0:CAP_C], k.ident[:, :])
                for t in range(LT, nt):
                    nc.tensor.matmul(bank(k, 5, 1, 301)[0:CAP_C, :], onehot[:, b, t, 0:CAP_C], gate_tok[:, b, t:t + 1],
                                     start=t == LT, stop=t == nt - 1)
                for t in range(LT):
                    last = nc.tensor.matmul(bank(k, 5, 1, 300)[0:CAP_L, :], onehot[:, b, t, :], gate_tok[:, b, t:t + 1],
                                            start=t == 0, stop=t == LT - 1)
                last.then_inc(s.gathered, 1)

            def give_back(e, pair, before):
                pe.wait_ge(s.back_copied, e + 1)
                for j, (t, half) in enumerate(jobs):
                    if j >= 2:
                        pe.wait_ge(s.added, before + j - 1)
                    if t < LT:
                        nc.tensor.matmul(bank(k, 6 + j % 2), backT[:, pair, t * P:(t + 1) * P], y2[:, half, :],
                                         start=True, stop=True).then_inc(s.combined, 1)
                    else:
                        nc.tensor.matmul(bank(k, 6 + j % 2), backC[0:2 * CAP_C, pair, (t - LT) * P:(t - LT + 1) * P],
                                         yc[0:2 * CAP_C, half, :], start=True, stop=True).then_inc(s.combined, 1)

            pe.wait_ge(s.cleared, 5)
            gather(0, 0, 0)
            with pe.Fori(0, EXPERTS // ROUND) as it:
                for x in range(ROUND):
                    e = it * ROUND + x
                    before = it * (2 * CJ) + x // 2 * CJ
                    pe.wait_ge(s.xin_ready, e + 1)
                    for j in range(4):
                        w = weights(e, j)
                        pe.wait_ge((s.hid_copied, s.y_ready)[j // 2], e * 2)
                        for a in range(KD):
                            last = nc.tensor.matmul(bank(k, j)[0:M, :], xinT[:, x % 2, a, :], w[:, a, :],
                                                    start=a == 0, stop=a == KD - 1)
                        last.then_inc(s.up, 1)
                    if x % 2 == 0:
                        pe.wait_ge(s.y_ready, e * 2)
                        give_back(e, 1 - x // 2, before)
                    gather(e + 1, (x + 1) % 2, before + CJ)
                    pe.wait_ge(s.hid_ready, e * 2 + 2)
                    for half in range(2):
                        for f in range(4):
                            last = nc.tensor.transpose(bank(k, half, T, f * T), hid[0:T, half, f * P:(f + 1) * P],
                                                       k.ident[0:T, 0:T])
                        last.then_inc(s.flipped, 1)
                    pe.wait_ge(s.hid_copied, e * 2 + 2)
                    for j in range(4, 6):
                        w = weights(e, j)
                        for a in range(KD):
                            last = nc.tensor.matmul(bank(k, j - 2)[0:M, :], hidT[:, a, :], w[:, a, :],
                                                    start=a == 0, stop=a == KD - 1)
                        last.then_inc(s.down, 1)
            pe.wait_ge(s.y_ready, EXPERTS * 2)
            give_back(EXPERTS, 1, EXPERTS // 2 * CJ)

        @block.scalar
        def _(act):
            def way_back(e, b, pair, row):
                act.wait_ge(s.gathered, e + 1)
                if with_ctx:
                    nc.scalar.activation(backC[row * CAP_C:(row + 1) * CAP_C, pair, :], bank(k, 7, CTX)[0:CAP_C, :], ACT.Copy)
                nc.scalar.activation(backT[row * CAP_L:(row + 1) * CAP_L, pair, :], bank(k, 6)[0:CAP_L, :],
                                     ACT.Copy)
                act.wait_ge(s.xin_ready, e + 1)
                if with_ctx:
                    nc.scalar.activation(gate_row[CAP_L:M, b:b + 1], bank(k, 5, 1, 301)[0:CAP_C, :], ACT.Copy)
                nc.scalar.activation(gate_row[0:CAP_L, b:b + 1], bank(k, 5, 1, 300)[0:CAP_L, :],
                                     ACT.Copy).then_inc(s.back_copied, 1)

            act.wait_ge(s.cleared, 5)
            way_back(0, 0, 0, 0)
            with act.Fori(0, EXPERTS // ROUND) as it:
                for x in range(ROUND):
                    e = it * ROUND + x
                    for half in range(2):
                        act.wait_ge(s.up, e * 4 + 2 * half + 1)
                        nc.scalar.activation(silu[0:M, half, :], bank(k, 2 * half)[0:M, :], ACT.Silu).then_inc(s.silued, 1)
                    y = (x + 1) % ROUND
                    way_back(e + 1, y % 2, y // 2, y % 2)
                    for half in range(2):
                        act.wait_ge(s.flipped, e * 2 + half + 1)
                        nc.scalar.activation(hidT[:, half * 4:half * 4 + 4, :], bank(k, half, 4 * T)
                                             .rearrange("p (a b) -> p a b", a=4)[:, :, 0:M], ACT.Copy).then_inc(s.hid_copied, 1)

        @block.vector
        def _(dve):
            def choose(e, b):
                nc.vector.tensor_copy(gate_tok[:, b, 0:nt].unsqueeze(2), aff[:, 0:nt, bass.ds(e, 1)])
                nc.vector.tensor_tensor(onehot[:, b, 0:nt, :], k.iota[:, :].unsqueeze(1).to_broadcast([P, nt, CAP_L]),
                                        slot[:, 0:nt, bass.ds(e, 1)].to_broadcast([P, nt, CAP_L]),
                                        ALU.is_equal).then_inc(s.onehot, 1)

            def modulate(e, b):
                dve.wait_ge(s.gathered, e + 1)
                for r, first, n in ((0, 0, CAP_L), (1, CAP_L, CAP_C))[:1 + with_ctx]:
                    col = lambda c: k.mod_cols[:, 2 + c, :, r].unsqueeze(2).to_broadcast([P, KD, n])
                    nc.vector.tensor_tensor(xinT[:, b, :, first:first + n], bank(k, 4 + r, KD * n)
                                            .rearrange("p (a c) -> p a c", a=KD), col(GAIN), ALU.mult).then_inc(s.weighted, 1)
                dve.wait_ge(s.weighted, (e + 1) * (1 + with_ctx))
                for r, first, n in ((0, 0, CAP_L), (1, CAP_L, CAP_C))[:1 + with_ctx]:
                    col = lambda c: k.mod_cols[:, 2 + c, :, r].unsqueeze(2).to_broadcast([P, KD, n])
                    x = xinT[:, b, :, first:first + n]
                    last = nc.vector.tensor_tensor(x, x, col(SHIFT), ALU.add)
                last.then_inc(s.xin_ready, 1)

            def sum_up(before):
                for j, (t, half) in enumerate(jobs):
                    dve.wait_ge(s.combined, before + j + 1)
                    x = acc[:, t, half * CHUNK:(half + 1) * CHUNK]
                    nc.vector.tensor_tensor(x, x, bank(k, 6 + j % 2), ALU.add).then_inc(s.added, 1)

            dve.wait_ge(s.cleared, 5 + nt)
            choose(0, 0)
            choose(1, 1)
            modulate(0, 0)
            with dve.Fori(0, EXPERTS // ROUND) as it:
                for x in range(ROUND):
                    e = it * ROUND + x
                    for half in range(2):
                        dve.wait_ge(s.silued, e * 2 + half + 1)
                        dve.wait_ge(s.up, e * 4 + 2 * half + 2)
                        nc.vector.tensor_tensor(hid[0:M, half, :], silu[0:M, half, :], bank(k, 2 * half + 1)[0:M, :],
                                                ALU.mult).then_inc(s.hid_ready, 1)
                    if x % 2 == 0:
                        sum_up(it * (2 * CJ) + x // 2 * CJ)
                    choose(e + 2, x % 2)
                    modulate(e + 1, (x + 1) % 2)
                    dve.wait_ge(s.back_copied, e + 1)
                    for half in range(2):
                        dve.wait_ge(s.down, e * 2 + half + 1)
                        got, g, row = bank(k, 2 + half), gate_row[:, x % 2:x % 2 + 1], x % 2
                        if with_ctx:
                            nc.vector.tensor_scalar(yc[row * CAP_C:(row + 1) * CAP_C, half, :], got[CAP_L:M, :], g[CAP_L:M, :],
                                                    None, ALU.mult)
                        nc.vector.tensor_scalar(y2[row * CAP_L:(row + 1) * CAP_L, half, :], got[0:CAP_L, :], g[0:CAP_L, :],
                                                None, ALU.mult).then_inc(s.y_ready, 1)
            sum_up(EXPERTS // 2 * CJ)
            last_sum = (EXPERTS // 2 + 1) * CJ
            dve.wait_ge(s.added, last_sum)
            w0 = (EXPERTS + 1) * (1 + with_ctx)
            for t in range(nt):
                nc.vector.tensor_tensor(acc[:, t, :], acc[:, t, :], k.gates[:, 2 + (t >= LT), :], ALU.mult).then_inc(s.weighted, 1)
                dve.wait_ge(s.weighted, w0 + t + 1)
                nc.vector.tensor_tensor(k.X[:, t, :], k.X[:, t, :], acc[:, t, :], ALU.add).then_inc(s.added, 1)
    k.c += EXPERTS * W_CHUNKS


def expert_layer(k, l, with_ctx):
    nc = k.nc
    A, B, C, E = k.big
    feat = lambda buf: buf[:, :, :].rearrange("p a b -> p (a b)").rearrange("p (a b) -> p a b", a=KD)
    segs = SEGS2 if with_ctx else SEGS2[:1]
    tiles = TILES2 if with_ctx else TILES2[:LT]
    modulated_norm(k, 1, A, feat(B), segs)
    with ExitStack() as mem:
        aff = mem.enter_context(nc.sbuf_tensor(f"aff{l}", [P, LT + CT, EPAD], F32))
        slot = mem.enter_context(nc.sbuf_tensor(f"slot{l}", [P, LT + CT, EPAD], F32))
        route(k, l, feat(B), aff, slot, tiles)
        experts(k, l, A, aff, slot, C, B, E, with_ctx)



CH = 64
PAIRS = 8
DIRS = 2
RATE = math.exp(-0.5)
MIX_R, MIX_W, MIX_K, MIX_V, MIX_A, MIX_G = range(6)
DOUBLINGS = 5


def rwkv_chunks(d):
    lora1 = []
    for n, name in enumerate(("rw_w1_2", "rw_a1_2")):
        for z in range(DIRS):
            at = (DIRS * n + z) * CH
            lora1.append((lambda slot, at=at: slot[:, :, at:at + CH], d[name][0, z].rearrange("(a p) r -> p a r", p=P)))
    lora1.append((lambda slot: slot[:, :, 4 * CH:4 * CH + P], d["rw_g1_2"][0].rearrange("(a p) r -> p a r", p=P)))
    flat = lambda slot: slot.rearrange("p a b -> p (a b)")
    lora2 = [(lambda slot, n=n: flat(slot)[:, n * D:(n + 1) * D],
              d[name][0].rearrange("z r n -> (z r) n") if n < 2 else d[name][0])
             for n, name in enumerate(("rw_w2_2", "rw_a2_2", "rw_g2_2"))]
    lora2 += [(lambda slot, z=z, h=h: flat(slot)[h * CH:(h + 1) * CH, 3 * D + z * BANK:3 * D + (z + 1) * BANK],
               d["rw_w0_2"][0, z, h * BANK:(h + 1) * BANK].partition_broadcast(CH)) for z in range(DIRS) for h in range(2)]
    halves = lambda name: [columns(d[name][0], n) for n in range(2)]
    return [lora1] + halves("rw_w_r_2") + halves("rw_w_v_2") + halves("rw_w_k_2") + [lora2, [], []] + halves("rw_w_o_2")


def rwkv_project(k, hT, xx, bufs, tw, ta, tg, R, V, K):
    nc = k.nc
    c0 = k.c
    order = [MIX_W, MIX_A, MIX_G, MIX_R, MIX_V, MIX_K]
    xs = [bufs[n] for n in (0, 1, 0, 1, 0, 0)]
    tokens = [(0, SEQ), (SEQ, CTX)]
    jobs = [(0, 0, 0, t) for t in tokens] + [(1, 0, 2 * CH, t) for t in tokens] + [(2, 0, 4 * CH, tokens[0])]
    jobs += [(3, 1 + f // 4, f % 4 * P, tokens[0]) for f in range(KD)]
    jobs += [(4, 3 + n, t * P, None) for n in range(2) for t in range(LT + CT)]
    jobs += [(5, 5 + f // 4, f % 4 * P, t) for f in range(KD) for t in tokens]
    end = [max(j for j, x in enumerate(jobs) if x[0] == m) + 1 for m in range(6)]
    chunk_end = [max(j for j, x in enumerate(jobs) if x[1] == c) + 1 for c in range(7)]
    with stage(k, "shifted mixed product act_out dve_out") as (block, s):
        @block.sync
        def _(sp):
            feed(k, sp, c0, s.product, chunk_end)

        @block.vector
        def _(dve):
            for first, n in tokens:
                h, x = hT[:, :, first:first + n], xx[:, :, first:first + n]
                nc.vector.tensor_tensor(x[:, :, 1:n - 1], h[:, :, 0:n - 2], h[:, :, 2:n], ALU.add)
                nc.vector.tensor_copy(x[:, :, 0:1], h[:, :, 1:2])
                nc.vector.tensor_copy(x[:, :, n - 1:n], h[:, :, n - 2:n - 1]).then_inc(s.shifted, 1)
            dve.wait_ge(s.shifted, 2)
            nc.vector.scalar_tensor_tensor(xx[:, :, :], xx[:, :, :], 0.5, hT[:, :, :], ALU.mult,
                                           ALU.subtract).then_inc(s.shifted, 1)
            dve.wait_ge(s.shifted, 3)

            def mix(m):
                if m >= 2:
                    dve.wait_ge(s.product, end[m - 2] if m < 5 else end[m - 1])
                for a in range(KD):
                    nc.vector.scalar_tensor_tensor(xs[m][:, a, :], xx[:, a, :], k.mix_cols[:, order[m], a:a + 1], hT[:, a, :],
                                                   ALU.mult, ALU.add).then_inc(s.mixed, 1)

            mix(0)
            mix(1)
            for m in range(6):
                out(k, dve, s, jobs, range(end[m - 1] if m else 0, end[m]), 1, tw, ta, tg, R, V, K)
                if m < 3:
                    mix(m + 2)
                elif m == 4:
                    mix(5)

        @block.scalar
        def _(act):
            out(k, act, s, jobs, range(len(jobs)), 0, tw, ta, tg, R, V, K)

        @block.tensor
        def _(pe):
            for j, (m, c, at, moving) in enumerate(jobs):
                w = chunk_here(k, pe, c0 + c)
                pe.wait_ge(s.mixed, KD * (m + 1))
                if j >= BANKS:
                    pe.wait_ge((s.act_out, s.dve_out)[j % 2], (j - BANKS) // 2 + 1)
                for a in range(KD):
                    st = dict(start=a == 0, stop=a == KD - 1)
                    if moving is None:
                        last = nc.tensor.matmul(bank(k, j % BANKS), xs[m][:, a, at:at + P], w[:, a, :], **st)
                    else:
                        first, n = moving
                        last = nc.tensor.matmul(bank(k, j % BANKS, n), w[:, a, at:at + P], xs[m][:, a, first:first + n], **st)
                last.then_inc(s.product, 1)
    k.c += 7


def out(k, eng, s, jobs, which, mine, tw, ta, tg, R, V, K):
    nc = k.nc
    for j in which:
        m, c, at, moving = jobs[j]
        if j % 2 != mine:
            continue
        eng.wait_ge(s.product, j + 1)
        done = (s.act_out, s.dve_out)[mine]
        got = bank(k, j % BANKS)
        copy = (lambda o, i: nc.scalar.activation(o, i, ACT.Copy)) if mine == 0 else nc.vector.tensor_copy
        if moving is None:
            n, t = c - 3, at // P
            for half in range(2):
                for par in range(2):
                    dst = V[par * CH:(par + 1) * CH, 2 * t + half, n * 4:n * 4 + 4, :]
                    src = got[half * CH:(half + 1) * CH, :].rearrange("t (p h i) -> t p h i", p=4, h=2)[:, :, par, :]
                    last = copy(dst, src)
            last.then_inc(done, 1)
            continue
        first, n = moving
        f = (c - 1) % 2 * 4 + at // P
        dst = {0: tw, 1: ta, 2: tg}.get(m)
        dst = dst[:, first:first + n] if dst is not None else (R if m == 3 else K)[:, f, first:first + n]
        copy(dst, got[:, 0:n]).then_inc(done, 1)


def rwkv_keys(k, K, KK, sq, tw, tg):
    nc = k.nc
    with stage(k, "saved scaled squared summed rooted bounded inverted done") as (block, s):
        @block.sync
        def _(sp):
            sp.dma_start(k.x_saved, k.X[:, 0:LT, :]).then_inc(s.saved, 16)
            sp.wait_ge(s.saved, 16)

        @block.scalar
        def _(act):
            nc.scalar.activation(tw[:, :], tw[:, :], ACT.Tanh)
            nc.scalar.activation(tg[:, :], tg[:, :], ACT.Sigmoid)
            for a in range(KD):
                act.wait_ge(s.scaled, a + 1)
                if a >= 2:
                    act.wait_ge(s.done, a - 1)
                nc.scalar.activation(sq[:, a % 2, :], KK[:, a, :], ACT.Square).then_inc(s.squared, 1)
                act.wait_ge(s.summed, a + 1)
                nc.scalar.activation(sq[:, a % 2, :], bank(k, 2 * (a % 2), TOK2), ACT.Sqrt).then_inc(s.rooted, 1)

        @block.tensor
        def _(pe):
            for a in range(KD):
                pe.wait_ge(s.squared, a + 1)
                if a >= 2:
                    pe.wait_ge(s.rooted, a - 1)
                nc.tensor.matmul(bank(k, 2 * (a % 2)), k.head_ones[:, :], sq[:, a % 2, 0:SEQ], start=True, stop=True)
                nc.tensor.matmul(bank(k, 2 * (a % 2) + 1, CTX), k.head_ones[:, :], sq[:, a % 2, SEQ:TOK2], start=True,
                                 stop=True).then_inc(s.summed, 1)

        @block.vector
        def _(dve):
            for a in range(KD):
                nc.vector.tensor_scalar(KK[:, a, :], K[:, a, :], k.kk_cols[:, a:a + 1], None, ALU.mult).then_inc(s.scaled, 1)
            for a in range(KD):
                dve.wait_ge(s.rooted, a + 1)
                x = sq[:, a % 2, :]
                nc.vector.tensor_scalar(x, x, 1e-12, None, ALU.max).then_inc(s.bounded, 1)
                dve.wait_ge(s.bounded, a + 1)
                nc.vector.reciprocal(x, x).then_inc(s.inverted, 1)
                dve.wait_ge(s.inverted, a + 1)
                nc.vector.tensor_tensor(KK[:, a, :], KK[:, a, :], x, ALU.mult).then_inc(s.done, 1)


class Events:

    def __init__(self, sem, names, base):
        self.sem, self.names, self.base, self.next = sem, names, base, 0

    def value(self, it, name):
        return it * len(self.names) + (self.base + self.names.index(name) + 1)

    def before(self, it):
        return it * len(self.names) + self.base

    def done(self, ins, name):
        assert self.names[self.next % len(self.names)] == name, name
        self.next += 1
        ins.then_inc(self.sem, 1)


def scan_events(lat):
    middle = {1: "b", 2: "ar", 3: "br"} if lat else {1: "b"}
    pe = ["dec", "iclr", "cumulate"] + (["bonus"] if lat else []) + ["gram_m", "gram_n", "beta_rows", "kappa_rows"]
    act = ["decay_gate", "iclr_gate", "d_inc", "d_exc", "d_inv", "spread0", "beta_rows", "kappa_rows"]
    dve = ["dec", "iclr", "m", "kt", "akk"] + (["bon", "bonus_in"] if lat else []) + ["alpha", "end"] + \
          (["rho"] if lat else []) + ["beta", "kappa"] + (["bonus"] if lat else []) + ["mask_m", "mask_n", "first"]
    for n in range(1, DOUBLINGS):
        pe += [f"square{n}", f"merged{n}"] + ([f"gram_{middle[n]}"] if n in middle else [])
        act += [f"square{n}", f"spread{n}"]
        dve += [f"merged{n}", f"product{n}"] + ([f"mask_{middle[n]}"] if n in middle else [])
    n = DOUBLINGS
    pe += [f"square{n}", f"product{n}", "start", f"product{n + 1}", "sk"] + (["y"] if lat else []) + ["state"]
    act += [f"square{n}", "start", "sk"]
    dve += [f"product{n}", f"product{n + 1}"] + (["y"] if lat else []) + ["state", "decayed"]
    return dict(pe=pe, act=act, dve=dve, pool=["tokens", "rates", "values"])


def rwkv_scan(k, K, KK, R, V, tw, ta, Y, bonus, lora2, tiles, small, wide):
    nc = k.nc
    (T_dec, T_rho, T_alpha, T_mp0, T_beta, T_kappa, T_n, T_brow, T_krow, T_mp1, T_v, T_state) = tiles
    w2, a2, w0 = lora2[:, 0:D], lora2[:, D:2 * D], lora2[:, 3 * D:4 * D]
    twc, tac, d_end = small
    own = lambda t, z: t[:, z * BANK:(z + 1) * BANK]
    pairs = lambda t, z: own(t, z).rearrange("p (a x) -> p a x", a=PAIRS)
    mp = lambda z: (T_mp0, T_mp1)[z].rearrange("p (a e x) -> p a e x", e=2, x=CH)
    m_of, p_of = (lambda z: mp(z)[:, :, 0, :]), (lambda z: mp(z)[:, :, 1, :])
    n_wide = lambda z: wide[:, z * D:(z + 1) * D].rearrange("p (a h x) -> p a h x", h=2, x=CH)
    quad = lambda q, z: bank(k, 4 * z + q)
    quad3 = lambda q, z: quad(q, z).rearrange("p (a x) -> p a x", a=PAIRS)
    V2 = V[:, :, :, :].rearrange("p c a i -> p c (a i)")
    Y2 = Y[:, :, :, :].rearrange("p c a i -> p c (a i)")
    phases = [(False, CTX // CH, SEQ, SEQ // CH), (True, SEQ // CH, 0, 0)]

    def columns_of(it, z, steps, first):
        return it * CH + first if z == 0 else it * -CH + (first + (steps - 1) * CH)

    def chunk_of(it, z, steps, first):
        return it + first if z == 0 else it * -1 + (first + steps - 1)

    names = "pe0 pe1 act0 act1 dve0 dve1 pool0 pool1"
    with stage(k, "cleared begun " + names) as (block, s):

        def phase_list():
            base = dict(pe=0, act=0, dve=0, pool=0)
            for lat, steps, first, chunk in phases:
                ev = scan_events(lat)
                yield lat, steps, first, chunk, {n: [Events(s[f"{n}{z}"], ev[n], base[n]) for z in range(DIRS)]
                                                 for n in base}
                for n in base:
                    base[n] += steps * len(ev[n])

        def in_turn(eng, steps, front, both):
            front(0, 0)
            both(0, 0, 1, 0)
            with eng.Fori(0, steps - 1) as it:
                both(1, it, 0, it + 1)
                both(0, it + 1, 1, it + 1)
            both(1, steps - 1, None, None)

        @block.gpsimd
        def _(pool):
            nc.gpsimd.memset(T_state, 0.0).then_inc(s.cleared, 1)
            nc.gpsimd.memset(Y2, 0.0).then_inc(s.cleared, 1)
            nc.gpsimd.memset(bonus[:, :, :], 0.0).then_inc(s.cleared, 1)
            nc.gpsimd.memset(wide, 0.0).then_inc(s.cleared, 1)
            pool.wait_ge(s.cleared, 4)
            for lat, steps, first, chunk, ev in phase_list():
                def front(z, it):
                    mine, lo, c = ev["pool"][z], z * CH, columns_of(it, z, steps, first)
                    if lat or not isinstance(it, int):
                        pool.wait_ge(ev["pe"][z].sem, ev["pe"][z].before(it))
                    mine.done(nc.gpsimd.tensor_copy(twc[lo:lo + CH, :], tw[lo:lo + CH, bass.ds(c, CH)]), "tokens")
                    pool.wait_ge(mine.sem, mine.value(it, "tokens"))
                    mine.done(nc.gpsimd.tensor_copy(tac[lo:lo + CH, :], ta[lo:lo + CH, bass.ds(c, CH)]), "rates")
                    pool.wait_ge(mine.sem, mine.value(it, "rates"))
                    mine.done(nc.gpsimd.tensor_copy(own(T_v, z).unsqueeze(1), V2[:, bass.ds(chunk_of(it, z, steps, chunk), 1), :]),
                              "values")
                    pool.wait_ge(mine.sem, mine.value(it, "values"))

                def both(z, it, z2, it2):
                    if z2 is not None:
                        front(z2, it2)

                in_turn(pool, steps, front, both)

        @block.tensor
        def _(pe):
            def heads(q, z, *terms):
                for p in range(PAIRS):
                    for par in range(2):
                        lo = par * CH
                        for n, (lhs, rhs) in enumerate(terms):
                            last = nc.tensor.matmul(quad(q, z)[lo:lo + CH, p * CH:(p + 1) * CH], lhs(z, p)[lo:lo + CH, :],
                                                    rhs(z, p)[lo:lo + CH, :], start=n == 0, stop=n == len(terms) - 1)
                return last

            block_of = lambda t: lambda z, p: pairs(t, z)[:, p, :]
            alpha, rho, beta, kappa = (block_of(t) for t in (T_alpha, T_rho, T_beta, T_kappa))
            m_, n_, p_ = (lambda z, p: m_of(z)[:, p, :]), block_of(T_n), (lambda z, p: p_of(z)[:, p, :])
            b_, ar, br = block_of(T_dec), block_of(T_beta), block_of(T_kappa)
            x_, sk, v_, st = m_, block_of(T_n), block_of(T_v), block_of(T_state)
            brow, krow = block_of(T_brow), block_of(T_krow)
            eye = lambda z, p: k.eye2[:, :]
            chunk_here(k, pe, k.c)
            pe.wait_ge(s.cleared, 4)
            for lat, steps, first, chunk, ev in phase_list():
                def wait(sem, value):
                    pe.wait_ge(sem, value)
                    pe.sem_inc(s.begun, 1)

                def after(who, z, it, name):
                    wait(ev[who][z].sem, ev[who][z].value(it, name))

                def low_rank(z, it):
                    if lat or not isinstance(it, int):
                        wait(ev["dve"][z].sem, ev["dve"][z].before(it))
                        wait(ev["act"][z].sem, ev["act"][z].before(it))
                    lo = z * CH
                    after("pool", z, it, "tokens")
                    for half in range(2):
                        last = nc.tensor.matmul(quad(0, z)[half * CH:(half + 1) * CH, :], twc[lo:lo + CH, :],
                                                w2[lo:lo + CH, half * BANK:(half + 1) * BANK], start=True, stop=True)
                    ev["pe"][z].done(last, "dec")
                    after("pool", z, it, "rates")
                    for p in range(PAIRS):
                        last = nc.tensor.matmul(quad3(2, z)[:, p, :], a2[lo:lo + CH, p * P:(p + 1) * P], tac[lo:lo + CH, :],
                                                start=True, stop=True)
                    ev["pe"][z].done(last, "iclr")

                def cumulate(z, it):
                    after("act", z, it, "decay_gate")
                    for p in range(PAIRS):
                        lo, at = p // 4 * CH, p % 4 * P
                        last = nc.tensor.matmul(bank(k, 4 * z + p // 4, P, at), own(T_dec, z)[lo:lo + CH, at:at + P],
                                                k.running[lo:lo + CH, z, :], start=True, stop=True)
                    ev["pe"][z].done(last, "cumulate")

                def bonus_sum(z, it):
                    after("dve", z, it, "bonus_in")
                    for p in range(PAIRS):
                        for par in range(2):
                            lo = par * CH
                            last = nc.tensor.matmul(quad(3, z)[lo:lo + CH, p:p + 1], pairs(T_dec, z)[lo:lo + CH, p, :],
                                                    k.head_ones[lo:lo + CH, lo:lo + 1], start=True, stop=True)
                    ev["pe"][z].done(last, "bonus")

                def front(z, it):
                    low_rank(z, it)
                    cumulate(z, it)
                    if lat:
                        bonus_sum(z, it)

                def both(z, it, z2, it2):
                    mine = ev["pe"][z]
                    after("dve", z, it, "kappa")
                    mine.done(heads(0, z, (beta, alpha)), "gram_m")
                    mine.done(heads(1, z, (alpha, beta)), "gram_n")
                    if z2 is not None:
                        low_rank(z2, it2)
                    mine.done(heads(2, z, (beta, eye)), "beta_rows")
                    if lat:
                        after("dve", z, it, "bonus")
                    mine.done(heads(3, z, (kappa, eye)), "kappa_rows")
                    after("dve", z, it, "first")
                    for n in range(1, DOUBLINGS):
                        if n > 1:
                            after("act", z, it, f"square{n - 1}")
                            after("dve", z, it, f"merged{n - 1}")
                        mine.done(heads(0, z, (m_, n_)), f"square{n}")
                        if n == 1:
                            after("act", z, it, "beta_rows")
                        else:
                            after("dve", z, it, f"product{n - 1}")
                        after("act", z, it, f"spread{n - 1}")
                        for p in range(PAIRS):
                            last = nc.tensor.matmul(bank(k, 4 * z + 1, P, p * P), n_wide(z)[:, p, :, :].rearrange("p h x -> p (h x)"),
                                                    mp(z)[:, p, :, :].rearrange("p e x -> p (e x)"), start=True, stop=True)
                        mine.done(last, f"merged{n}")
                        if n == 1:
                            after("act", z, it, "kappa_rows")
                            mine.done(heads(3, z, (kappa, alpha)), "gram_b")
                        elif lat and n == 2:
                            after("dve", z, it, "mask_b")
                            mine.done(heads(3, z, (beta, rho)), "gram_ar")
                        elif lat and n == 3:
                            after("dve", z, it, "mask_ar")
                            mine.done(heads(3, z, (kappa, rho)), "gram_br")
                        if z2 is not None and n == 2:
                            cumulate(z2, it2)
                        if z2 is not None and n == 4 and lat:
                            bonus_sum(z2, it2)
                    n = DOUBLINGS
                    after("act", z, it, f"square{n - 1}")
                    after("dve", z, it, f"merged{n - 1}")
                    mine.done(heads(0, z, (m_, n_)), f"square{n}")
                    after("dve", z, it, f"product{n - 1}")
                    after("act", z, it, f"spread{n - 1}")
                    for p in range(PAIRS):
                        last = nc.tensor.matmul(quad3(1, z)[:, p, :], n_wide(z)[:, p, :, :].rearrange("p h x -> p (h x)"),
                                                p_of(z)[:, p, :], start=True, stop=True)
                    mine.done(last, f"product{n}")
                    after("pool", z, it, "values")
                    after("dve", z, it, "mask_br" if lat else "mask_b")
                    mine.done(heads(3, z, (alpha, st), (b_, v_)), "start")
                    after("act", z, it, f"square{n}")
                    after("dve", z, it, f"product{n}")
                    mine.done(heads(2, z, (n_, p_)), f"product{n + 1}")
                    after("act", z, it, "start")
                    after("dve", z, it, f"product{n + 1}")
                    mine.done(heads(0, z, (p_, x_)), "sk")
                    after("act", z, it, "sk")
                    if lat:
                        mine.done(heads(1, z, (rho, st), (ar, sk), (br, v_)), "y")
                    mine.done(heads(2, z, (brow, sk), (krow, v_)), "state")

                in_turn(pe, steps, front, both)

        @block.scalar
        def _(act):
            act.wait_ge(s.cleared, 4)
            copy = lambda to, q, z: nc.scalar.activation(own(to, z), quad(q, z), ACT.Copy)
            for lat, steps, first, chunk, ev in phase_list():
                def after(who, z, it, name):
                    act.wait_ge(ev[who][z].sem, ev[who][z].value(it, name))

                def gates(z, it):
                    after("dve", z, it, "dec")
                    ev["act"][z].done(nc.scalar.activation(own(T_dec, z), own(T_dec, z), ACT.Sigmoid), "decay_gate")
                    after("dve", z, it, "iclr")
                    ev["act"][z].done(nc.scalar.activation(own(T_beta, z), own(T_beta, z), ACT.Sigmoid), "iclr_gate")

                def decays(z, it):
                    mine = ev["act"][z]
                    after("pe", z, it, "cumulate")
                    sums = bank(k, 4 * z, 2 * BANK).rearrange("p (a e x) -> p a e x", e=2, x=CH)
                    mine.done(nc.scalar.activation(pairs(T_rho, z), sums[:, :, 0, :], ACT.Exp, scale=-RATE), "d_inc")
                    mine.done(nc.scalar.activation(pairs(T_alpha, z), sums[:, :, 1, :], ACT.Exp, scale=-RATE), "d_exc")
                    mine.done(nc.scalar.activation(m_of(z), sums[:, :, 0, :], ACT.Exp, scale=RATE), "d_inv")

                def spread(z, n):
                    for par in range(2):
                        rows = slice(par * CH, (par + 1) * CH)
                        last = nc.scalar.activation(n_wide(z)[rows, :, par, :], pairs(T_n, z)[rows], ACT.Copy)
                    ev["act"][z].done(last, f"spread{n}")

                def front(z, it):
                    gates(z, it)
                    decays(z, it)

                def both(z, it, z2, it2):
                    mine = ev["act"][z]
                    after("dve", z, it, "mask_n")
                    spread(z, 0)
                    after("pe", z, it, "beta_rows")
                    mine.done(copy(T_brow, 2, z), "beta_rows")
                    after("pe", z, it, "kappa_rows")
                    mine.done(copy(T_krow, 3, z), "kappa_rows")
                    if z2 is not None:
                        gates(z2, it2)
                    for n in range(1, DOUBLINGS + 1):
                        after("pe", z, it, f"square{n}")
                        after("act", z, it, f"spread{n - 1}")
                        mine.done(copy(T_n, 0, z), f"square{n}")
                        if n < DOUBLINGS:
                            after("pe", z, it, f"merged{n}")
                            after("act", z, it, f"square{n}")
                            spread(z, n)
                        if z2 is not None and n == 2:
                            decays(z2, it2)
                    after("pe", z, it, "start")
                    mine.done(nc.scalar.activation(m_of(z), quad3(3, z), ACT.Copy), "start")
                    after("pe", z, it, "sk")
                    mine.done(copy(T_n, 0, z), "sk")

                in_turn(act, steps, front, both)

        @block.vector
        def _(dve):
            mask = lambda m, z: m[:, z, :].unsqueeze(1).to_broadcast([P, PAIRS, CH])
            spread = lambda c: c.unsqueeze(2).to_broadcast([P, PAIRS, CH])
            tt, stt = nc.vector.tensor_tensor, nc.vector.scalar_tensor_tensor
            dve.wait_ge(s.cleared, 4)
            for lat, steps, first, chunk, ev in phase_list():
                def after(who, z, it, name):
                    dve.wait_ge(ev[who][z].sem, ev[who][z].value(it, name))

                def tokens(t, z, it):
                    return t[:, :, bass.ds(columns_of(it, z, steps, first), CH)]

                def low_rank(z, it):
                    mine = ev["dve"][z]
                    after("pe", z, it, "dec")
                    mine.done(tt(own(T_dec, z), quad(0, z), own(w0, z), ALU.add), "dec")
                    after("pe", z, it, "iclr")
                    mine.done(tt(pairs(T_beta, z), quad3(2, z), spread(k.a0_cols[:, z * PAIRS:(z + 1) * PAIRS]), ALU.add), "iclr")

                def keys(z, it):
                    mine = ev["dve"][z]
                    after("act", z, it, "iclr_gate")
                    mine.done(stt(pairs(T_kappa, z), pairs(T_beta, z), -1.0, spread(k.ka_cols[:, :]), ALU.add, ALU.mult), "m")
                    after("dve", z, it, "m")
                    mine.done(stt(pairs(T_kappa, z), pairs(T_kappa, z), 1.0, tokens(K, z, it), ALU.add, ALU.mult), "kt")

                def rates(z, it):
                    mine = ev["dve"][z]
                    mine.done(tt(pairs(T_beta, z), pairs(T_beta, z), tokens(KK, z, it), ALU.mult), "akk")
                    if lat:
                        after("pe", z, it, "cumulate")
                        after("dve", z, it, "kt")
                        mine.done(tt(pairs(T_dec, z), pairs(T_kappa, z), tokens(R, z, it), ALU.mult), "bon")
                        after("dve", z, it, "bon")
                        mine.done(tt(pairs(T_dec, z), pairs(T_dec, z), spread(k.rk_cols[:, :]), ALU.mult), "bonus_in")

                def decayed_rows(z, it):
                    mine = ev["dve"][z]
                    after("act", z, it, "d_inv")
                    mine.done(tt(pairs(T_alpha, z), pairs(T_alpha, z), tokens(KK, z, it), ALU.mult), "alpha")
                    end = CH - 1 if z == 0 else 0
                    mine.done(nc.vector.tensor_copy(d_end[:, z * PAIRS:(z + 1) * PAIRS].unsqueeze(2),
                                                    pairs(T_rho, z)[:, :, end:end + 1]), "end")
                    if lat:
                        after("dve", z, it, "end")
                        mine.done(tt(pairs(T_rho, z), pairs(T_rho, z), tokens(R, z, it), ALU.mult), "rho")

                def raised_rows(z, it):
                    mine = ev["dve"][z]
                    after("dve", z, it, "akk")
                    mine.done(stt(pairs(T_beta, z), pairs(T_beta, z), -1.0, m_of(z), ALU.mult, ALU.mult), "beta")
                    after("dve", z, it, "bon" if lat else "kt")
                    mine.done(tt(pairs(T_kappa, z), pairs(T_kappa, z), m_of(z), ALU.mult), "kappa")

                def meet(z, it, name):
                    if z == 1:
                        after("dve", 0, it, name)
                    else:
                        after("dve", 1, it - 1, name)

                def bonus_out(z, it):
                    after("pe", z, it, "bonus")
                    meet(z, it, "bonus")
                    b = bonus[:, bass.ds(chunk_of(it, z, steps, chunk), 1), :]
                    ev["dve"][z].done(tt(b, b, quad(3, z)[:, 0:PAIRS].unsqueeze(1), ALU.add), "bonus")

                def front(z, it):
                    low_rank(z, it)
                    keys(z, it)
                    rates(z, it)
                    decayed_rows(z, it)
                    raised_rows(z, it)
                    if lat:
                        bonus_out(z, it)

                def both(z, it, z2, it2):
                    mine = ev["dve"][z]
                    after("pe", z, it, "gram_m")
                    after("dve", z, it, "kappa")
                    mine.done(tt(m_of(z), quad3(0, z), mask(k.before_m, z), ALU.mult), "mask_m")
                    after("pe", z, it, "gram_n")
                    mine.done(tt(pairs(T_n, z), quad3(1, z), mask(k.before_m, 1 - z), ALU.mult), "mask_n")
                    mine.done(nc.vector.tensor_copy(p_of(z), k.eye2[:, :].unsqueeze(1).to_broadcast([P, PAIRS, CH])), "first")
                    if z2 is not None:
                        low_rank(z2, it2)
                    both_of = bank(k, 4 * z + 1, 2 * BANK).rearrange("p (a e x) -> p a e x", e=2, x=CH)
                    for n in range(1, DOUBLINGS + 1):
                        if n < DOUBLINGS:
                            after("pe", z, it, f"merged{n}")
                            mine.done(nc.vector.tensor_copy(m_of(z), both_of[:, :, 0, :]), f"merged{n}")
                            after("dve", z, it, "first" if n == 1 else f"product{n - 1}")
                            mine.done(tt(p_of(z), p_of(z), both_of[:, :, 1, :], ALU.add), f"product{n}")
                        else:
                            for q in range(2):
                                after("pe", z, it, f"product{n + q}")
                                after("dve", z, it, f"product{n + q - 1}")
                                mine.done(tt(p_of(z), p_of(z), quad3(1 + q, z), ALU.add), f"product{n + q}")
                        if n == 1:
                            after("pe", z, it, "gram_b")
                            mine.done(tt(pairs(T_dec, z), quad3(3, z), mask(k.before_m, z), ALU.mult), "mask_b")
                        elif lat and n == 2:
                            after("pe", z, it, "gram_ar")
                            mine.done(tt(pairs(T_beta, z), quad3(3, z), mask(k.upto_m, z), ALU.mult), "mask_ar")
                        elif lat and n == 3:
                            after("pe", z, it, "gram_br")
                            mine.done(tt(pairs(T_kappa, z), quad3(3, z), mask(k.upto_m, z), ALU.mult), "mask_br")
                        if z2 is not None:
                            if n == 1:
                                keys(z2, it2)
                            elif n == 2:
                                rates(z2, it2)
                            elif n == 3:
                                decayed_rows(z2, it2)
                            elif n == 4:
                                raised_rows(z2, it2)
                            elif lat:
                                bonus_out(z2, it2)
                    if lat:
                        after("pe", z, it, "y")
                        meet(z, it, "y")
                        y = Y2[:, bass.ds(chunk_of(it, z, steps, chunk), 1), :]
                        mine.done(tt(y, y, quad(1, z).unsqueeze(1), ALU.add), "y")
                    after("pe", z, it, "state")
                    mine.done(tt(own(T_state, z), own(T_state, z), quad(2, z), ALU.add), "state")
                    after("dve", z, it, "state")
                    mine.done(tt(pairs(T_state, z), pairs(T_state, z), spread(d_end[:, z * PAIRS:(z + 1) * PAIRS]), ALU.mult),
                              "decayed")

                in_turn(dve, steps, front, both)


def rwkv_readout(k, Y, V, bonus, tg, lora2, mixT, spare, tables):
    nc = k.nc
    n_chunk = SEQ // CH
    g2 = lora2[:, 2 * D:3 * D]
    groups = n_chunk * PAIRS
    stat, ln, gateT = tables
    with stage(k, "restored vectors_here squared summed rooted step turned gate_made gate_out gated bonused") as (block, s):
        y3 = Y[:, :, :, :].rearrange("p c a i -> p (c a) i")
        v3 = V[:, 0:n_chunk, :, :].rearrange("p c a i -> p (c a) i")
        sq3 = spare.rearrange("p (g i) -> p g i", i=CH)
        over = lambda x: x.unsqueeze(2).to_broadcast([P, groups, CH])

        @block.sync
        def _(sp):
            sp.dma_start(k.X[:, 0:LT, :], k.x_saved).then_inc(s.restored, 16)
            for n, name in enumerate(("rw_ln_g_2", "rw_ln_b_2")):
                v = k.d[name][0].rearrange("(a h i) -> h a i", h=2, i=CH)
                for par in range(2):
                    sp.dma_start(ln[par * CH:(par + 1) * CH, n, :].rearrange("p (a i) -> p a i", i=CH),
                                 v[par].partition_broadcast(CH)).then_inc(s.vectors_here, 16)
            sp.wait_ge(s.restored, 16)

        @block.gpsimd
        def _(pool):
            nc.gpsimd.tensor_tensor(v3, v3, over(bonus[:, :, :].rearrange("p c a -> p (c a)")), ALU.mult).then_inc(s.bonused, 1)

        @block.vector
        def _(dve):
            chain = Chain(dve, s.step)
            chain(nc.vector.tensor_reduce(stat[:, 0, :], y3, AX.X, ALU.add))
            chain(nc.vector.tensor_scalar(stat[:, 0, :], stat[:, 0, :], 1.0 / CH, None, ALU.mult))
            chain(nc.vector.tensor_tensor(y3, y3, over(stat[:, 0, :]), ALU.subtract))
            dve.wait_ge(s.squared, 1)
            nc.vector.tensor_reduce(stat[:, 1, :], sq3, AX.X, ALU.add).then_inc(s.summed, 1)
            dve.wait_ge(s.rooted, 1)
            chain(nc.vector.reciprocal(stat[:, 3, :], stat[:, 2, :]))
            chain(nc.vector.tensor_tensor(y3, y3, over(stat[:, 3, :]), ALU.mult))
            yc = Y[:, :, :, :].rearrange("p c a i -> p c (a i)")
            row = lambda n: ln[:, n, :].unsqueeze(1).to_broadcast([P, n_chunk, PAIRS * CH])
            dve.wait_ge(s.vectors_here, 64)
            chain(nc.vector.tensor_tensor(yc, yc, row(0), ALU.mult))
            chain(nc.vector.tensor_tensor(yc, yc, row(1), ALU.add))
            dve.wait_ge(s.bonused, 1)
            chain(nc.vector.tensor_tensor(y3, y3, v3, ALU.add))
            for p in range(PAIRS):
                dve.wait_ge(s.turned, p + 1)
                dve.wait_ge(s.gate_out, p + 1)
                nc.vector.tensor_tensor(mixT[:, p, :], bank(k, p % 4), gateT[:, p % 2, :], ALU.mult).then_inc(s.gated, 1)

        @block.scalar
        def _(act):
            act.wait_ge(s.step, 3)
            nc.scalar.activation(sq3, y3, ACT.Square).then_inc(s.squared, 1)
            act.wait_ge(s.summed, 1)
            nc.scalar.activation(stat[:, 2, :], stat[:, 1, :], ACT.Sqrt, bias=64e-5, scale=1.0 / CH).then_inc(s.rooted, 1)
            for p in range(PAIRS):
                act.wait_ge(s.gate_made, p + 1)
                if p >= 2:
                    act.wait_ge(s.gated, p - 1)
                nc.scalar.activation(gateT[:, p % 2, :], bank(k, 4 + p % 4), ACT.Copy).then_inc(s.gate_out, 1)

        @block.tensor
        def _(pe):
            pe.wait_ge(s.step, 8)
            for p in range(PAIRS):
                if p >= 4:
                    pe.wait_ge(s.gated, p - 3)
                    pe.wait_ge(s.gate_out, p - 3)
                nc.tensor.matmul(bank(k, 4 + p % 4), g2[:, p * P:(p + 1) * P], tg[:, :], start=True,
                                 stop=True).then_inc(s.gate_made, 1)
                for c in range(n_chunk):
                    for par in range(2):
                        lo = par * CH
                        last = nc.tensor.matmul(bank(k, p % 4, CH, c * CH)[lo:lo + CH, :], Y[lo:lo + CH, c, p, :],
                                                k.eye2[lo:lo + CH, :], start=True, stop=True)
                last.then_inc(s.turned, 1)


def hold(k):
    with stage(k, "nothing") as (block, s):
        @block.sync
        def _(sp):
            for c in range(k.c, k.c + 3):
                if c + SLOTS < len(k.chunks):
                    load_chunk(k, sp, c + SLOTS)
    k.c += 3


def rwkv_layer(k):
    nc = k.nc
    A, B, C, E = k.big
    flat = lambda buf: buf[:, :, :].rearrange("p a b -> p (a b)")
    feat = lambda buf: flat(buf).rearrange("p (a b) -> p a b", a=KD)
    modulated_norm(k, 0, B, feat(A), SEGS2)
    with ExitStack() as mem:
        sb = lambda n, shape: mem.enter_context(nc.sbuf_tensor(f"rw_{n}", shape, F32))
        R = sb("R", [P, KD, SEQ])
        twc, tac = sb("twc", [P, CH]), sb("tac", [P, CH])
        d_end = sb("d_end", [P, DIRS * PAIRS])
        bonus = sb("bonus", [P, SEQ // CH, PAIRS])
        low = k.X[:, LT:LT + CT, :].rearrange("p a b -> p (a b)")
        tw, ta, tg = low[:, 0:TOK2], low[:, TOK2:2 * TOK2], low[:, 2 * TOK2:2 * TOK2 + SEQ]
        V = flat(C).rearrange("p (c a i) -> p c a i", c=TOK2 // CH, a=PAIRS)
        rwkv_project(k, feat(A), feat(E), (feat(B), feat(C)), tw, ta, tg, R, V, feat(E))
        K, KK = feat(E), feat(A)
        rwkv_keys(k, K, KK, flat(B)[:, 0:2 * TOK2].rearrange("p (a b) -> p a b", a=2), tw, tg)
        Y = flat(B)[:, 0:SEQ // CH * PAIRS * CH].rearrange("p (c a i) -> p c a i", c=SEQ // CH, a=PAIRS)
        left = flat(B)[:, SEQ // CH * PAIRS * CH:]
        slot = lambda n: k.ring[:, (k.c + n) % SLOTS].rearrange("p a b -> p (a b)")
        room = [left[:, 0:D], left[:, D:2 * D], k.gates[:, 1, :], k.gates[:, 3, :]]
        room += [slot(n)[:, x * D:(x + 1) * D] for n in (1, 2) for x in range(4)]
        rwkv_scan(k, K, KK, R, V, tw, ta, Y, bonus, slot(0), room, (twc, tac, d_end),
                  k.X[:, 0:DIRS, :].rearrange("p a b -> p (a b)"))
        mixT = flat(C)[:, 0:KD * SEQ].rearrange("p (a b) -> p a b", a=KD)
        room = flat(A)
        n = SEQ // CH * PAIRS
        tables = (room[:, 0:4 * n].rearrange("p (a b) -> p a b", a=4), room[:, D:2 * D].rearrange("p (a b) -> p a b", a=2),
                  room[:, 2 * D:3 * D].rearrange("p (a b) -> p a b", a=2))
        rwkv_readout(k, Y, V, bonus, tg, slot(0), mixT, flat(E)[:, 0:n * CH], tables)
    hold(k)
    add_projection(k, mixT, TILES2[:LT], k.X, lambda t: k.gates[:, 0, :])



def weight_chunks(d, layers):
    chunks = []
    for l in range(DEPTH):
        if f"hybrid{l}" in layers:
            w = d["w_in"][l]
            chunks += [columns(w, n) for n in (0, 1, 4, 5, 2, 6, 3, 7)]
            chunks += [columns(d["w_out"][l], n) for n in range(2)]
    p = {n: d[n + "_2"] for n in ("ada_w", "na_w_qkv", "na_w_o")}
    for l in range(DEPTH):
        if f"ada{l}" in layers:
            chunks += [columns(p["ada_w"][l], n) for n in range(SECTIONS * D // CHUNK)]
        if l == 0 and "na" in layers:
            chunks += [columns(p["na_w_qkv"][0], n) for n in range(6)] + [columns(p["na_w_o"][0], n) for n in range(2)]
        if l == 1 and "rwkv" in layers:
            chunks += rwkv_chunks(d)
        if f"moe{l}" in layers:
            chunks += [[(lambda slot: slot, expert_chunk(d, l, e, j))] for e in range(EXPERTS) for j in range(W_CHUNKS)]
    return chunks


RESIDENT = {
    "ident": [P, P],
    "norm_cols": [P, DEPTH, KD],
}
SECOND_RESIDENT = {
    "cond": [P, KD, 2], "norm1_cols": [P, DEPTH, KD], "norm2_cols": [P, DEPTH, KD], "pick_row": [2, 2, P],
    "na_q_cols": [P, 1], "na_k_cols": [P, 1], "col_mask": [P, GRID],
    "router": [P, DEPTH, KD, EXPERTS], "iota": [P, CAP_L],
    "mix_cols": [P, 6, KD], "kk_cols": [P, KD], "ka_cols": [P, PAIRS], "rk_cols": [P, PAIRS],
    "a0_cols": [P, DIRS * PAIRS], "running": [P, DIRS, 2 * CH], "before_m": [P, DIRS, CH],
    "upto_m": [P, DIRS, CH], "eye2": [P, CH], "head_ones": [P, P],
}
HYBRID_RESIDENT = {
    "rope_cos": [P, TOK], "rope_sin": [P, TOK], "rope_mirror": [P, P], "causal": [P, P],
    "pick_head": [FOX_HEADS, FOX_HEADS, P], "b_forget": [FOX_HEADS, DEPTH],
    "subln_cols": [P, DEPTH, DIFF_HEADS], "lam_vec": [P, DEPTH, 4, HEAD], "w_forget": [P, DEPTH, KD, FOX_HEADS],
}


def resident(k, mem, shapes):
    tiles = {n: mem.enter_context(k.nc.sbuf_tensor(f"{n}_sb", s, F32)) for n, s in shapes.items()}
    k.update(tiles)
    return tiles


def load_resident(k, sp, tiles, here):
    total = 0
    for name, t in tiles.items():
        src = k.d[name]
        if name == "lam_vec":
            src = src.partition_broadcast(P)
        sp.dma_start(t[:], src).then_inc(here, 16)
        total += 16
    return total


def build(nc, d, out, layers, dump):
    k = Named(nc=nc, d=d, stage_no=0, c=0)
    k.chunks = weight_chunks(d, layers)
    k.bias_rows = nc.dram_tensor("bias_rows", [NA_HEADS * REL_ROWS, GRID, PAD], F32).ap()
    k.x_saved = nc.dram_tensor("x_saved", [P, LT, D], F32).ap()
    with ExitStack() as mem:
        k.psum = mem.enter_context(nc.psum_tensor("psum", [P, BANKS * BANK], F32))
        k.ring = mem.enter_context(nc.sbuf_tensor("ring", [P, SLOTS, KD, CHUNK], F32))
        k.X = mem.enter_context(nc.sbuf_tensor("X", [P, LT + CT, D], F32))
        k.chunk_loaded = [nc.alloc_semaphore(f"chunk_loaded{n}") for n in range(SLOTS)]
        always = resident(k, mem, RESIDENT)
        with ExitStack() as first:
            mine = resident(k, first, HYBRID_RESIDENT)
            with stage(k, "here scaled") as (block, s):
                @block.sync
                def _(sp):
                    total = load_resident(k, sp, {**always, **mine}, s.here)
                    for t in range(LT):
                        sp.dma_start(k.X[:, t, :], d["x"][0, t * P:(t + 1) * P, :]).then_inc(s.here, 16)
                    sp.dma_start(k.X[0:NMETA, LT, :], d["meta_tokens"]).then_inc(s.here, 16)
                    for c in range(min(SLOTS, len(k.chunks))):
                        load_chunk(k, sp, c)
                    sp.wait_ge(s.here, total + 16 * (LT + 1))

                @block.vector
                def _(dve):
                    dve.wait_ge(s.here, 16 * (len(always) + len(mine) + LT + 1))
                    for l in range(DEPTH):
                        init = 0.8 - 0.6 * math.exp(-0.3 * l)
                        nc.vector.tensor_scalar(k.subln_cols[:, l, :], k.subln_cols[:, l, :], 1.0 - init, None,
                                                ALU.mult).then_inc(s.scaled, 1)
            for l in range(DEPTH):
                if f"hybrid{l}" in layers:
                    hybrid_layer(k, l)
            if "final" in layers:
                final_norm(k)
        with ExitStack() as second:
            sb = lambda n, shape: second.enter_context(nc.sbuf_tensor(n, shape, F32))
            mine = resident(k, second, SECOND_RESIDENT)
            k.big = [sb(f"big{n}", [P, LT + CT, D]) for n in range(4)]
            k.gates = sb("gates", [P, 4, D])
            k.mod_cols = sb("mod_cols", [P, 4, KD, 2])
            k.cond_silu = sb("cond_silu", [P, KD, 2])
            with stage(k, "here scaled") as (block, s):
                @block.sync
                def _(sp):
                    total = load_resident(k, sp, mine, s.here)
                    for t in range(CT):
                        sp.dma_start(k.X[:, LT + t, :], d["ctx_2"][0, t * P:(t + 1) * P, :]).then_inc(s.here, 16)
                    sp.wait_ge(s.here, total + 16 * CT)

                @block.vector
                def _(dve):
                    dve.wait_ge(s.here, 16 * (len(mine) + CT))
                    nc.vector.tensor_scalar(k.na_q_cols[:, :], k.na_q_cols[:, :], HEAD ** -0.5, None,
                                            ALU.mult).then_inc(s.scaled, 1)
            for l in range(DEPTH):
                if f"ada{l}" in layers:
                    modulation(k, l)
                if l == 0 and "na" in layers:
                    neighbour_layer(k, 0)
                if l == 1 and "rwkv" in layers:
                    rwkv_layer(k)
                if f"moe{l}" in layers:
                    expert_layer(k, l, l < DEPTH - 1)
        with k.nc.Block() as block:
            stored = nc.alloc_semaphore("stored")

            @block.sync
            def _(sp):
                for t in range(LT):
                    sp.dma_start(out[0, t * P:(t + 1) * P, :], k.X[:, t, :]).then_inc(stored, 16)
                n = LT
                if dump is not None:
                    sp.dma_start(dump[:, 0:CT * D], k.X[:, LT:LT + CT, :]).then_inc(stored, 16)
                    n += 1
                sp.wait_ge(stored, 16 * n)



def host_arrays(inputs):
    a = {n: np.ascontiguousarray(np.asarray(v)) for n, v in inputs.items()}
    f = np.float32
    a["ident"] = np.eye(P, dtype=f)
    half = HEAD // 2
    inv = f(10000.0) ** (-np.arange(half, dtype=f) / f(half))
    pos = np.concatenate([np.arange(NMETA, TOK), np.arange(NMETA)]).astype(f)
    ang = inv[np.arange(P) % half][:, None] * pos[None, :]
    a["rope_cos"], a["rope_sin"] = np.cos(ang).astype(f), np.sin(ang).astype(f)
    mirror = np.zeros((P, P), f)
    for p in range(P):
        if p % HEAD < half:
            mirror[p + half, p] = -1
        else:
            mirror[p - half, p] = 1
    a["rope_mirror"] = mirror
    a["causal"] = np.where(np.arange(P)[None, :] <= np.arange(P)[:, None], f(0), f(NEG))
    a["pick_head"] = np.repeat(np.eye(FOX_HEADS, dtype=f)[:, :, None], P, axis=2)
    cols = lambda v: np.ascontiguousarray(np.moveaxis(v.reshape(v.shape[:-1] + (-1, P)), -1, 0))
    a["norm_cols"] = cols(a["norm_g"])
    a["subln_cols"] = cols(a["subln_g"])
    a["b_forget"] = np.ascontiguousarray(a["b_forget"].T)
    a["lam_vec"] = np.stack([a["lam_q1"], a["lam_k1"], a["lam_q2"], a["lam_k2"]], axis=1)
    a["w_forget"] = np.ascontiguousarray(a["w_in"][:, :, 4096:].reshape(DEPTH, KD, P, FOX_HEADS).transpose(2, 0, 1, 3))
    a["cond"] = cols(np.stack([a["c_2"][0], a["c_ctx_2"]], axis=0)).transpose(0, 2, 1).copy()
    a["norm1_cols"], a["norm2_cols"] = cols(a["norm1_g_2"]), cols(a["norm2_g_2"])
    a["pick_row"] = np.repeat(np.eye(2, dtype=f)[:, :, None], P, axis=2)
    a["na_q_cols"], a["na_k_cols"] = (np.tile(a[n].T, (2, 1)) for n in ("na_q_g_2", "na_k_g_2"))
    c = np.arange(GRID)
    start = np.clip(c - WIN_COLS // 2, 0, GRID - WIN_COLS)[:, None]
    inside = (c[None, :] >= start) & (c[None, :] < start + WIN_COLS)
    a["col_mask"] = np.tile(np.where(inside, f(0), f(NEG)), (2, 1))
    a["router"] = np.ascontiguousarray(a["moe_router_2"].reshape(DEPTH, KD, P, EXPERTS).transpose(2, 0, 1, 3))
    a["iota"] = np.tile(np.arange(CAP_L, dtype=f), (P, 1))
    s_, t_ = np.meshgrid(np.arange(CH), np.arange(CH), indexing="ij")
    both = lambda fwd, bwd: np.ascontiguousarray(np.tile(np.stack([fwd, bwd], axis=1), (2, 1, 1)).astype(f))
    a["running"] = both(np.hstack([s_ <= t_, s_ < t_]), np.hstack([s_ >= t_, s_ > t_]))
    a["before_m"], a["upto_m"] = both(t_ > s_, t_ < s_), both(t_ >= s_, t_ <= s_)
    a["eye2"] = np.tile(np.eye(CH, dtype=f), (2, 1))
    a["head_ones"] = np.kron(np.eye(2, dtype=f), np.ones((CH, CH), f))
    a["mix_cols"], a["kk_cols"] = cols(a["rw_mix_2"][0]), cols(a["rw_k_k_2"][0])
    a["ka_cols"] = cols(a["rw_k_a_2"][0])
    a["rk_cols"] = cols(a["rw_r_k_2"][0].reshape(-1))
    a["a0_cols"] = cols(a["rw_a0_2"][0]).reshape(P, DIRS * PAIRS)
    return a


_TABLES_OF = {
    "norm_g", "subln_g", "lam_q1", "lam_k1", "lam_q2", "lam_k2", "c_2", "c_ctx_2", "norm1_g_2", "norm2_g_2",
    "na_q_g_2", "na_k_g_2", "moe_router_2", "rw_mix_2", "rw_k_k_2", "rw_k_a_2", "rw_r_k_2", "rw_a0_2",
}
_LAYERS = ("hybrid0", "hybrid1", "final", "ada0", "na", "moe0", "ada1", "rwkv", "moe1")


def kernel(**inputs):
    import concourse.bacc as _bacc
    from concourse import mybir as _mybir
    from concourse.bass_utils import run_bass_kernel_spmd as _run

    arrays = {n: v for n, v in host_arrays(inputs).items()
              if n not in _TABLES_OF and not n.startswith(("mla_", "swa_"))}
    nc = _bacc.Bacc("TRN2", target_bir_lowering=False, num_devices=1)
    d = {n: nc.dram_tensor(n, a.shape, _mybir.dt.from_np(a.dtype), kind="ExternalInput").ap() for n, a in arrays.items()}
    out = nc.dram_tensor("out", (1, SEQ, D), F32, kind="ExternalOutput").ap()
    build(nc, d, out, _LAYERS, None)
    r = _run(nc, [arrays], core_ids=[0])
    return r.results[0]["out"]
```

```python
from contextlib import ExitStack, contextmanager
import math

import numpy as np

import concourse.bass as bass
import concourse.mybir as mybir

F32 = mybir.dt.float32
ALU = mybir.AluOpType
ACT = mybir.ActivationFunctionType
AX = mybir.AxisListType

P = 128
BANK = 512
BANKS = 8
D = 1024
KD = D // P
SEQ = 512
LT = SEQ // P
NMETA = 16
CTX = 256
CT = CTX // P
DEPTH = 2
EPS = 1e-6
HEAD = 64
CHUNK = 512
SLOTS = 3
NEG = -1e30


class Named(dict):

    def __getattr__(self, name):
        return self[name]

    def __setattr__(self, name, value):
        self[name] = value


def bank(k, b, n=BANK, first=0):
    return k.psum[:, b * BANK + first:b * BANK + first + n]


@contextmanager
def stage(k, names):
    k.stage_no += 1
    sems = {n: k.nc.alloc_semaphore(f"{n}_{k.stage_no}") for n in names.split()}
    with k.nc.Block() as block:
        yield block, Named(sems)
    k.nc.clear_and_free_semaphores(list(sems.values()))
    k.nc.all_engine_barrier()


class Chain:

    def __init__(self, eng, sem, base=0):
        self.eng, self.sem, self.base, self.n = eng, sem, base, 0

    def __call__(self, ins):
        self.n += 1
        ins.then_inc(self.sem, 1)
        self.eng.wait_ge(self.sem, self.base + self.n)



def load_chunk(k, sp, c):
    slot = c % SLOTS
    for place, src in k.chunks[c]:
        sp.dma_start(place(k.ring[:, slot]), src).then_inc(k.chunk_loaded[slot], 16)


def feed(k, sp, c0, product, ends):
    for n, end in enumerate(ends):
        if c0 + n + SLOTS < len(k.chunks):
            sp.wait_ge(product, end)
            load_chunk(k, sp, c0 + n + SLOTS)


def chunk_here(k, pe, c):
    total = 16 * sum(len(k.chunks[x]) for x in range(c % SLOTS, c + 1, SLOTS))
    pe.wait_ge(k.chunk_loaded[c % SLOTS], total)
    return k.ring[:, c % SLOTS]


def columns(w, n):
    src = w[:, n * CHUNK:(n + 1) * CHUNK].rearrange("(a p) n -> p a n", p=P)
    return [(lambda slot: slot, src)]



def turn_count(segs):
    return len(segs) * KD


def turn_tensor(k, pe, s, src, segs):
    j = 0
    for tiles, rows, _ in segs:
        for a in range(KD):
            if j >= BANKS:
                pe.wait_ge((s.act_turned, s.dve_turned)[j % 2], (j - BANKS) // 2 + 1)
            for n, t in enumerate(tiles):
                last = k.nc.tensor.transpose(bank(k, j % BANKS, rows, n * rows),
                                             src[0:rows, t, a * P:(a + 1) * P], k.ident[0:rows, 0:rows])
            last.then_inc(s.turned, 1)
            j += 1


def turn_out(k, eng, s, dst, segs, scale, shift, mine):
    j = 0
    for g, (tiles, rows, col) in enumerate(segs):
        for a in range(KD):
            if j % 2 == mine:
                n = len(tiles) * rows
                eng.wait_ge(s.turned, j + 1)
                out, got = dst[:, a, col:col + n], bank(k, j % BANKS, n)
                sc = scale(g, a) if scale else 1.0
                sh = shift(g, a) if shift else 0.0
                if mine == 0:
                    k.nc.scalar.activation(out, got, ACT.Identity, bias=sh, scale=sc).then_inc(s.act_turned, 1)
                else:
                    k.nc.vector.tensor_scalar(out, got, sc, sh, ALU.mult, ALU.add).then_inc(s.dve_turned, 1)
            j += 1


def turn(k, src, dst, segs, scale=None, shift=None):
    with stage(k, "turned act_turned dve_turned") as (block, s):
        @block.tensor
        def _(pe):
            turn_tensor(k, pe, s, src, segs)

        @block.scalar
        def _(act):
            turn_out(k, act, s, dst, segs, scale, shift, 0)

        @block.vector
        def _(dve):
            turn_out(k, dve, s, dst, segs, scale, shift, 1)


def norm_turn(k, src, xn, dst, segs, scale, shift=None):
    nc = k.nc
    tiles = [(t, rows) for ts, rows, _ in segs for t in ts]
    with ExitStack() as mem, stage(k, "cleared summed rooted inverted normed turned act_turned dve_turned") as (block, s):
        junk = mem.enter_context(nc.sbuf_tensor(f"junk{k.stage_no}", [P, D], F32))
        stat = mem.enter_context(nc.sbuf_tensor(f"stat{k.stage_no}", [P, 3, 8], F32))

        @block.gpsimd
        def _(pool):
            nc.gpsimd.memset(stat[:, 0, :], 1.0).then_inc(s.cleared, 1)

        @block.scalar
        def _(act):
            act.wait_ge(s.cleared, 1)
            for n, (t, rows) in enumerate(tiles):
                if n:
                    act.wait_ge(s.summed, n)
                nc.scalar.activation(junk[0:rows, :], src[0:rows, t, :], ACT.Square,
                                     accum_out=stat[0:rows, 0, n:n + 1]).then_inc(s.summed, 1)
            act.wait_ge(s.summed, len(tiles))
            nc.scalar.activation(stat[:, 1, :], stat[:, 0, :], ACT.Sqrt, bias=EPS, scale=1.0 / D).then_inc(s.rooted, 1)
            turn_out(k, act, s, dst, segs, scale, shift, 0)

        @block.vector
        def _(dve):
            dve.wait_ge(s.rooted, 1)
            nc.vector.reciprocal(stat[:, 2, :], stat[:, 1, :]).then_inc(s.inverted, 1)
            dve.wait_ge(s.inverted, 1)
            for n, (t, rows) in enumerate(tiles):
                nc.vector.tensor_scalar(xn[0:rows, t, :], src[0:rows, t, :], stat[0:rows, 2, n:n + 1], None,
                                        ALU.mult).then_inc(s.normed, 1)
            turn_out(k, dve, s, dst, segs, scale, shift, 1)

        @block.tensor
        def _(pe):
            pe.wait_ge(s.normed, len(tiles))
            turn_tensor(k, pe, s, xn, segs)



TOK = SEQ + NMETA
HSEGS = [(list(range(LT)), P, 0), ([LT], NMETA, SEQ)]
HTILES = [(t, P) for t in range(LT)] + [(LT, NMETA)]
DIFF_HEADS = 4
FOX_HEADS = 8


def hybrid_project(k, l, uT, qkT, V, Z, zf):
    nc = k.nc
    c0 = k.c
    jobs = 16
    rows_jobs = 4 * len(HTILES)
    NH = TOK // 2
    halves = [slice(h * NH, (h + 1) * NH) for h in range(2)]
    META_PARTS = 4
    meta_part = lambda q: slice(q * P // META_PARTS, q * P // META_PARTS + NMETA)
    meta_cols = lambda q: slice(q * CHUNK // META_PARTS, (q + 1) * CHUNK // META_PARTS)
    with stage(k, "wf_here product act_out dve_out") as (block, s):
        @block.sync
        def _(sp):
            feed(k, sp, c0, s.product, [4 * (n + 1) for n in range(4)]
                 + [jobs + 1 + len(HTILES) * (n + 1) for n in range(4)])

        @block.tensor
        def _(pe):
            for j in range(jobs):
                c, f = c0 + j // 4, j % 4
                w = chunk_here(k, pe, c)
                if j >= 4:
                    pe.wait_ge(s.act_out, j - 3)
                    pe.wait_ge(s.dve_out, j - 3)
                for a in range(KD):
                    st = dict(start=a == 0, stop=a == KD - 1)
                    for h in range(2):
                        last = nc.tensor.matmul(bank(k, 2 * (j % 4) + h, NH), w[:, a, f * P:(f + 1) * P], uT[:, a, halves[h]], **st)
                last.then_inc(s.product, 1)
            pe.wait_ge(s.act_out, jobs)
            pe.wait_ge(s.dve_out, jobs)
            wf = k.w_forget[:, l]
            for a in range(KD):
                st = dict(start=a == 0, stop=a == KD - 1)
                for h in range(2):
                    last = nc.tensor.matmul(bank(k, h, NH)[0:FOX_HEADS, :], wf[:, a, :], uT[:, a, halves[h]], **st)
            last.then_inc(s.product, 1)
            for j in range(rows_jobs):
                c, (t, rows) = c0 + 4 + j // len(HTILES), HTILES[j % len(HTILES)]
                w = chunk_here(k, pe, c)
                b = 2 + j % 6
                if j >= 6:
                    pe.wait_ge((s.act_out, s.dve_out)[j % 2], jobs + 1 + (j - 6) // 2 + 1)
                for a in range(KD):
                    st = dict(start=a == 0, stop=a == KD - 1)
                    if rows == P:
                        last = nc.tensor.matmul(bank(k, b), uT[:, a, t * P:(t + 1) * P], w[:, a, :], **st)
                    else:
                        for q in range(META_PARTS):
                            last = nc.tensor.matmul(bank(k, b, CHUNK // META_PARTS)[meta_part(q), :], uT[:, a, SEQ:TOK],
                                                    w[:, a, meta_cols(q)], **st)
                last.then_inc(s.product, 1)

        def rows_out(eng, mine):
            for j in range(rows_jobs):
                if j % 2 != mine:
                    continue
                n, (t, rows) = j // len(HTILES), HTILES[j % len(HTILES)]
                eng.wait_ge(s.product, jobs + 1 + j + 1)
                got = bank(k, 2 + j % 6)
                out = (V, V, Z, Z)[n][0:rows, t, (n % 2) * CHUNK:(n % 2 + 1) * CHUNK]
                pairs = [(out, got)]
                if rows < P:
                    pairs = [(out[:, meta_cols(q)], got[meta_part(q), 0:CHUNK // META_PARTS]) for q in range(META_PARTS)]
                for into, part in pairs:
                    last = nc.scalar.activation(into, part, ACT.Copy) if mine == 0 else nc.vector.tensor_copy(into, part)
                last.then_inc((s.act_out, s.dve_out)[mine], 1)

        @block.scalar
        def _(act):
            for j in range(jobs):
                act.wait_ge(s.product, j + 1)
                nc.scalar.mul(qkT[:, j, halves[0]], bank(k, 2 * (j % 4), NH), (0.125, 1.0)[j // 4 % 2]).then_inc(s.act_out, 1)
            act.wait_ge(s.product, jobs + 1)
            nc.scalar.activation(zf[:, halves[0]], bank(k, 0, NH)[0:FOX_HEADS, :], ACT.Identity,
                                 bias=k.b_forget[:, l:l + 1]).then_inc(s.act_out, 1)
            rows_out(act, 0)

        @block.vector
        def _(dve):
            for j in range(jobs):
                dve.wait_ge(s.product, j + 1)
                nc.vector.tensor_scalar(qkT[:, j, halves[1]], bank(k, 2 * (j % 4) + 1, NH), (0.125, 1.0)[j // 4 % 2], None,
                                        ALU.mult).then_inc(s.dve_out, 1)
            dve.wait_ge(s.product, jobs + 1)
            nc.vector.tensor_scalar(zf[:, halves[1]], bank(k, 1, NH)[0:FOX_HEADS, :], k.b_forget[:, l:l + 1], None,
                                    ALU.add).then_inc(s.dve_out, 1)
            rows_out(dve, 1)
    k.c += 8


def hybrid_prepare(k, l, qkT, Z, zf, ncum, lam, spare):
    nc = k.nc
    lam_init = 0.8 - 0.6 * math.exp(-0.3 * l)
    with ExitStack() as mem, stage(k, "mirrored rotated act_step dve_step pool_step gated lam_exp") as (block, s):
        room = spare[:, :, :].rearrange("p a b -> p (a b)")
        spun = room[:, 0:2 * TOK].rearrange("p (a b) -> p a b", a=2)
        work = room[0:FOX_HEADS, 2 * TOK:6 * TOK].rearrange("p (a b) -> p a b", a=4)
        lam_junk = room[:, 6 * TOK:6 * TOK + 2 * HEAD].rearrange("p (a b) -> p a b", a=2)

        @block.tensor
        def _(pe):
            for j in range(8):
                if j >= 4:
                    pe.wait_ge(s.rotated, j - 3)
                nc.tensor.matmul(bank(k, 2 * (j % 4)), k.rope_mirror[:, :], qkT[:, j, 0:SEQ], start=True, stop=True)
                nc.tensor.matmul(bank(k, 2 * (j % 4) + 1, NMETA), k.rope_mirror[:, :], qkT[:, j, SEQ:TOK],
                                 start=True, stop=True).then_inc(s.mirrored, 1)

        @block.scalar
        def _(act):
            act.wait_ge(s.dve_step, 2)
            nc.scalar.activation(lam[:, 2:4], lam[:, 0:2], ACT.Exp).then_inc(s.lam_exp, 1)
            chain = Chain(act, s.act_step)
            chain(nc.scalar.activation(work[:, 0, :], zf[:, :], ACT.Abs))
            chain(nc.scalar.activation(work[:, 1, :], work[:, 0, :], ACT.Exp, scale=-1.0))
            chain(nc.scalar.activation(work[:, 0, :], work[:, 1, :], ACT.Ln, bias=1.0))
            for t, rows in HTILES:
                nc.scalar.activation(Z[0:rows, t, :], Z[0:rows, t, :], ACT.Silu).then_inc(s.gated, 1)

        @block.vector
        def _(dve):
            for m in range(2):
                nc.vector.tensor_tensor_reduce(lam_junk[:, m, :], k.lam_vec[:, l, 2 * m, :], k.lam_vec[:, l, 2 * m + 1, :],
                                               1.0, 0.0, ALU.mult, ALU.add, lam[:, m:m + 1]).then_inc(s.dve_step, 1)
            chain = Chain(dve, s.dve_step, 2)
            dve.wait_ge(s.lam_exp, 1)
            chain(nc.vector.scalar_tensor_tensor(lam[:, 4:5], lam[:, 3:4], -lam_init, lam[:, 2:3], ALU.add, ALU.subtract))
            chain(nc.vector.tensor_scalar(work[:, 2, :], zf[:, :], 0.0, None, ALU.min))
            chain(nc.vector.memset(work[:, 3, :], 1.0))
            dve.wait_ge(s.act_step, 3)
            chain(nc.vector.tensor_tensor(zf[:, :], work[:, 0, :], work[:, 2, :], ALU.subtract))
            chain(nc.vector.tensor_tensor_scan(ncum[:, SEQ:TOK], work[:, 3, 0:NMETA], zf[:, SEQ:TOK], 0.0, ALU.mult, ALU.add))
            chain(nc.vector.tensor_tensor_scan(ncum[:, 0:SEQ], work[:, 3, 0:SEQ], zf[:, 0:SEQ], ncum[:, TOK - 1:TOK],
                                               ALU.mult, ALU.add))
            for j in range(8):
                b = spun[:, j % 2, :]
                dve.wait_ge(s.mirrored, j + 1)
                nc.vector.tensor_tensor(b[:, 0:SEQ], bank(k, 2 * (j % 4)), k.rope_sin[:, 0:SEQ], ALU.mult)
                chain(nc.vector.tensor_tensor(b[:, SEQ:TOK], bank(k, 2 * (j % 4) + 1, NMETA), k.rope_sin[:, SEQ:TOK], ALU.mult))
                chain(nc.vector.tensor_tensor(qkT[:, j, :], qkT[:, j, :], k.rope_cos[:, :], ALU.mult))
                nc.vector.tensor_tensor(qkT[:, j, :], qkT[:, j, :], b, ALU.add).then_inc(s.rotated, 1)


def hybrid_units(last):
    units = []
    for i, rows in HTILES[:LT] if last else HTILES:
        nk = i + 1 if i < LT else 0
        for h in range(DIFF_HEADS):
            units.append((i, rows, nk, h, [(h, 4 + h, 0), (h, 4 + h, 1)]))
        for h in range(FOX_HEADS):
            units.append((i, rows, nk, DIFF_HEADS + h, [(8 + h // 2, 12 + h // 2, h % 2)]))
    return units


def hybrid_attend(k, qkT, V, Z, O, ncum, lam, spare, last_layer):
    nc = k.nc
    units = hybrid_units(last_layer)
    maps, first = [], []
    for u, unit in enumerate(units):
        first.append(len(maps))
        maps += [(u, m) for m in unit[4]]
    diff_before = lambda u: sum(len(x[4]) == 2 for x in units[:u])
    with ExitStack() as mem, stage(k, "scored masked peaked exped mixed flipped copied valued stored scaled") as (block, s):
        sb = lambda n, shape: mem.enter_context(nc.sbuf_tensor(f"{n}{k.stage_no}", shape, F32))
        room = spare[:, :, :].rearrange("p a b -> p (a b)")
        prob = room[:, 0:2 * TOK].rearrange("p (a b) -> p a b", a=2)
        probT = room[:, 2 * TOK:2 * TOK + 10 * P].rearrange("p (a b) -> p a b", a=2)
        stat = sb("stat", [P, 2, 4])

        def extent(nk):
            return nk * P + NMETA

        @block.tensor
        def _(pe):
            def scores(u):
                i, rows, nk, head, ms = units[u]
                for x, (qt, kt, half) in enumerate(ms):
                    m = first[u] + x
                    ps = bank(k, 2 * (m % 2), 2 * BANK)
                    if m >= 2:
                        pe.wait_ge(s.exped, m - 1)
                    lo = half * HEAD
                    parts = ([(0, nk * P, 0)] if nk else []) + [(nk * P, NMETA, SEQ)]
                    q = qkT[lo:lo + HEAD, qt, i * P:i * P + rows]
                    fox = head >= DIFF_HEADS
                    for at, n, key in parts:
                        last = nc.tensor.matmul(ps[0:rows, at:at + n], q, qkT[lo:lo + HEAD, kt, key:key + n],
                                                start=True, stop=not fox)
                        if fox:
                            last = nc.tensor.matmul(ps[0:rows, at:at + n], k.pick_head[:, head - DIFF_HEADS, 0:rows],
                                                    ncum[:, key:key + n], start=False, stop=True)
                    last.then_inc(s.scored, 1)

            def flip_over(u):
                i, rows, nk, head, ms = units[u]
                p = prob[:, first[u] % 2, :]
                flip = bank(k, 4, 2 * BANK)
                if len(ms) == 2:
                    pe.wait_ge(s.mixed, diff_before(u) + 1)
                else:
                    pe.wait_ge(s.exped, first[u] + 1)
                if u >= 1:
                    pe.wait_ge(s.copied, u)
                for j in range(nk):
                    nc.tensor.transpose(flip[:, j * P:j * P + rows], p[0:rows, j * P:(j + 1) * P], k.ident[0:rows, 0:rows])
                nc.tensor.transpose(flip[0:NMETA, nk * P:nk * P + rows], p[0:rows, nk * P:nk * P + NMETA],
                                    k.ident[0:rows, 0:rows]).then_inc(s.flipped, 1)

            def values(u):
                i, rows, nk, head, ms = units[u]
                pe.wait_ge(s.copied, u + 1)
                if u >= 2:
                    pe.wait_ge(s.stored, u - 1)
                pt = probT[:, u % 2, :]
                if head < DIFF_HEADS:
                    cols = slice(head * P, (head + 1) * P)
                else:
                    cols = slice(512 + (head - DIFF_HEADS) * HEAD, 512 + (head - DIFF_HEADS + 1) * HEAD)
                n = cols.stop - cols.start
                out = bank(k, 6 + u % 2, n)[0:rows, :]
                for j in range(nk):
                    nc.tensor.matmul(out, pt[:, j * P:j * P + rows], V[:, j, cols], start=j == 0, stop=False)
                nc.tensor.matmul(out, pt[0:NMETA, nk * P:nk * P + rows], V[0:NMETA, LT, cols], start=nk == 0,
                                 stop=True).then_inc(s.valued, 1)

            scores(0)
            for u in range(len(units)):
                early = u + 1 < len(units) and len(units[u][4]) == len(units[u + 1][4]) == 1
                if early:
                    scores(u + 1)
                if u >= 1:
                    values(u - 1)
                if u + 1 < len(units) and not early:
                    scores(u + 1)
                flip_over(u)
            values(len(units) - 1)

        @block.vector
        def _(dve):
            def peak(m):
                u, _ = maps[m]
                i, rows, nk, head, ms = units[u]
                ps = bank(k, 2 * (m % 2), 2 * BANK)
                at = (nk - 1) * P if nk else 0
                n = P if nk else NMETA
                dve.wait_ge(s.scored, m + 1)
                if m >= 2:
                    dve.wait_ge(s.exped, m - 1)
                nc.vector.tensor_tensor(ps[0:rows, at:at + n], ps[0:rows, at:at + n], k.causal[0:rows, 0:n],
                                        ALU.add).then_inc(s.masked, 1)
                dve.wait_ge(s.masked, m + 1)
                nc.vector.tensor_reduce(stat[0:rows, m % 2, 0:1], ps[0:rows, 0:extent(nk)], AX.X, ALU.max,
                                        negate=True).then_inc(s.peaked, 1)

            scaled = [0]

            def scale(ins):
                scaled[0] += 1
                ins.then_inc(s.scaled, 1)
                dve.wait_ge(s.scaled, scaled[0])

            def finish(u):
                i, rows, nk, head, ms = units[u]
                m = first[u]
                e = extent(nk)
                a, b = m % 2, (m + 1) % 2
                dve.wait_ge(s.exped, m + len(ms))
                if len(ms) == 2:
                    scale(nc.vector.reciprocal(stat[0:rows, b, 2:3], stat[0:rows, b, 1:2]))
                    scale(nc.vector.tensor_scalar(stat[0:rows, b, 3:4], stat[0:rows, a, 1:2], stat[0:rows, b, 2:3],
                                                  lam[0:rows, 4:5], ALU.mult, ALU.mult))
                    nc.vector.scalar_tensor_tensor(prob[0:rows, a, 0:e], prob[0:rows, b, 0:e], stat[0:rows, b, 3:4],
                                                   prob[0:rows, a, 0:e], ALU.mult, ALU.add).then_inc(s.mixed, 1)
                scale(nc.vector.reciprocal(keep[0:rows, u % 3, :], stat[0:rows, a, 1:2]))

            def store(u):
                i, rows, nk, head, ms = units[u]
                dve.wait_ge(s.valued, u + 1)
                if head < DIFF_HEADS:
                    nc.vector.tensor_scalar(O[0:rows, i, head * P:(head + 1) * P], bank(k, 6 + u % 2, P)[0:rows, :],
                                            keep[0:rows, u % 3, :], None, ALU.mult).then_inc(s.stored, 1)
                else:
                    c = 512 + (head - DIFF_HEADS) * HEAD
                    nc.vector.scalar_tensor_tensor(O[0:rows, i, c:c + HEAD], bank(k, 6 + u % 2, HEAD)[0:rows, :],
                                                   keep[0:rows, u % 3, :], Z[0:rows, i, c:c + HEAD],
                                                   ALU.mult, ALU.mult).then_inc(s.stored, 1)

            keep = sb("keep", [P, 3, 1])
            for x in range(len(units[0][4])):
                peak(x)
            for u in range(len(units)):
                early = u + 1 < len(units) and len(units[u][4]) == len(units[u + 1][4]) == 1
                if early:
                    peak(first[u + 1])
                finish(u)
                if u + 1 < len(units) and not early:
                    for x in range(len(units[u + 1][4])):
                        peak(first[u + 1] + x)
                if u >= 1:
                    store(u - 1)
            store(len(units) - 1)

        @block.scalar
        def _(act):
            def exponent(m):
                u, _ = maps[m]
                i, rows, nk, head, ms = units[u]
                e = extent(nk)
                act.wait_ge(s.peaked, m + 1)
                before = [v for v in range(u) if any((first[v] + x) % 2 == m % 2 for x in range(len(units[v][4])))]
                if before:
                    act.wait_ge(s.flipped, before[-1] + 1)
                    d = diff_before(before[-1] + 1)
                    if d:
                        act.wait_ge(s.mixed, d)
                nc.scalar.activation(prob[0:rows, m % 2, 0:e], bank(k, 2 * (m % 2), 2 * BANK)[0:rows, 0:e], ACT.Exp,
                                     bias=stat[0:rows, m % 2, 0:1], accum_out=stat[0:rows, m % 2, 1:2]).then_inc(s.exped, 1)

            def copy(u):
                i, rows, nk, head, ms = units[u]
                act.wait_ge(s.flipped, u + 1)
                if u >= 2:
                    act.wait_ge(s.valued, u - 1)
                flip = bank(k, 4, 2 * BANK)
                if nk:
                    nc.scalar.activation(probT[:, u % 2, 0:nk * P], flip[:, 0:nk * P], ACT.Copy)
                nc.scalar.activation(probT[0:NMETA, u % 2, nk * P:nk * P + rows], flip[0:NMETA, nk * P:nk * P + rows],
                                     ACT.Copy).then_inc(s.copied, 1)

            for x in range(len(units[0][4])):
                exponent(x)
            for u in range(len(units)):
                copy_next = u
                if u + 1 < len(units) and len(units[u + 1][4]) == 1 and len(units[u][4]) == 1:
                    exponent(first[u + 1])
                    copy(u)
                else:
                    copy(u)
                    if u + 1 < len(units):
                        for x in range(len(units[u + 1][4])):
                            exponent(first[u + 1] + x)


def hybrid_gate(k, O, Z, tiles):
    nc = k.nc
    with ExitStack() as mem, stage(k, "cleared summed rooted step") as (block, s):
        sb = lambda n, shape: mem.enter_context(nc.sbuf_tensor(f"{n}{k.stage_no}", shape, F32))
        sq = sb("sq", [P, 2, 512])
        stat = sb("stat", [P, 2, 5 * DIFF_HEADS])

        @block.gpsimd
        def _(pool):
            nc.gpsimd.memset(stat[:, 0, :], 1.0).then_inc(s.cleared, 1)

        @block.vector
        def _(dve):
            chain = Chain(dve, s.step)
            dve.wait_ge(s.cleared, 1)
            for t, rows in tiles:
                o = O[0:rows, t, 0:512]
                chain(nc.vector.tensor_tensor(sq[0:rows, t % 2, :], o, o, ALU.mult))
                nc.vector.tensor_reduce(stat[0:rows, 0, t * 4:t * 4 + 4],
                                        sq[0:rows, t % 2, :].rearrange("p (h d) -> p h d", h=4), AX.X,
                                        ALU.add).then_inc(s.summed, 1)
            dve.wait_ge(s.rooted, 1)
            chain(nc.vector.reciprocal(stat[:, 0, :], stat[:, 1, :]))
            for t, rows in tiles:
                o = O[0:rows, t, 0:512]
                chain(nc.vector.tensor_tensor(o.rearrange("p (h d) -> p h d", h=4), o.rearrange("p (h d) -> p h d", h=4),
                                              stat[0:rows, 0, t * 4:t * 4 + 4].unsqueeze(2).to_broadcast([rows, 4, P]),
                                              ALU.mult))
                chain(nc.vector.tensor_tensor(o, o, Z[0:rows, t, 0:512], ALU.mult))

        @block.scalar
        def _(act):
            act.wait_ge(s.summed, len(tiles))
            nc.scalar.activation(stat[:, 1, :], stat[:, 0, :], ACT.Sqrt, bias=EPS, scale=1.0 / P).then_inc(s.rooted, 1)


def add_projection(k, srcT, tiles, X, gate=None):
    nc = k.nc
    c0 = k.c
    jobs = [(n, t, rows) for n in range(2) for t, rows in tiles]
    with ExitStack() as mem, stage(k, "product added gated") as (block, s):
        if gate is not None:
            part = mem.enter_context(nc.sbuf_tensor(f"part{k.stage_no}", [P, 2, CHUNK], F32))

        @block.sync
        def _(sp):
            feed(k, sp, c0, s.product, [len(tiles) * (n + 1) for n in range(2)])

        @block.tensor
        def _(pe):
            for j, (n, t, rows) in enumerate(jobs):
                w = chunk_here(k, pe, c0 + n)
                if j >= BANKS:
                    pe.wait_ge(s.added, j - BANKS + 1)
                for a in range(KD):
                    last = nc.tensor.matmul(bank(k, j % BANKS)[0:rows, :], srcT[:, a, t * P:t * P + rows], w[:, a, :],
                                            start=a == 0, stop=a == KD - 1)
                last.then_inc(s.product, 1)

        @block.vector
        def _(dve):
            for j, (n, t, rows) in enumerate(jobs):
                dve.wait_ge(s.product, j + 1)
                x = X[0:rows, t, n * CHUNK:(n + 1) * CHUNK]
                got = bank(k, j % BANKS)[0:rows, :]
                if gate is not None:
                    nc.vector.tensor_tensor(part[0:rows, j % 2, :], got, gate(t)[:, n * CHUNK:(n + 1) * CHUNK],
                                            ALU.mult).then_inc(s.gated, 1)
                    dve.wait_ge(s.gated, j + 1)
                    got = part[0:rows, j % 2, :]
                nc.vector.tensor_tensor(x, x, got, ALU.add).then_inc(s.added, 1)
    k.c += 2


def hybrid_layer(k, l):
    nc = k.nc
    last = l == DEPTH - 1
    with ExitStack() as mem:
        sb = lambda n, shape: mem.enter_context(nc.sbuf_tensor(f"h{l}_{n}", shape, F32))
        uT = sb("uT", [P, KD, TOK])
        O = sb("O", [P, 5, D])
        norm_turn(k, k.X, O, uT, HSEGS, lambda g, a: k.norm_cols[:, l, a:a + 1])
        with ExitStack() as inner:
            sbi = lambda n, shape: inner.enter_context(nc.sbuf_tensor(f"h{l}_{n}", shape, F32))
            qkT = sbi("qkT", [P, 16, TOK])
            V = sbi("V", [P, 5, D])
            Z = sbi("Z", [P, 5, D])
            zf = sbi("zf", [FOX_HEADS, TOK])
            ncum = sbi("ncum", [FOX_HEADS, TOK])
            lam = sbi("lam", [P, 8])
            hybrid_project(k, l, uT, qkT, V, Z, zf)
            hybrid_prepare(k, l, qkT, Z, zf, ncum, lam, O)
            hybrid_attend(k, qkT, V, Z, O, ncum, lam, uT, last)
            tiles = HTILES[:LT] if last else HTILES
            hybrid_gate(k, O, Z, tiles)
        lam_init = 0.8 - 0.6 * math.exp(-0.3 * l)
        turn(k, O, uT, HSEGS[:1] if last else HSEGS,
             lambda g, a: k.subln_cols[:, l, a:a + 1] if a < 4 else 1.0)
        add_projection(k, uT, tiles, k.X)


def second_start(k, tiles, norm):
    nc = k.nc
    with ExitStack() as mem, stage(k, "here scaled summed rooted step gain_here") as (block, s):
        sb = lambda n, shape: mem.enter_context(nc.sbuf_tensor(f"{n}{k.stage_no}", shape, F32))
        junk, stat, gain = sb("junk", [P, D]), sb("stat", [P, 3, LT]), sb("gain", [P, D])

        @block.sync
        def _(sp):
            if norm:
                sp.dma_start(gain[:, :], k.d["final_g"].partition_broadcast(P)).then_inc(s.gain_here, 16)
            total = load_resident(k, sp, tiles, s.here)
            sp.wait_ge(k.bias_stored, 32)
            for t in range(CT):
                sp.dma_start(k.X[:, LT + t, :], k.d["ctx_2"][0, t * P:(t + 1) * P, :]).then_inc(s.here, 16)
            sp.wait_ge(s.here, total + 16 * CT)

        @block.scalar
        def _(act):
            if not norm:
                return
            for t in range(LT):
                if t:
                    act.wait_ge(s.summed, t)
                nc.scalar.activation(junk[:, :], k.X[:, t, :], ACT.Square,
                                     accum_out=stat[:, 0, t:t + 1]).then_inc(s.summed, 1)
            act.wait_ge(s.summed, LT)
            nc.scalar.activation(stat[:, 1, :], stat[:, 0, :], ACT.Sqrt, bias=EPS, scale=1.0 / D).then_inc(s.rooted, 1)

        @block.vector
        def _(dve):
            if norm:
                dve.wait_ge(s.rooted, 1)
                chain = Chain(dve, s.step)
                chain(nc.vector.reciprocal(stat[:, 2, :], stat[:, 1, :]))
                dve.wait_ge(s.gain_here, 16)
                for t in range(LT):
                    chain(nc.vector.scalar_tensor_tensor(k.X[:, t, :], k.X[:, t, :], stat[:, 2, t:t + 1], gain[:, :],
                                                         ALU.mult, ALU.mult))
            dve.wait_ge(s.here, 16 * (len(tiles) + CT))
            nc.vector.tensor_scalar(k.na_q_cols[:, :], k.na_q_cols[:, :], HEAD ** -0.5, None, ALU.mult).then_inc(s.scaled, 1)



TOK2 = SEQ + CTX
SEGS2 = [(list(range(LT)), P, 0), (list(range(LT, LT + CT)), P, SEQ)]
TILES2 = [(t, P) for t in range(LT + CT)]
SECTIONS = 6
SHIFT, GAIN = 0, 1


def modulation(k, l):
    nc = k.nc
    c0 = k.c
    n_chunks = SECTIONS * D // CHUNK
    mods = k.big[0][0:2, :, :].rearrange("p a b -> p (a b)")
    offset = k.big[1][0:2, :, :].rearrange("p a b -> p (a b)")
    PARTS = 4
    PW, CW = P // PARTS, CHUNK // PARTS
    with stage(k, "bias_here cond_ready product moved added turned columned gate_made gate_out step") as (block, s):
        @block.sync
        def _(sp):
            sp.dma_start(offset, k.d["ada_b_2"][l].partition_broadcast(2)).then_inc(s.bias_here, 16)
            feed(k, sp, c0, s.product, range(1, n_chunks + 1))

        @block.scalar
        def _(act):
            nc.scalar.activation(k.cond_silu[:, :, :], k.cond[:, :, :], ACT.Silu).then_inc(s.cond_ready, 1)
            for j in range(8):
                act.wait_ge(s.gate_made, j + 1)
                nc.scalar.activation(k.gates[:, j // 2, j % 2 * CHUNK:(j % 2 + 1) * CHUNK], bank(k, j % 4),
                                     ACT.Copy).then_inc(s.gate_out, 1)

        @block.tensor
        def _(pe):
            pe.wait_ge(s.cond_ready, 1)
            for n in range(n_chunks):
                w = chunk_here(k, pe, c0 + n)
                if n >= 6:
                    pe.wait_ge(s.added, n - 5)
                for a in range(KD):
                    for q in range(PARTS):
                        last = nc.tensor.matmul(bank(k, n % 6, CW)[q * PW:q * PW + 2, :], k.cond_silu[:, a, :],
                                                w[:, a, q * CW:(q + 1) * CW], start=a == 0, stop=a == KD - 1)
                last.then_inc(s.product, 1)
            pe.wait_ge(s.added, n_chunks)
            for x, sec in enumerate((0, 1, 3, 4)):
                for a in range(KD):
                    at = sec * D + a * P
                    last = nc.tensor.transpose(bank(k, 6, 2, (x * KD + a) * 2), mods[:, at:at + P], k.ident[0:2, 0:2])
            last.then_inc(s.turned, 1)
            for j in range(8):
                g, half = j // 2, j % 2
                at = (2, 5)[g // 2] * D + half * CHUNK
                if j >= 4:
                    pe.wait_ge(s.gate_out, j - 3)
                nc.tensor.matmul(bank(k, j % 4), k.pick_row[:, g % 2, :], mods[:, at:at + CHUNK],
                                 start=True, stop=True).then_inc(s.gate_made, 1)

        @block.vector
        def _(dve):
            dve.wait_ge(s.bias_here, 16)
            for n in range(n_chunks):
                dve.wait_ge(s.product, n + 1)
                for q in range(PARTS):
                    last = nc.vector.tensor_copy(mods[:, n * CHUNK + q * CW:n * CHUNK + (q + 1) * CW],
                                                 bank(k, n % 6, CW)[q * PW:q * PW + 2, :])
                last.then_inc(s.moved, 1)
                dve.wait_ge(s.moved, n + 1)
                m = mods[:, n * CHUNK:(n + 1) * CHUNK]
                nc.vector.tensor_tensor(m, m, offset[:, n * CHUNK:(n + 1) * CHUNK], ALU.add).then_inc(s.added, 1)
            dve.wait_ge(s.turned, 1)
            chain = Chain(dve, s.step)
            chain(nc.vector.tensor_copy(k.mod_cols[:, :, :, :].rearrange("p s a r -> p (s a r)"), bank(k, 6, 64)))
            for x, g in ((1, k.norm1_cols), (3, k.norm2_cols)):
                chain(nc.vector.scalar_tensor_tensor(k.mod_cols[:, x, :, :], k.mod_cols[:, x, :, :], 1.0,
                                                     g[:, l, :].unsqueeze(2).to_broadcast([P, KD, 2]), ALU.add, ALU.mult))
    k.c += n_chunks


def project_rows(k, srcT, tiles, outs):
    nc = k.nc
    c0 = k.c
    jobs = [(n, t, rows) for n in range(len(outs)) for t, rows in tiles]
    with stage(k, "product act_out dve_out") as (block, s):
        @block.sync
        def _(sp):
            feed(k, sp, c0, s.product, [len(tiles) * (n + 1) for n in range(len(outs))])

        @block.tensor
        def _(pe):
            for j, (n, t, rows) in enumerate(jobs):
                w = chunk_here(k, pe, c0 + n)
                if j >= BANKS:
                    pe.wait_ge((s.act_out, s.dve_out)[j % 2], (j - BANKS) // 2 + 1)
                for a in range(KD):
                    last = nc.tensor.matmul(bank(k, j % BANKS)[0:rows, :], srcT[:, a, t * P:t * P + rows], w[:, a, :],
                                            start=a == 0, stop=a == KD - 1)
                last.then_inc(s.product, 1)

        @block.scalar
        def _(act):
            for j in range(0, len(jobs), 2):
                n, t, rows = jobs[j]
                act.wait_ge(s.product, j + 1)
                nc.scalar.activation(outs[n](t), bank(k, j % BANKS)[0:rows, :], ACT.Copy).then_inc(s.act_out, 1)

        @block.vector
        def _(dve):
            for j in range(1, len(jobs), 2):
                n, t, rows = jobs[j]
                dve.wait_ge(s.product, j + 1)
                nc.vector.tensor_copy(outs[n](t), bank(k, j % BANKS)[0:rows, :]).then_inc(s.dve_out, 1)
    k.c += len(outs)


NA_HEADS = 16
GRID = 64
WIN_ROWS, WIN_COLS = 8, 16
REL_ROWS, REL_COLS = 2 * WIN_ROWS - 1, 2 * WIN_COLS - 1
PAD = 2 * GRID


def head_norm(k, rows3, tiles, eps_width):
    nc = k.nc
    heads = NA_HEADS
    with ExitStack() as mem, stage(k, "squared summed rooted step") as (block, s):
        sb = lambda n, shape: mem.enter_context(nc.sbuf_tensor(f"{n}{k.stage_no}", shape, F32))
        sq = sb("sq", [P, 2, D])
        stat = sb("stat", [P, 2, len(tiles) * heads])

        @block.scalar
        def _(act):
            for n, (t, rows) in enumerate(tiles):
                if n >= 2:
                    act.wait_ge(s.summed, n - 1)
                nc.scalar.activation(sq[:, n % 2, :], rows3[:, t, :], ACT.Square).then_inc(s.squared, 1)
            act.wait_ge(s.summed, len(tiles))
            nc.scalar.activation(stat[:, 1, :], stat[:, 0, :], ACT.Sqrt, bias=EPS, scale=1.0 / HEAD).then_inc(s.rooted, 1)

        @block.vector
        def _(dve):
            for n, (t, rows) in enumerate(tiles):
                dve.wait_ge(s.squared, n + 1)
                nc.vector.tensor_reduce(stat[:, 0, n * heads:(n + 1) * heads],
                                        sq[:, n % 2, :].rearrange("p (h d) -> p h d", h=heads), AX.X,
                                        ALU.add).then_inc(s.summed, 1)
            dve.wait_ge(s.rooted, 1)
            chain = Chain(dve, s.step)
            chain(nc.vector.reciprocal(stat[:, 0, :], stat[:, 1, :]))
            for n, (t, rows) in enumerate(tiles):
                x = rows3[:, t, :].rearrange("p (h d) -> p h d", h=heads)
                chain(nc.vector.tensor_tensor(x, x, stat[:, 0, n * heads:(n + 1) * heads].unsqueeze(2)
                                              .to_broadcast([P, heads, HEAD]), ALU.mult))


def load_bias(k, sp, pad, here):
    first = GRID - WIN_COLS
    src = k.d["na_rpb_2"][0].rearrange("h r c -> (h r) c").rearrange("(a p) c -> p a c", a=2)
    sp.dma_start(pad[0:src.shape[0], :, first:first + REL_COLS], src).then_inc(here, 16)


def store_bias(k, sp, pad):
    rows = NA_HEADS * REL_ROWS // 2
    for a in range(2):
        sp.dma_start(k.bias_rows[a * rows:(a + 1) * rows], pad[0:rows, a, :].unsqueeze(1).to_broadcast([rows, GRID, PAD])
                     ).then_inc(k.bias_stored, 16)


def neighbour_attend(k, qT, kT, V, oT):
    nc = k.nc
    tiles = LT + CT
    units = [(h, t) for h in range(NA_HEADS) for t in range(tiles)]
    lat_before = lambda u: u // tiles * LT + min(u % tiles, LT)
    with ExitStack() as mem, stage(k, "even_bias odd_bias biased scored masked peaked exped inverted scaled flipped copied valued stored") as (block, s):
        sb = lambda n, shape: mem.enter_context(nc.sbuf_tensor(f"{n}{k.stage_no}", shape, F32))
        bias = sb("bias", [P, 2, 16 * GRID])
        prob = sb("prob", [P, 2, TOK2])
        probT = sb("probT", [P, TOK2])
        stat = sb("stat", [P, 2, 3])

        def extent(t):
            return TOK2 if t < LT else CTX

        @block.sync
        def _(sp):
            for h in range(NA_HEADS):
                if h >= 2:
                    sp.wait_ge(s.masked, LT * (h - 1))
                for half in range(2):
                    src = bass.AP(tensor=k.bias_rows.tensor, offset=h * REL_ROWS * GRID * PAD + GRID - 1,
                                  ap=[[PAD - 1, GRID], [GRID * PAD, REL_ROWS], [1, GRID]])
                    dst = bias[half * GRID:(half + 1) * GRID, h % 2, half * GRID:half * GRID + REL_ROWS * GRID]
                    sp.dma_start(dst.rearrange("p (a b) -> p a b", b=GRID), src).then_inc((s.even_bias, s.odd_bias)[h % 2], 16)

        @block.tensor
        def _(pe):
            def scores(u):
                h, t = units[u]
                lo = h % 2 * HEAD
                ps = bank(k, 2 * (u % 2), 2 * BANK)
                if u >= 2:
                    pe.wait_ge(s.exped, u - 1)
                q = qT[lo:lo + HEAD, h // 2, t * P:(t + 1) * P]
                at = 0
                if t < LT:
                    nc.tensor.matmul(ps[:, 0:SEQ], q, kT[lo:lo + HEAD, h // 2, 0:SEQ], start=True, stop=True)
                    at = SEQ
                nc.tensor.matmul(ps[:, at:at + CTX], q, kT[lo:lo + HEAD, h // 2, SEQ:TOK2], start=True,
                                 stop=True).then_inc(s.scored, 1)

            def flip(u):
                flip = bank(k, 4, 2 * BANK)
                n = extent(units[u][1]) // P
                pe.wait_ge(s.scaled, u + 1)
                if u >= 1:
                    pe.wait_ge(s.copied, u)
                for j in range(n):
                    last = nc.tensor.transpose(flip[:, j * P:(j + 1) * P], prob[:, u % 2, j * P:(j + 1) * P], k.ident[:, :])
                last.then_inc(s.flipped, 1)

            def values(u):
                h, t = units[u]
                lo = h % 2 * HEAD
                n = extent(t) // P
                pe.wait_ge(s.copied, u + 1)
                if u >= 2:
                    pe.wait_ge(s.stored, u - 1)
                for j in range(n):
                    kt = j if t < LT else LT + j
                    last = nc.tensor.matmul(bank(k, 6 + u % 2, P)[lo:lo + HEAD, :], V[:, kt, h * HEAD:(h + 1) * HEAD],
                                            probT[:, j * P:(j + 1) * P], start=j == 0, stop=j == n - 1)
                last.then_inc(s.valued, 1)

            scores(0)
            for u in range(len(units)):
                if u + 1 < len(units):
                    scores(u + 1)
                if u >= 1:
                    values(u - 1)
                flip(u)
            values(len(units) - 1)

        @block.vector
        def _(dve):
            def peak(u):
                h, t = units[u]
                ps = bank(k, 2 * (u % 2), 2 * BANK)
                if t == 0:
                    dve.wait_ge((s.even_bias, s.odd_bias)[h % 2], 32 * (h // 2 + 1))
                    b = bias[:, h % 2, GRID:REL_ROWS * GRID].rearrange("p (a b) -> p a b", b=GRID)
                    nc.vector.tensor_tensor(b, b, k.col_mask[:, :].unsqueeze(1).to_broadcast([P, REL_ROWS - 1, GRID]),
                                            ALU.add).then_inc(s.biased, 1)
                    dve.wait_ge(s.biased, h + 1)
                dve.wait_ge(s.scored, u + 1)
                if t < LT:
                    first = (WIN_ROWS - 1 - 2 * t) * GRID
                    nc.vector.tensor_tensor(ps[:, 0:SEQ], ps[:, 0:SEQ], bias[:, h % 2, first:first + SEQ],
                                            ALU.add).then_inc(s.masked, 1)
                    dve.wait_ge(s.masked, lat_before(u) + 1)
                nc.vector.tensor_reduce(stat[:, u % 2, 0:1], ps[:, 0:extent(t)], AX.X, ALU.max,
                                        negate=True).then_inc(s.peaked, 1)

            def normalise(u):
                h, t = units[u]
                dve.wait_ge(s.exped, u + 1)
                nc.vector.reciprocal(stat[:, u % 2, 2:3], stat[:, u % 2, 1:2]).then_inc(s.inverted, 1)
                dve.wait_ge(s.inverted, u + 1)
                p = prob[:, u % 2, 0:extent(t)]
                nc.vector.tensor_scalar(p, p, stat[:, u % 2, 2:3], None, ALU.mult).then_inc(s.scaled, 1)

            def store(u):
                h, t = units[u]
                lo = h % 2 * HEAD
                dve.wait_ge(s.valued, u + 1)
                nc.vector.tensor_copy(oT[lo:lo + HEAD, h // 2, t * P:(t + 1) * P],
                                      bank(k, 6 + u % 2, P)[lo:lo + HEAD, :]).then_inc(s.stored, 1)

            peak(0)
            for u in range(len(units)):
                normalise(u)
                if u + 1 < len(units):
                    peak(u + 1)
                if u >= 1:
                    store(u - 1)
            store(len(units) - 1)

        @block.scalar
        def _(act):
            def exponent(u):
                h, t = units[u]
                act.wait_ge(s.peaked, u + 1)
                if u >= 2:
                    act.wait_ge(s.flipped, u - 1)
                nc.scalar.activation(prob[:, u % 2, 0:extent(t)], bank(k, 2 * (u % 2), extent(t)), ACT.Exp,
                                     bias=stat[:, u % 2, 0:1], accum_out=stat[:, u % 2, 1:2]).then_inc(s.exped, 1)

            exponent(0)
            for u in range(len(units)):
                if u + 1 < len(units):
                    exponent(u + 1)
                act.wait_ge(s.flipped, u + 1)
                if u >= 1:
                    act.wait_ge(s.valued, u)
                n = extent(units[u][1])
                nc.scalar.activation(probT[:, 0:n], bank(k, 4, n), ACT.Copy).then_inc(s.copied, 1)


def modulated_norm(k, which, xn, dst, segs):
    col = lambda x: lambda g, a: k.mod_cols[:, 2 * which + x, a, g:g + 1]
    norm_turn(k, k.X, xn, dst, segs, col(GAIN), col(SHIFT))


def neighbour_layer(k, j):
    A, B, C, V = k.big
    feat = lambda buf: buf[:, :, :].rearrange("p a b -> p (a b)").rearrange("p (a b) -> p a b", a=KD)
    modulated_norm(k, 0, B, feat(A), SEGS2)
    place = lambda buf, n: lambda t: buf[:, t, n * CHUNK:(n + 1) * CHUNK]
    project_rows(k, feat(A), TILES2, [place(buf, n) for buf in (B, C, V) for n in range(2)])
    head_norm(k, B, TILES2, HEAD)
    head_norm(k, C, TILES2, HEAD)
    turn(k, B, feat(A), SEGS2, lambda g, a: k.na_q_cols[:, j:j + 1])
    turn(k, C, feat(B), SEGS2, lambda g, a: k.na_k_cols[:, j:j + 1])
    neighbour_attend(k, feat(A), feat(B), V, feat(C))
    add_projection(k, feat(C), TILES2, k.X, lambda t: k.gates[:, 0 if t < LT else 1, :])



EXPERTS = 16
CAP_L, CAP_C = 2 * SEQ // EXPERTS, 2 * CTX // EXPERTS
ROUND = 4
EPAD = EXPERTS + ROUND
W_CHUNKS = 6


def expert_chunk(d, l, e, j):
    name = ("moe_w1_2", "moe_w3_2", "moe_w1_2", "moe_w3_2", "moe_w2_2", "moe_w2_2")[j]
    half = (0, 0, 1, 1, 0, 1)[j]
    return d[name][l, e].rearrange("(a p) n -> p a n", p=P)[:, :, half * CHUNK:(half + 1) * CHUNK]


def route(k, l, hT, aff, slot, tiles):
    nc = k.nc
    streams = [(0, SEQ, CAP_L)] + ([(SEQ, CTX, CAP_C)] if len(tiles) > LT else [])
    n_tok = sum(n for _, n, _ in streams)
    nt = len(tiles)
    with ExitStack() as mem, stage(k, "logits exped turned placed step ready") as (block, s):
        sb = lambda n, shape: mem.enter_context(nc.sbuf_tensor(f"{n}{k.stage_no}", shape, F32))
        stat = sb("stat", [P, 2, 8])
        affT, left, rank = sb("affT", [EXPERTS, TOK2]), sb("left", [EXPERTS, TOK2]), sb("rank", [EXPERTS, TOK2])
        ones = sb("ones", [EXPERTS, SEQ])
        best = sb("best", [EXPERTS, 8])
        raw = sb("raw", [P, nt, EXPERTS])

        @block.tensor
        def _(pe):
            for t in range(nt):
                for a in range(KD):
                    last = nc.tensor.matmul(bank(k, 0, EXPERTS, t * EXPERTS), hT[:, a, t * P:(t + 1) * P],
                                            k.router[:, l, a, :], start=a == 0, stop=a == KD - 1)
            last.then_inc(s.logits, 1)
            pe.wait_ge(s.ready, 1)
            for t in range(nt):
                last = nc.tensor.transpose(bank(k, 1, P, t * P)[0:EXPERTS, :], aff[:, t, 0:EXPERTS], k.ident[:, :])
            last.then_inc(s.turned, 1)
            pe.wait_ge(s.ready, 2)
            for t in range(nt):
                last = nc.tensor.transpose(bank(k, 3, EXPERTS, t * EXPERTS), rank[:, t * P:(t + 1) * P],
                                           k.ident[0:EXPERTS, 0:EXPERTS])
            last.then_inc(s.placed, 1)

        @block.scalar
        def _(act):
            act.wait_ge(s.step, 4)
            nc.scalar.activation(raw[:, :, :], raw[:, :, :], ACT.Exp).then_inc(s.exped, 1)

        @block.vector
        def _(dve):
            chain = Chain(dve, s.step)
            chain(nc.vector.memset(slot[:, :, :], -1.0))
            chain(nc.vector.memset(aff[:, :, :], 0.0))
            dve.wait_ge(s.logits, 1)
            lg = bank(k, 0, nt * EXPERTS).rearrange("p (t e) -> p t e", t=nt)
            wide = lambda x: x.unsqueeze(2).to_broadcast([P, nt, EXPERTS])
            chain(nc.vector.tensor_reduce(stat[:, 0, 0:nt], lg, AX.X, ALU.max))
            chain(nc.vector.tensor_tensor(raw[:, :, :], lg, wide(stat[:, 0, 0:nt]), ALU.subtract))
            dve.wait_ge(s.exped, 1)
            chain(nc.vector.tensor_reduce(stat[:, 0, 0:nt], raw[:, :, :], AX.X, ALU.add))
            chain(nc.vector.reciprocal(stat[:, 1, 0:nt], stat[:, 0, 0:nt]))
            nc.vector.tensor_tensor(aff[:, 0:nt, 0:EXPERTS], raw[:, :, :], wide(stat[:, 1, 0:nt]), ALU.mult).then_inc(s.ready, 1)
            chain(nc.vector.memset(ones[:, :], 1.0))
            dve.wait_ge(s.turned, 1)
            chain(nc.vector.tensor_copy(affT[:, 0:n_tok], bank(k, 1, n_tok)[0:EXPERTS, :]))
            chain(nc.vector.tensor_copy(left[:, 0:n_tok], affT[:, 0:n_tok]))
            for first, n, cap in streams:
                row = left[:, first:first + n]
                for _ in range(cap // 8):
                    chain(nc.vector.max(best[:, :], row))
                    chain(nc.vector.match_replace(row, best[:, :], row, -1.0))
            chosen = left[:, 0:n_tok]
            chain(nc.vector.tensor_scalar(chosen, chosen, 0.0, None, ALU.is_lt))
            for first, n, cap in streams:
                chain(nc.vector.tensor_tensor_scan(rank[:, first:first + n], ones[:, 0:n], left[:, first:first + n], 0.0,
                                                   ALU.mult, ALU.add))
            chain(nc.vector.tensor_tensor(rank[:, 0:n_tok], rank[:, 0:n_tok], chosen, ALU.mult))
            nc.vector.tensor_scalar(rank[:, 0:n_tok], rank[:, 0:n_tok], -1.0, None, ALU.add).then_inc(s.ready, 1)
            dve.wait_ge(s.placed, 1)
            chain(nc.vector.tensor_copy(slot[:, 0:nt, 0:EXPERTS], bank(k, 3, nt * EXPERTS)
                                        .rearrange("p (t e) -> p t e", t=nt)))


def experts(k, l, xn, aff, slot, acc, room_a, room_b, with_ctx):
    nc = k.nc
    c0 = k.c
    M = CAP_L + (CAP_C if with_ctx else 0)
    nt = LT + (CT if with_ctx else 0)
    jobs = [(t, half) for t in range(nt) for half in range(2)]
    CJ = len(jobs)
    Stream = lambda first, n, at: Named(first=first, n=n, at=at, parts=P // n, width=CHUNK * n // P)
    streams = [Stream(0, CAP_L, 0)]
    if with_ctx:
        streams.append(Stream(CAP_L, CAP_C, streams[0].width))
    W = sum(r.width for r in streams)
    flat_a = room_a[:, :, :].rearrange("p a b -> p (a b)")
    flat_b = room_b[:, :, :].rearrange("p a b -> p (a b)")

    def carve(flat, at, *dims):
        n = math.prod(dims)
        letters = "abcd"[:len(dims)]
        pat = f"p ({' '.join(letters)}) -> p {' '.join(letters)}"
        return flat[:, at:at + n].rearrange(pat, **dict(zip(letters, dims))), at + n

    onehot, at = carve(flat_a, 0, 2, LT + CT, 2 * CAP_L)
    gate_tok, at = carve(flat_a, at, 2, (LT + CT) * 2)
    xinT, at = carve(flat_a, at, 4, KD, M)
    hidT, at = carve(flat_a, at, KD, M)
    assert at <= (LT + CT) * D
    HALF_K = KD // 2
    y2, at = carve(flat_b, 0, 2, CHUNK)
    backT, at = carve(flat_b, at, 2, SEQ)
    yc, at = carve(flat_b, at, 2, CHUNK)
    hid, at = carve(flat_b, at, 2, CHUNK)
    silu, at = carve(flat_b, at, 2, CHUNK)
    backC, at = carve(flat_b, at, 2, CTX)
    gate_row, at = carve(flat_b, at, 2, 2)
    assert at <= (LT + CT) * D

    with stage(k, "cleared onehot gathered xin_ready turned_back back_copied up silued hid_ready flipped hid_copied down y_ready "
                  "combined added weighted") as (block, s):
        loaded0 = [16 * sum(len(k.chunks[x]) for x in range(n, c0, SLOTS)) for n in range(SLOTS)]

        @block.gpsimd
        def _(pool):
            for x in (y2, yc, backT[:, 1, :], backC[:, 1, :]):
                nc.gpsimd.memset(x, 0.0).then_inc(s.cleared, 1)
            for t in range(nt):
                nc.gpsimd.memset(acc[:, t, :], 0.0).then_inc(s.cleared, 1)

        @block.sync
        def _(sp):
            for e in range(EXPERTS):
                for j in range(W_CHUNKS):
                    c = c0 + e * W_CHUNKS + j + SLOTS
                    if c < len(k.chunks):
                        if j < 4:
                            sp.wait_ge(s.up, e * 4 + j + 1)
                        else:
                            sp.wait_ge(s.down, e * 2 + j - 3)
                        load_chunk(k, sp, c)

        @block.tensor
        def _(pe):
            def weights(e, j):
                n = (c0 + j) % SLOTS
                pe.wait_ge(k.chunk_loaded[n], e * (16 * W_CHUNKS // SLOTS) + loaded0[n] + 16 * (j // SLOTS + 1))
                return k.ring[:, n]

            def gather(pair, b, h):
                for n in range(HALF_K):
                    a = h * HALF_K + n
                    for t in range(LT):
                        last = nc.tensor.matmul(bank(k, 4, 2 * CAP_L, n * 2 * CAP_L), xn[:, t, a * P:(a + 1) * P], onehot[:, b, t, :],
                                                start=t == 0, stop=t == LT - 1)
                    for t in range(LT, nt):
                        last = nc.tensor.matmul(bank(k, 5, 2 * CAP_C, n * 2 * CAP_C), xn[:, t, a * P:(a + 1) * P],
                                                onehot[:, b, t, :].rearrange("p (x c) -> p x c", x=2)[:, :, 0:CAP_C],
                                                start=t == LT, stop=t == nt - 1)
                return last

            def way_back(y):
                b, x = y // 2, y % 2
                of = lambda t, n: onehot[:, b, t, x * CAP_L:x * CAP_L + n]
                gate = lambda t: gate_tok[:, b, 2 * t + x:2 * t + x + 1]
                for t in range(LT):
                    nc.tensor.matmul(bank(k, 5, 1, 300)[0:CAP_L, :], of(t, CAP_L), gate(t), start=t == 0, stop=t == LT - 1)
                for t in range(LT, nt):
                    nc.tensor.matmul(bank(k, 5, 1, 301)[0:CAP_C, :], of(t, CAP_C), gate(t), start=t == LT, stop=t == nt - 1)
                for t in range(LT, nt):
                    nc.tensor.transpose(bank(k, 7, P, (t - LT) * P)[0:CAP_C, :], of(t, CAP_C), k.ident[:, :])
                for t in range(LT):
                    last = nc.tensor.transpose(bank(k, 6, P, t * P)[0:CAP_L, :], of(t, CAP_L), k.ident[:, :])
                return last

            def rows_by(rowsT, w, b, second_half=None):
                for r in streams:
                    for a in range(KD):
                        if second_half is not None and r.first == 0 and a == HALF_K:
                            pe.wait_ge(s.hid_copied, second_half)
                        for q in range(r.parts):
                            last = nc.tensor.matmul(bank(k, b, r.width, r.at)[q * r.n:(q + 1) * r.n, :],
                                                    rowsT[:, a, r.first:r.first + r.n], w[:, a, q * r.width:(q + 1) * r.width],
                                                    start=a == 0, stop=a == KD - 1)
                return last

            def fetch(e, x):
                pe.wait_ge(s.onehot, it * (ROUND // 2) + (x // 2 + 2))
                pe.wait_ge(s.xin_ready, e + 2)
                pe.wait_ge(s.back_copied, e + 1)
                gather(x // 2 + 1, 1 - x // 2, x % 2).then_inc(s.gathered, 1)

            def give_back(e, pair, before):
                pe.wait_ge(s.back_copied, e + 1)
                for j, (t, half) in enumerate(jobs):
                    if j >= 2:
                        pe.wait_ge(s.added, before + j - 1)
                    if t < LT:
                        nc.tensor.matmul(bank(k, 6 + j % 2), backT[:, pair, t * P:(t + 1) * P], y2[:, half, :],
                                         start=True, stop=True).then_inc(s.combined, 1)
                    else:
                        nc.tensor.matmul(bank(k, 6 + j % 2), backC[0:2 * CAP_C, pair, (t - LT) * P:(t - LT + 1) * P],
                                         yc[0:2 * CAP_C, half, :], start=True, stop=True).then_inc(s.combined, 1)

            pe.wait_ge(s.cleared, 4)
            pe.wait_ge(s.onehot, 1)
            gather(0, 0, 0).then_inc(s.gathered, 1)
            pe.wait_ge(s.xin_ready, 1)
            gather(0, 0, 1).then_inc(s.gathered, 1)
            pe.wait_ge(s.xin_ready, 2)
            way_back(0).then_inc(s.turned_back, 1)
            with pe.Fori(0, EXPERTS // ROUND) as it:
                for x in range(ROUND):
                    e = it * ROUND + x
                    before = it * (2 * CJ) + x // 2 * CJ
                    pe.wait_ge(s.xin_ready, it * ROUND + (x // 2 * 2 + 2))
                    for j in range(4):
                        w = weights(e, j)
                        pe.wait_ge((s.hid_copied, s.y_ready)[j // 2], e * 2)
                        rows_by(xinT[:, x], w, j).then_inc(s.up, 1)
                        if x % 2 == 0 and j == 1:
                            pe.wait_ge(s.y_ready, e * 2)
                            give_back(e, 1 - x // 2, before)
                        if j == 2:
                            fetch(e, x)
                    for half in range(2):
                        pe.wait_ge(s.hid_ready, e * 2 + half + 1)
                        for f in range(W // P):
                            last = nc.tensor.transpose(bank(k, half, P, f * P), hid[:, half, f * P:(f + 1) * P], k.ident[:, :])
                        last.then_inc(s.flipped, 1)
                        if half == 0:
                            pe.wait_ge(s.xin_ready, e + 3)
                            pe.wait_ge(s.added, before + CJ)
                            way_back((x + 1) % ROUND).then_inc(s.turned_back, 1)
                    pe.wait_ge(s.hid_copied, e * 2 + 1)
                    for j in range(4, 6):
                        w = weights(e, j)
                        rows_by(hidT, w, j - 2, e * 2 + 2 if j == 4 else None).then_inc(s.down, 1)
            pe.wait_ge(s.y_ready, EXPERTS * 2)
            give_back(EXPERTS, 1, EXPERTS // 2 * CJ)

        @block.scalar
        def _(act):
            def way_back(e, b, pair, row):
                act.wait_ge(s.turned_back, e + 1)
                if with_ctx:
                    nc.scalar.activation(backC[row * CAP_C:(row + 1) * CAP_C, pair, :], bank(k, 7, CTX)[0:CAP_C, :], ACT.Copy)
                nc.scalar.activation(backT[row * CAP_L:(row + 1) * CAP_L, pair, :], bank(k, 6)[0:CAP_L, :],
                                     ACT.Copy)
                for n, r in enumerate(streams):
                    for q in range(r.parts):
                        last = nc.scalar.activation(gate_row[q * r.n:(q + 1) * r.n, b, n:n + 1], bank(k, 5, 1, 300 + n)[0:r.n, :],
                                                    ACT.Copy)
                last.then_inc(s.back_copied, 1)

            act.wait_ge(s.cleared, 4)
            way_back(0, 0, 0, 0)
            with act.Fori(0, EXPERTS // ROUND) as it:
                for x in range(ROUND):
                    e = it * ROUND + x
                    for half in range(2):
                        act.wait_ge(s.up, e * 4 + 2 * half + 1)
                        nc.scalar.activation(silu[:, half, 0:W], bank(k, 2 * half, W), ACT.Silu).then_inc(s.silued, 1)
                    for half in range(2):
                        if half == 1:
                            y = (x + 1) % ROUND
                            way_back(e + 1, y % 2, y // 2, y % 2)
                        act.wait_ge(s.flipped, e * 2 + half + 1)
                        for r in streams:
                            into = hidT[:, half * 4:half * 4 + 4, r.first:r.first + r.n].rearrange("p (q f) m -> p f q m", q=r.parts)
                            got = bank(k, half, r.width, r.at).rearrange("p (f q m) -> p f q m", q=r.parts, m=r.n)
                            last = nc.scalar.activation(into, got, ACT.Copy)
                        last.then_inc(s.hid_copied, 1)

        @block.vector
        def _(dve):
            def choose(e, b):
                nc.vector.tensor_copy(gate_tok[:, b, 0:2 * nt].rearrange("p (t x) -> p t x", x=2), aff[:, 0:nt, bass.ds(e, 2)])
                for x in range(2):
                    last = nc.vector.tensor_tensor(onehot[:, b, 0:nt, x * CAP_L:(x + 1) * CAP_L],
                                                   k.iota[:, :].unsqueeze(1).to_broadcast([P, nt, CAP_L]),
                                                   slot[:, 0:nt, bass.ds(e + x, 1)].to_broadcast([P, nt, CAP_L]), ALU.is_equal)
                last.then_inc(s.onehot, 1)

            def modulate(part, b, h):
                rows = lambda x, r: xinT[:, 2 * b + x, h * HALF_K:(h + 1) * HALF_K, r.first:r.first + r.n]
                col = lambda c, m, r: k.mod_cols[:, 2 + c, h * HALF_K:(h + 1) * HALF_K, m].unsqueeze(2).to_broadcast([P, HALF_K, r.n])
                dve.wait_ge(s.gathered, part + 1)
                for m, r in enumerate(streams):
                    got = bank(k, 4 + m, HALF_K * 2 * r.n).rearrange("p (a x c) -> p a x c", a=HALF_K, x=2)
                    for x in range(2):
                        last = nc.vector.tensor_tensor(rows(x, r), got[:, :, x, :], col(GAIN, m, r), ALU.mult)
                last.then_inc(s.weighted, 1)
                dve.wait_ge(s.weighted, part + 1)
                for m, r in enumerate(streams):
                    for x in range(2):
                        last = nc.vector.tensor_tensor(rows(x, r), rows(x, r), col(SHIFT, m, r), ALU.add)
                last.then_inc(s.xin_ready, 1)

            def sum_up(before):
                for j, (t, half) in enumerate(jobs):
                    dve.wait_ge(s.combined, before + j + 1)
                    x = acc[:, t, half * CHUNK:(half + 1) * CHUNK]
                    nc.vector.tensor_tensor(x, x, bank(k, 6 + j % 2), ALU.add).then_inc(s.added, 1)

            dve.wait_ge(s.cleared, 4 + nt)
            choose(0, 0)
            choose(2, 1)
            modulate(0, 0, 0)
            modulate(1, 0, 1)
            with dve.Fori(0, EXPERTS // ROUND) as it:
                for x in range(ROUND):
                    e = it * ROUND + x
                    for half in range(2):
                        if half == 1:
                            if x % 2 == 0:
                                sum_up(it * (2 * CJ) + x // 2 * CJ)
                            modulate(e + 2, 1 - x // 2, x % 2)
                        dve.wait_ge(s.silued, e * 2 + half + 1)
                        dve.wait_ge(s.up, e * 4 + 2 * half + 2)
                        nc.vector.tensor_tensor(hid[:, half, 0:W], silu[:, half, 0:W], bank(k, 2 * half + 1, W),
                                                ALU.mult).then_inc(s.hid_ready, 1)
                    if x % 2 == 1:
                        dve.wait_ge(s.turned_back, e + 1)
                        choose(it * ROUND + (x // 2 * 2 + 4), x // 2)
                    dve.wait_ge(s.back_copied, e + 1)
                    for half in range(2):
                        dve.wait_ge(s.down, e * 2 + half + 1)
                        row = x % 2
                        for n, r in enumerate(streams):
                            for q in range(r.parts):
                                mine = slice(q * r.n, (q + 1) * r.n)
                                last = nc.vector.tensor_scalar((y2, yc)[n][row * r.n:(row + 1) * r.n, half,
                                                                           q * r.width:(q + 1) * r.width],
                                                               bank(k, 2 + half, r.width, r.at)[mine, :],
                                                               gate_row[mine, row, n:n + 1], None, ALU.mult)
                        last.then_inc(s.y_ready, 1)
            sum_up(EXPERTS // 2 * CJ)
            last_sum = (EXPERTS // 2 + 1) * CJ
            dve.wait_ge(s.added, last_sum)
            w0 = EXPERTS + 2
            for t in range(nt):
                nc.vector.tensor_tensor(acc[:, t, :], acc[:, t, :], k.gates[:, 2 + (t >= LT), :], ALU.mult).then_inc(s.weighted, 1)
                dve.wait_ge(s.weighted, w0 + t + 1)
                nc.vector.tensor_tensor(k.X[:, t, :], k.X[:, t, :], acc[:, t, :], ALU.add).then_inc(s.added, 1)
    k.c += EXPERTS * W_CHUNKS


def expert_layer(k, l, with_ctx):
    nc = k.nc
    A, B, C, E = k.big
    feat = lambda buf: buf[:, :, :].rearrange("p a b -> p (a b)").rearrange("p (a b) -> p a b", a=KD)
    segs = SEGS2 if with_ctx else SEGS2[:1]
    tiles = TILES2 if with_ctx else TILES2[:LT]
    modulated_norm(k, 1, A, feat(B), segs)
    with ExitStack() as mem:
        aff = mem.enter_context(nc.sbuf_tensor(f"aff{l}", [P, LT + CT, EPAD], F32))
        slot = mem.enter_context(nc.sbuf_tensor(f"slot{l}", [P, LT + CT, EPAD], F32))
        route(k, l, feat(B), aff, slot, tiles)
        experts(k, l, A, aff, slot, C, B, E, with_ctx)



CH = 64
PAIRS = 8
DIRS = 2
RATE = math.exp(-0.5)
MIX_R, MIX_W, MIX_K, MIX_V, MIX_A, MIX_G = range(6)
DOUBLINGS = 5


def rwkv_chunks(d):
    lora1 = []
    for n, name in enumerate(("rw_w1_2", "rw_a1_2")):
        for z in range(DIRS):
            at = (DIRS * n + z) * CH
            lora1.append((lambda slot, at=at: slot[:, :, at:at + CH], d[name][0, z].rearrange("(a p) r -> p a r", p=P)))
    lora1.append((lambda slot: slot[:, :, 4 * CH:4 * CH + P], d["rw_g1_2"][0].rearrange("(a p) r -> p a r", p=P)))
    flat = lambda slot: slot.rearrange("p a b -> p (a b)")
    lora2 = [(lambda slot, n=n: flat(slot)[:, n * D:(n + 1) * D],
              d[name][0].rearrange("z r n -> (z r) n")) for n, name in enumerate(("rw_w2_2", "rw_a2_2"))]
    lora2 += [(lambda slot, z=z, h=h: flat(slot)[h * CH:(h + 1) * CH, 2 * D + z * BANK:2 * D + (z + 1) * BANK],
               d["rw_w0_2"][0, z, h * BANK:(h + 1) * BANK].partition_broadcast(CH)) for z in range(DIRS) for h in range(2)]
    halves = lambda name: [columns(d[name][0], n) for n in range(2)]
    return [lora1] + halves("rw_w_r_2") + halves("rw_w_v_2") + halves("rw_w_k_2") + [lora2, [], []] + halves("rw_w_o_2")


def rwkv_project(k, hT, xx, bufs, tw, ta, tg, R, V, K):
    nc = k.nc
    c0 = k.c
    order = [MIX_W, MIX_A, MIX_G, MIX_R, MIX_V, MIX_K]
    xs = [bufs[n] for n in (0, 1, 0, 1, 0, 0)]
    tokens = [(0, SEQ), (SEQ, CTX)]
    jobs = [(0, 0, 0, t) for t in tokens] + [(1, 0, 2 * CH, t) for t in tokens] + [(2, 0, 4 * CH, tokens[0])]
    jobs += [(3, 1 + f // 4, f % 4 * P, tokens[0]) for f in range(KD)]
    jobs += [(4, 3 + n, t * P, None) for n in range(2) for t in range(LT + CT)]
    jobs += [(5, 5 + f // 4, f % 4 * P, t) for f in range(KD) for t in tokens]
    end = [max(j for j, x in enumerate(jobs) if x[0] == m) + 1 for m in range(6)]
    chunk_end = [max(j for j, x in enumerate(jobs) if x[1] == c) + 1 for c in range(7)]
    with stage(k, "shifted mixed product act_out dve_out") as (block, s):
        @block.sync
        def _(sp):
            feed(k, sp, c0, s.product, chunk_end)

        @block.vector
        def _(dve):
            for first, n in tokens:
                h, x = hT[:, :, first:first + n], xx[:, :, first:first + n]
                nc.vector.tensor_tensor(x[:, :, 1:n - 1], h[:, :, 0:n - 2], h[:, :, 2:n], ALU.add)
                nc.vector.tensor_copy(x[:, :, 0:1], h[:, :, 1:2])
                nc.vector.tensor_copy(x[:, :, n - 1:n], h[:, :, n - 2:n - 1]).then_inc(s.shifted, 1)
            dve.wait_ge(s.shifted, 2)
            nc.vector.scalar_tensor_tensor(xx[:, :, :], xx[:, :, :], 0.5, hT[:, :, :], ALU.mult,
                                           ALU.subtract).then_inc(s.shifted, 1)
            dve.wait_ge(s.shifted, 3)

            def mix(m):
                if m >= 2:
                    dve.wait_ge(s.product, end[m - 2] if m < 5 else end[m - 1])
                for a in range(KD):
                    nc.vector.scalar_tensor_tensor(xs[m][:, a, :], xx[:, a, :], k.mix_cols[:, order[m], a:a + 1], hT[:, a, :],
                                                   ALU.mult, ALU.add).then_inc(s.mixed, 1)

            mix(0)
            mix(1)
            for m in range(6):
                out(k, dve, s, jobs, range(end[m - 1] if m else 0, end[m]), 1, tw, ta, tg, R, V, K)
                if m < 3:
                    mix(m + 2)
                elif m == 4:
                    mix(5)

        @block.scalar
        def _(act):
            out(k, act, s, jobs, range(len(jobs)), 0, tw, ta, tg, R, V, K)

        @block.tensor
        def _(pe):
            for j, (m, c, at, moving) in enumerate(jobs):
                w = chunk_here(k, pe, c0 + c)
                pe.wait_ge(s.mixed, KD * (m + 1))
                if j >= BANKS:
                    pe.wait_ge((s.act_out, s.dve_out)[j % 2], (j - BANKS) // 2 + 1)
                for a in range(KD):
                    st = dict(start=a == 0, stop=a == KD - 1)
                    if moving is None:
                        last = nc.tensor.matmul(bank(k, j % BANKS), xs[m][:, a, at:at + P], w[:, a, :], **st)
                    else:
                        first, n = moving
                        last = nc.tensor.matmul(bank(k, j % BANKS, n), w[:, a, at:at + P], xs[m][:, a, first:first + n], **st)
                last.then_inc(s.product, 1)
    k.c += 7


def out(k, eng, s, jobs, which, mine, tw, ta, tg, R, V, K):
    nc = k.nc
    for j in which:
        m, c, at, moving = jobs[j]
        if j % 2 != mine:
            continue
        eng.wait_ge(s.product, j + 1)
        done = (s.act_out, s.dve_out)[mine]
        got = bank(k, j % BANKS)
        copy = (lambda o, i: nc.scalar.activation(o, i, ACT.Copy)) if mine == 0 else nc.vector.tensor_copy
        if moving is None:
            n, t = c - 3, at // P
            for half in range(2):
                for par in range(2):
                    dst = V[par * CH:(par + 1) * CH, 2 * t + half, n * 4:n * 4 + 4, :]
                    src = got[half * CH:(half + 1) * CH, :].rearrange("t (p h i) -> t p h i", p=4, h=2)[:, :, par, :]
                    last = copy(dst, src)
            last.then_inc(done, 1)
            continue
        first, n = moving
        f = (c - 1) % 2 * 4 + at // P
        dst = {0: tw, 1: ta, 2: tg}.get(m)
        dst = dst[:, first:first + n] if dst is not None else (R if m == 3 else K)[:, f, first:first + n]
        copy(dst, got[:, 0:n]).then_inc(done, 1)


def rwkv_keys(k, K, KK, sq, tw, tg):
    nc = k.nc
    GROUP = 4
    QP = P // GROUP
    groups = KD // GROUP
    quarter = lambda a: slice(a % GROUP * QP, (a % GROUP + 1) * QP)
    around = slice((P - QP) // 2, (P + QP) // 2)
    norm = lambda g: sq[:, g * GROUP, :]
    spans = [(0, SEQ), (SEQ, CTX)]
    head_spread = k.gates[:, 1, 0:P]
    with stage(k, "saved table_here scaled squared summed rooted bounded inverted spread done") as (block, s):
        @block.sync
        def _(sp):
            sp.dma_start(head_spread, k.d["head_spread"]).then_inc(s.table_here, 16)
            sp.dma_start(k.x_saved, k.X[:, 0:LT, :]).then_inc(s.saved, 16)
            sp.wait_ge(s.saved, 16)

        @block.scalar
        def _(act):
            for a in range(KD):
                act.wait_ge(s.scaled, a + 1)
                nc.scalar.activation(sq[:, a, :], KK[:, a, :], ACT.Square).then_inc(s.squared, 1)
            for g in range(groups):
                act.wait_ge(s.summed, g + 1)
                nc.scalar.activation(norm(g), bank(k, 2 * g, TOK2), ACT.Sqrt).then_inc(s.rooted, 1)
            nc.scalar.activation(tw[:, :], tw[:, :], ACT.Tanh)
            nc.scalar.activation(tg[:, :], tg[:, :], ACT.Sigmoid)

        @block.tensor
        def _(pe):
            for g in range(groups):
                pe.wait_ge(s.squared, (g + 1) * GROUP)
                for n, (first, width) in enumerate(spans):
                    for a in range(g * GROUP, (g + 1) * GROUP):
                        last = nc.tensor.matmul(bank(k, 2 * g + n, width)[quarter(a), :], k.head_ones[:, around],
                                                sq[:, a, first:first + width], start=True, stop=True)
                last.then_inc(s.summed, 1)
            pe.wait_ge(s.table_here, 16)
            for a in range(KD):
                pe.wait_ge(s.inverted, a // GROUP + 1)
                if a >= 2:
                    pe.wait_ge(s.done, a - 1)
                for n, (first, width) in enumerate(spans):
                    last = nc.tensor.matmul(bank(k, 2 * groups + 2 * (a % 2) + n, width), head_spread[quarter(a), :],
                                            norm(a // GROUP)[quarter(a), first:first + width], start=True, stop=True)
                last.then_inc(s.spread, 1)

        @block.vector
        def _(dve):
            for a in range(KD):
                nc.vector.tensor_scalar(KK[:, a, :], K[:, a, :], k.kk_cols[:, a:a + 1], None, ALU.mult).then_inc(s.scaled, 1)
            dve.wait_ge(s.scaled, KD)
            for g in range(groups):
                dve.wait_ge(s.rooted, g + 1)
                nc.vector.tensor_scalar(norm(g), norm(g), 1e-12, None, ALU.max).then_inc(s.bounded, 1)
                dve.wait_ge(s.bounded, g + 1)
                nc.vector.reciprocal(norm(g), norm(g)).then_inc(s.inverted, 1)
            for a in range(KD):
                dve.wait_ge(s.spread, a + 1)
                nc.vector.tensor_tensor(KK[:, a, :], KK[:, a, :], bank(k, 2 * groups + 2 * (a % 2), TOK2), ALU.mult).then_inc(s.done, 1)


class Events:

    def __init__(self, sem, names, base):
        self.sem, self.names, self.base, self.next = sem, names, base, 0

    def value(self, it, name):
        return it * len(self.names) + (self.base + self.names.index(name) + 1)

    def before(self, it):
        return it * len(self.names) + self.base

    def done(self, ins, name):
        assert self.names[self.next % len(self.names)] == name, name
        self.next += 1
        ins.then_inc(self.sem, 1)


def scan_events(lat):
    late = {3: "ar", 4: "br"} if lat else {}
    pe = ["dec", "iclr", "cumulate"] + (["bonus"] if lat else []) + ["gram_n", "beta_products", "kappa_products"]
    act = ["decay_gate", "iclr_gate", "d_inc", "d_exc", "d_inv", "spread_beta", "spread_kappa", "beta_rows", "spread0", "kappa_rows"]
    dve = ["dec", "iclr", "m", "kt", "akk"] + (["bon", "bonus_in"] if lat else []) + ["alpha", "end"] + \
          (["rho"] if lat else []) + ["beta", "kappa"] + (["bonus"] if lat else []) + ["mask_n", "mask_m", "first", "mask_b"]
    for n in range(1, DOUBLINGS):
        pe += [f"square{n}", f"merged{n}"] + ([f"gram_{late[n]}"] if n in late else [])
        act += [f"square{n}", f"spread{n}"]
        dve += [f"merged{n}", f"product{n}"] + ([f"mask_{late[n]}"] if n in late else [])
    n = DOUBLINGS
    pe += [f"square{n}", f"product{n}", "start", f"product{n + 1}", "sk"] + (["y"] if lat else []) + ["state"]
    act += [f"square{n}", "start", "sk"]
    dve += [f"product{n}", f"product{n + 1}"] + (["y"] if lat else []) + ["state", "decayed"]
    return dict(pe=pe, act=act, dve=dve, pool=["tokens", "rates", "values"])


def rwkv_scan(k, K, KK, R, V, tw, ta, Y, bonus, lora2, tiles, small, wide):
    nc = k.nc
    (T_dec, T_rho, T_ae0, T_mp0, T_beta, T_kappa, T_n, T_brow, T_krow, T_mp1, T_v, T_state) = tiles
    w2, a2, w0, T_ae1 = (lora2[:, n * D:(n + 1) * D] for n in range(4))
    twc, tac, d_end = small
    own = lambda t, z: t[:, z * BANK:(z + 1) * BANK]
    pairs = lambda t, z: own(t, z).rearrange("p (a x) -> p a x", a=PAIRS)
    mp = lambda z: (T_mp0, T_mp1)[z].rearrange("p (a e x) -> p a e x", e=2, x=CH)
    m_of, p_of = (lambda z: mp(z)[:, :, 0, :]), (lambda z: mp(z)[:, :, 1, :])
    n_wide = lambda z: wide[:, z * D:(z + 1) * D].rearrange("p (a h x) -> p a h x", h=2, x=CH)
    k_wide = lambda z: wide[:, (DIRS + z) * D:(DIRS + z + 1) * D].rearrange("p (a h x) -> p a h x", h=2, x=CH)
    ae = lambda z: (T_ae0, T_ae1)[z].rearrange("p (a e x) -> p a e x", e=2, x=CH)
    alpha_of = lambda z: ae(z)[:, :, 0, :]
    side = lambda q, z, e: bank(k, 4 * z + q, 2 * BANK).rearrange("p (a e x) -> p a e x", e=2, x=CH)[:, :, e, :]
    quad = lambda q, z: bank(k, 4 * z + q)
    quad3 = lambda q, z: quad(q, z).rearrange("p (a x) -> p a x", a=PAIRS)
    V2 = V[:, :, :, :].rearrange("p c a i -> p c (a i)")
    Y2 = Y[:, :, :, :].rearrange("p c a i -> p c (a i)")
    phases = [(False, CTX // CH, SEQ, SEQ // CH), (True, SEQ // CH, 0, 0)]

    def columns_of(it, z, steps, first):
        return it * CH + first if z == 0 else it * -CH + (first + (steps - 1) * CH)

    def chunk_of(it, z, steps, first):
        return it + first if z == 0 else it * -1 + (first + steps - 1)

    names = "pe0 pe1 act0 act1 dve0 dve1 pool0 pool1"
    with stage(k, "cleared begun " + names) as (block, s):

        def phase_list():
            base = dict(pe=0, act=0, dve=0, pool=0)
            for lat, steps, first, chunk in phases:
                ev = scan_events(lat)
                yield lat, steps, first, chunk, {n: [Events(s[f"{n}{z}"], ev[n], base[n]) for z in range(DIRS)]
                                                 for n in base}
                for n in base:
                    base[n] += steps * len(ev[n])

        def in_turn(eng, steps, front, both, tail):
            front(0, 0)
            both(0, 0, 1, None, 0)
            with eng.Fori(0, steps - 1) as it:
                both(1, it, 0, it, it + 1)
                both(0, it + 1, 1, it, it + 1)
            both(1, steps - 1, 0, steps - 1, None)
            tail(1, steps - 1)

        @block.gpsimd
        def _(pool):
            nc.gpsimd.memset(T_state, 0.0).then_inc(s.cleared, 1)
            nc.gpsimd.memset(Y2, 0.0).then_inc(s.cleared, 1)
            nc.gpsimd.memset(bonus[:, :, :], 0.0).then_inc(s.cleared, 1)
            nc.gpsimd.memset(wide, 0.0).then_inc(s.cleared, 1)
            for z in range(DIRS):
                nc.gpsimd.tensor_copy(ae(z)[:, :, 1, :], k.eye2[:, :].unsqueeze(1).to_broadcast([P, PAIRS, CH])).then_inc(s.cleared, 1)
            pool.wait_ge(s.cleared, 6)
            for lat, steps, first, chunk, ev in phase_list():
                def front(z, it):
                    mine, lo, c = ev["pool"][z], z * CH, columns_of(it, z, steps, first)
                    pe = ev["pe"][z]
                    if not isinstance(it, int):
                        pool.wait_ge(pe.sem, pe.value(it - 1, "iclr"))
                    elif lat:
                        pool.wait_ge(pe.sem, pe.before(it))
                    mine.done(nc.gpsimd.tensor_copy(twc[lo:lo + CH, :], tw[lo:lo + CH, bass.ds(c, CH)]), "tokens")
                    pool.wait_ge(mine.sem, mine.value(it, "tokens"))
                    mine.done(nc.gpsimd.tensor_copy(tac[lo:lo + CH, :], ta[lo:lo + CH, bass.ds(c, CH)]), "rates")
                    pool.wait_ge(mine.sem, mine.value(it, "rates"))
                    if not isinstance(it, int):
                        pool.wait_ge(pe.sem, pe.before(it))
                    mine.done(nc.gpsimd.tensor_copy(own(T_v, z).unsqueeze(1), V2[:, bass.ds(chunk_of(it, z, steps, chunk), 1), :]),
                              "values")
                    pool.wait_ge(mine.sem, mine.value(it, "values"))

                def both(z, it, y, tail_it, front_it):
                    if front_it is not None:
                        front(y, front_it)

                in_turn(pool, steps, front, both, lambda z, it: None)

        @block.tensor
        def _(pe):
            def heads(q, z, *terms):
                for p in range(PAIRS):
                    for par in range(2):
                        lo = par * CH
                        for n, (lhs, rhs) in enumerate(terms):
                            last = nc.tensor.matmul(quad(q, z)[lo:lo + CH, p * CH:(p + 1) * CH], lhs(z, p)[lo:lo + CH, :],
                                                    rhs(z, p)[lo:lo + CH, :], start=n == 0, stop=n == len(terms) - 1)
                return last

            block_of = lambda t: lambda z, p: pairs(t, z)[:, p, :]
            rho, beta, kappa = (block_of(t) for t in (T_rho, T_beta, T_kappa))
            alpha = lambda z, p: alpha_of(z)[:, p, :]
            m_, n_, p_ = (lambda z, p: m_of(z)[:, p, :]), block_of(T_n), (lambda z, p: p_of(z)[:, p, :])
            b_, ar, br = block_of(T_dec), block_of(T_beta), block_of(T_kappa)
            x_, sk, v_, st = m_, block_of(T_n), block_of(T_v), block_of(T_state)
            brow, krow = block_of(T_brow), block_of(T_krow)
            chunk_here(k, pe, k.c)
            pe.wait_ge(s.cleared, 6)
            for lat, steps, first, chunk, ev in phase_list():
                def wait(sem, value):
                    pe.wait_ge(sem, value)
                    pe.sem_inc(s.begun, 1)

                def after(who, z, it, name):
                    wait(ev[who][z].sem, ev[who][z].value(it, name))

                def pairs_product(q, z, lhs, rhs):
                    for p in range(PAIRS):
                        last = nc.tensor.matmul(bank(k, 4 * z + q, P, p * P), lhs(z)[:, p, :, :].rearrange("p h x -> p (h x)"),
                                                rhs(z)[:, p, :, :].rearrange("p e x -> p (e x)"), start=True, stop=True)
                    return last

                def low_rank(z, it):
                    if lat or not isinstance(it, int):
                        wait(ev["dve"][z].sem, ev["dve"][z].before(it))
                        wait(ev["act"][z].sem, ev["act"][z].before(it))
                    lo = z * CH
                    after("pool", z, it, "tokens")
                    for half in range(2):
                        last = nc.tensor.matmul(quad(0, z)[half * CH:(half + 1) * CH, :], twc[lo:lo + CH, :],
                                                w2[lo:lo + CH, half * BANK:(half + 1) * BANK], start=True, stop=True)
                    ev["pe"][z].done(last, "dec")
                    after("pool", z, it, "rates")
                    for p in range(PAIRS):
                        last = nc.tensor.matmul(quad3(2, z)[:, p, :], a2[lo:lo + CH, p * P:(p + 1) * P], tac[lo:lo + CH, :],
                                                start=True, stop=True)
                    ev["pe"][z].done(last, "iclr")

                def cumulate(z, it):
                    after("act", z, it, "decay_gate")
                    for p in range(PAIRS):
                        lo, at = p // 4 * CH, p % 4 * P
                        last = nc.tensor.matmul(bank(k, 4 * z + p // 4, P, at), own(T_dec, z)[lo:lo + CH, at:at + P],
                                                k.running[lo:lo + CH, z, :], start=True, stop=True)
                    ev["pe"][z].done(last, "cumulate")

                def bonus_sum(z, it):
                    after("dve", z, it, "bonus_in")
                    for p in range(PAIRS):
                        for par in range(2):
                            lo = par * CH
                            last = nc.tensor.matmul(quad(3, z)[lo:lo + CH, p:p + 1], pairs(T_dec, z)[lo:lo + CH, p, :],
                                                    k.head_ones[lo:lo + CH, lo:lo + 1], start=True, stop=True)
                    ev["pe"][z].done(last, "bonus")

                def front(z, it):
                    low_rank(z, it)
                    cumulate(z, it)

                def ends(z, it):
                    mine = ev["pe"][z]
                    after("pool", z, it, "values")
                    after("dve", z, it, "mask_br" if lat else "mask_b")
                    mine.done(heads(3, z, (alpha, st), (b_, v_)), "start")
                    after("act", z, it, f"square{DOUBLINGS}")
                    after("dve", z, it, f"product{DOUBLINGS}")
                    mine.done(heads(2, z, (n_, p_)), f"product{DOUBLINGS + 1}")

                def solve(z, it):
                    after("act", z, it, "start")
                    after("dve", z, it, f"product{DOUBLINGS + 1}")
                    ev["pe"][z].done(heads(0, z, (p_, x_)), "sk")

                def results(z, it):
                    after("act", z, it, "sk")
                    if lat:
                        ev["pe"][z].done(heads(3, z, (rho, st), (ar, sk), (br, v_)), "y")

                def state(z, it):
                    ev["pe"][z].done(heads(1, z, (brow, sk), (krow, v_)), "state")

                def tail(z, it):
                    ends(z, it)
                    solve(z, it)
                    results(z, it)
                    state(z, it)

                def both(z, it, y, tail_it, front_it):
                    mine = ev["pe"][z]
                    if tail_it is not None:
                        ends(y, tail_it)
                    if lat:
                        bonus_sum(z, it)
                    after("dve", z, it, "beta")
                    mine.done(heads(2, z, (alpha, beta)), "gram_n")
                    after("act", z, it, "spread_beta")
                    mine.done(pairs_product(0, z, n_wide, ae), "beta_products")
                    after("dve", z, it, "mask_n")
                    if lat:
                        after("dve", z, it, "bonus")
                    after("act", z, it, "spread_kappa")
                    mine.done(pairs_product(2, z, k_wide, ae), "kappa_products")
                    if tail_it is not None:
                        solve(y, tail_it)
                    after("act", z, it, "beta_rows")
                    after("dve", z, it, "first")
                    for n in range(1, DOUBLINGS):
                        if n > 1:
                            after("act", z, it, f"square{n - 1}")
                            after("dve", z, it, f"merged{n - 1}")
                        mine.done(heads(0, z, (m_, n_)), f"square{n}")
                        if n == 1:
                            after("act", z, it, "kappa_rows")
                            after("dve", z, it, "mask_b")
                        else:
                            after("dve", z, it, f"product{n - 1}")
                            after("act", z, it, f"spread{n - 1}")
                        mine.done(pairs_product(1, z, n_wide, mp), f"merged{n}")
                        if lat and n == 3:
                            mine.done(heads(3, z, (beta, rho)), "gram_ar")
                        elif lat and n == 4:
                            after("dve", z, it, "mask_ar")
                            mine.done(heads(3, z, (kappa, rho)), "gram_br")
                        if n == 1 and tail_it is not None:
                            results(y, tail_it)
                        elif n == 2 and tail_it is not None:
                            state(y, tail_it)
                        if n == 3 and front_it is not None:
                            low_rank(y, front_it)
                        elif n == 4 and front_it is not None:
                            cumulate(y, front_it)
                    n = DOUBLINGS
                    after("act", z, it, f"square{n - 1}")
                    after("dve", z, it, f"merged{n - 1}")
                    mine.done(heads(0, z, (m_, n_)), f"square{n}")
                    after("dve", z, it, f"product{n - 1}")
                    after("act", z, it, f"spread{n - 1}")
                    for p in range(PAIRS):
                        last = nc.tensor.matmul(quad3(1, z)[:, p, :], n_wide(z)[:, p, :, :].rearrange("p h x -> p (h x)"),
                                                p_of(z)[:, p, :], start=True, stop=True)
                    mine.done(last, f"product{n}")

                in_turn(pe, steps, front, both, tail)

        @block.scalar
        def _(act):
            act.wait_ge(s.cleared, 6)
            copy = lambda to, q, z: nc.scalar.activation(own(to, z), quad(q, z), ACT.Copy)
            for lat, steps, first, chunk, ev in phase_list():
                def after(who, z, it, name):
                    act.wait_ge(ev[who][z].sem, ev[who][z].value(it, name))

                def gates(z, it):
                    after("dve", z, it, "dec")
                    ev["act"][z].done(nc.scalar.activation(own(T_dec, z), own(T_dec, z), ACT.Sigmoid), "decay_gate")
                    after("dve", z, it, "iclr")
                    ev["act"][z].done(nc.scalar.activation(own(T_beta, z), own(T_beta, z), ACT.Sigmoid), "iclr_gate")

                def decays(z, it):
                    mine = ev["act"][z]
                    after("pe", z, it, "cumulate")
                    sums = bank(k, 4 * z, 2 * BANK).rearrange("p (a e x) -> p a e x", e=2, x=CH)
                    mine.done(nc.scalar.activation(pairs(T_rho, z), sums[:, :, 0, :], ACT.Exp, scale=-RATE), "d_inc")
                    mine.done(nc.scalar.activation(alpha_of(z), sums[:, :, 1, :], ACT.Exp, scale=-RATE), "d_exc")
                    mine.done(nc.scalar.activation(m_of(z), sums[:, :, 0, :], ACT.Exp, scale=RATE), "d_inv")

                def spread(to, src, z, name):
                    for par in range(2):
                        rows = slice(par * CH, (par + 1) * CH)
                        last = nc.scalar.activation(to(z)[rows, :, par, :], pairs(src, z)[rows], ACT.Copy)
                    ev["act"][z].done(last, name)

                def spreads(z, it):
                    after("dve", z, it, "beta")
                    spread(n_wide, T_beta, z, "spread_beta")
                    after("dve", z, it, "kappa")
                    spread(k_wide, T_kappa, z, "spread_kappa")

                def front(z, it):
                    gates(z, it)
                    decays(z, it)
                    spreads(z, it)

                def start_out(z, it):
                    after("pe", z, it, "start")
                    ev["act"][z].done(nc.scalar.activation(m_of(z), quad3(3, z), ACT.Copy), "start")

                def sk_out(z, it):
                    after("pe", z, it, "sk")
                    ev["act"][z].done(copy(T_n, 0, z), "sk")

                def tail(z, it):
                    start_out(z, it)
                    sk_out(z, it)

                def both(z, it, y, tail_it, front_it):
                    mine = ev["act"][z]
                    if tail_it is not None:
                        start_out(y, tail_it)
                    after("dve", z, it, "mask_m")
                    mine.done(nc.scalar.activation(pairs(T_brow, z), side(0, z, 1), ACT.Copy), "beta_rows")
                    spread(n_wide, T_n, z, "spread0")
                    after("pe", z, it, "kappa_products")
                    mine.done(nc.scalar.activation(pairs(T_krow, z), side(2, z, 1), ACT.Copy), "kappa_rows")
                    if tail_it is not None:
                        sk_out(y, tail_it)
                    for n in range(1, DOUBLINGS + 1):
                        after("pe", z, it, f"square{n}")
                        after("act", z, it, f"spread{n - 1}")
                        mine.done(copy(T_n, 0, z), f"square{n}")
                        if n < DOUBLINGS:
                            after("pe", z, it, f"merged{n}")
                            after("act", z, it, f"square{n}")
                            spread(n_wide, T_n, z, f"spread{n}")
                        if n == 3 and front_it is not None:
                            gates(y, front_it)
                        elif n == 4 and front_it is not None:
                            decays(y, front_it)
                    if front_it is not None:
                        spreads(y, front_it)

                in_turn(act, steps, front, both, tail)

        @block.vector
        def _(dve):
            mask = lambda m, z: m[:, z, :].unsqueeze(1).to_broadcast([P, PAIRS, CH])
            spread = lambda c: c.unsqueeze(2).to_broadcast([P, PAIRS, CH])
            tt, stt = nc.vector.tensor_tensor, nc.vector.scalar_tensor_tensor
            dve.wait_ge(s.cleared, 6)
            for lat, steps, first, chunk, ev in phase_list():
                def after(who, z, it, name):
                    dve.wait_ge(ev[who][z].sem, ev[who][z].value(it, name))

                def tokens(t, z, it):
                    return t[:, :, bass.ds(columns_of(it, z, steps, first), CH)]

                def low_rank(z, it):
                    mine = ev["dve"][z]
                    after("pe", z, it, "dec")
                    mine.done(tt(own(T_dec, z), quad(0, z), own(w0, z), ALU.add), "dec")
                    after("pe", z, it, "iclr")
                    mine.done(tt(pairs(T_beta, z), quad3(2, z), spread(k.a0_cols[:, z * PAIRS:(z + 1) * PAIRS]), ALU.add), "iclr")

                def keys(z, it):
                    mine = ev["dve"][z]
                    after("act", z, it, "iclr_gate")
                    mine.done(stt(pairs(T_kappa, z), pairs(T_beta, z), -1.0, spread(k.ka_cols[:, :]), ALU.add, ALU.mult), "m")
                    after("dve", z, it, "m")
                    mine.done(stt(pairs(T_kappa, z), pairs(T_kappa, z), 1.0, tokens(K, z, it), ALU.add, ALU.mult), "kt")

                def rates(z, it):
                    mine = ev["dve"][z]
                    mine.done(tt(pairs(T_beta, z), pairs(T_beta, z), tokens(KK, z, it), ALU.mult), "akk")
                    if lat:
                        after("pe", z, it, "cumulate")
                        after("dve", z, it, "kt")
                        mine.done(tt(pairs(T_dec, z), pairs(T_kappa, z), tokens(R, z, it), ALU.mult), "bon")
                        after("dve", z, it, "bon")
                        mine.done(tt(pairs(T_dec, z), pairs(T_dec, z), spread(k.rk_cols[:, :]), ALU.mult), "bonus_in")

                def decayed_rows(z, it):
                    mine = ev["dve"][z]
                    after("act", z, it, "d_inv")
                    mine.done(tt(alpha_of(z), alpha_of(z), tokens(KK, z, it), ALU.mult), "alpha")
                    end = CH - 1 if z == 0 else 0
                    mine.done(nc.vector.tensor_copy(d_end[:, z * PAIRS:(z + 1) * PAIRS].unsqueeze(2),
                                                    pairs(T_rho, z)[:, :, end:end + 1]), "end")
                    if lat:
                        after("dve", z, it, "end")
                        mine.done(tt(pairs(T_rho, z), pairs(T_rho, z), tokens(R, z, it), ALU.mult), "rho")

                def raised_rows(z, it):
                    mine = ev["dve"][z]
                    after("dve", z, it, "akk")
                    mine.done(stt(pairs(T_beta, z), pairs(T_beta, z), -1.0, m_of(z), ALU.mult, ALU.mult), "beta")
                    after("dve", z, it, "bon" if lat else "kt")
                    mine.done(tt(pairs(T_kappa, z), pairs(T_kappa, z), m_of(z), ALU.mult), "kappa")

                def meet(z, it, name):
                    if z == 1:
                        after("dve", 0, it, name)
                    else:
                        after("dve", 1, it - 1, name)

                def bonus_out(z, it):
                    after("pe", z, it, "bonus")
                    meet(z, it, "bonus")
                    b = bonus[:, bass.ds(chunk_of(it, z, steps, chunk), 1), :]
                    ev["dve"][z].done(tt(b, b, quad(3, z)[:, 0:PAIRS].unsqueeze(1), ALU.add), "bonus")

                def front(z, it):
                    low_rank(z, it)
                    keys(z, it)
                    rates(z, it)
                    decayed_rows(z, it)
                    raised_rows(z, it)

                def last_factor(z, it):
                    n = DOUBLINGS + 1
                    after("pe", z, it, f"product{n}")
                    after("dve", z, it, f"product{n - 1}")
                    ev["dve"][z].done(tt(p_of(z), p_of(z), quad3(2, z), ALU.add), f"product{n}")

                def results(z, it):
                    mine = ev["dve"][z]
                    if lat:
                        after("pe", z, it, "y")
                        meet(z, it, "y")
                        y = Y2[:, bass.ds(chunk_of(it, z, steps, chunk), 1), :]
                        mine.done(tt(y, y, quad(3, z).unsqueeze(1), ALU.add), "y")

                def state(z, it):
                    mine = ev["dve"][z]
                    after("pe", z, it, "state")
                    mine.done(tt(own(T_state, z), own(T_state, z), quad(1, z), ALU.add), "state")
                    after("dve", z, it, "state")
                    mine.done(tt(pairs(T_state, z), pairs(T_state, z), spread(d_end[:, z * PAIRS:(z + 1) * PAIRS]), ALU.mult),
                              "decayed")

                def tail(z, it):
                    last_factor(z, it)
                    results(z, it)
                    state(z, it)

                def both(z, it, y, tail_it, front_it):
                    mine = ev["dve"][z]
                    if tail_it is not None:
                        last_factor(y, tail_it)
                    if lat:
                        bonus_out(z, it)
                    after("pe", z, it, "gram_n")
                    mine.done(tt(pairs(T_n, z), quad3(2, z), mask(k.before_m, 1 - z), ALU.mult), "mask_n")
                    after("pe", z, it, "beta_products")
                    after("dve", z, it, "kappa")
                    mine.done(tt(m_of(z), side(0, z, 0), mask(k.before_m, z), ALU.mult), "mask_m")
                    mine.done(nc.vector.tensor_copy(p_of(z), k.eye2[:, :].unsqueeze(1).to_broadcast([P, PAIRS, CH])), "first")
                    after("act", z, it, "kappa_rows")
                    mine.done(tt(pairs(T_dec, z), side(2, z, 0), mask(k.before_m, z), ALU.mult), "mask_b")
                    for n in range(1, DOUBLINGS + 1):
                        if n < DOUBLINGS:
                            after("pe", z, it, f"merged{n}")
                            mine.done(nc.vector.tensor_copy(m_of(z), side(1, z, 0)), f"merged{n}")
                            after("dve", z, it, "first" if n == 1 else f"product{n - 1}")
                            mine.done(tt(p_of(z), p_of(z), side(1, z, 1), ALU.add), f"product{n}")
                        else:
                            after("pe", z, it, f"product{n}")
                            after("dve", z, it, f"product{n - 1}")
                            mine.done(tt(p_of(z), p_of(z), quad3(1, z), ALU.add), f"product{n}")
                        if lat and n == 3:
                            after("pe", z, it, "gram_ar")
                            mine.done(tt(pairs(T_beta, z), quad3(3, z), mask(k.upto_m, z), ALU.mult), "mask_ar")
                        elif lat and n == 4:
                            after("pe", z, it, "gram_br")
                            mine.done(tt(pairs(T_kappa, z), quad3(3, z), mask(k.upto_m, z), ALU.mult), "mask_br")
                        if n == 1 and tail_it is not None:
                            results(y, tail_it)
                        elif n == 2 and tail_it is not None:
                            state(y, tail_it)
                        if front_it is not None:
                            if n == 3:
                                low_rank(y, front_it)
                            elif n == 4:
                                keys(y, front_it)
                            elif n == 5:
                                rates(y, front_it)
                                decayed_rows(y, front_it)
                                raised_rows(y, front_it)

                in_turn(dve, steps, front, both, tail)


def rwkv_readout(k, Y, V, bonus, tg, mixT, spare, tables):
    nc = k.nc
    n_chunk = SEQ // CH
    groups = n_chunk * PAIRS
    stat, ln, gateT, g2 = tables
    with stage(k, "g2_here restored vectors_here squared summed rooted step turned gate_made gate_out gated bonused") as (block, s):
        y3 = Y[:, :, :, :].rearrange("p c a i -> p (c a) i")
        v3 = V[:, 0:n_chunk, :, :].rearrange("p c a i -> p (c a) i")
        sq3 = spare.rearrange("p (g i) -> p g i", i=CH)
        over = lambda x: x.unsqueeze(2).to_broadcast([P, groups, CH])

        @block.sync
        def _(sp):
            sp.dma_start(g2, k.d["rw_g2_2"][0]).then_inc(s.g2_here, 16)
            sp.dma_start(k.X[:, 0:LT, :], k.x_saved).then_inc(s.restored, 16)
            for n, name in enumerate(("rw_ln_g_2", "rw_ln_b_2")):
                v = k.d[name][0].rearrange("(a h i) -> h a i", h=2, i=CH)
                for par in range(2):
                    sp.dma_start(ln[par * CH:(par + 1) * CH, n, :].rearrange("p (a i) -> p a i", i=CH),
                                 v[par].partition_broadcast(CH)).then_inc(s.vectors_here, 16)
            sp.wait_ge(s.restored, 16)

        @block.gpsimd
        def _(pool):
            nc.gpsimd.tensor_tensor(v3, v3, over(bonus[:, :, :].rearrange("p c a -> p (c a)")), ALU.mult).then_inc(s.bonused, 1)

        @block.vector
        def _(dve):
            chain = Chain(dve, s.step)
            chain(nc.vector.tensor_reduce(stat[:, 0, :], y3, AX.X, ALU.add))
            chain(nc.vector.tensor_scalar(stat[:, 0, :], stat[:, 0, :], 1.0 / CH, None, ALU.mult))
            chain(nc.vector.tensor_tensor(y3, y3, over(stat[:, 0, :]), ALU.subtract))
            dve.wait_ge(s.squared, 1)
            nc.vector.tensor_reduce(stat[:, 1, :], sq3, AX.X, ALU.add).then_inc(s.summed, 1)
            dve.wait_ge(s.rooted, 1)
            chain(nc.vector.reciprocal(stat[:, 3, :], stat[:, 2, :]))
            chain(nc.vector.tensor_tensor(y3, y3, over(stat[:, 3, :]), ALU.mult))
            yc = Y[:, :, :, :].rearrange("p c a i -> p c (a i)")
            row = lambda n: ln[:, n, :].unsqueeze(1).to_broadcast([P, n_chunk, PAIRS * CH])
            dve.wait_ge(s.vectors_here, 64)
            chain(nc.vector.tensor_tensor(yc, yc, row(0), ALU.mult))
            chain(nc.vector.tensor_tensor(yc, yc, row(1), ALU.add))
            dve.wait_ge(s.bonused, 1)
            chain(nc.vector.tensor_tensor(y3, y3, v3, ALU.add))
            for p in range(PAIRS):
                dve.wait_ge(s.turned, p + 1)
                dve.wait_ge(s.gate_out, p + 1)
                nc.vector.tensor_tensor(mixT[:, p, :], bank(k, p % 4), gateT[:, p % 2, :], ALU.mult).then_inc(s.gated, 1)

        @block.scalar
        def _(act):
            act.wait_ge(s.step, 3)
            nc.scalar.activation(sq3, y3, ACT.Square).then_inc(s.squared, 1)
            act.wait_ge(s.summed, 1)
            nc.scalar.activation(stat[:, 2, :], stat[:, 1, :], ACT.Sqrt, bias=64e-5, scale=1.0 / CH).then_inc(s.rooted, 1)
            for p in range(PAIRS):
                act.wait_ge(s.gate_made, p + 1)
                if p >= 2:
                    act.wait_ge(s.gated, p - 1)
                nc.scalar.activation(gateT[:, p % 2, :], bank(k, 4 + p % 4), ACT.Copy).then_inc(s.gate_out, 1)

        @block.tensor
        def _(pe):
            pe.wait_ge(s.step, 8)
            pe.wait_ge(s.g2_here, 16)
            for p in range(PAIRS):
                if p >= 4:
                    pe.wait_ge(s.gated, p - 3)
                    pe.wait_ge(s.gate_out, p - 3)
                nc.tensor.matmul(bank(k, 4 + p % 4), g2[:, p * P:(p + 1) * P], tg[:, :], start=True,
                                 stop=True).then_inc(s.gate_made, 1)
                for c in range(n_chunk):
                    for par in range(2):
                        lo = par * CH
                        last = nc.tensor.matmul(bank(k, p % 4, CH, c * CH)[lo:lo + CH, :], Y[lo:lo + CH, c, p, :],
                                                k.eye2[lo:lo + CH, :], start=True, stop=True)
                last.then_inc(s.turned, 1)


def hold(k):
    with stage(k, "nothing") as (block, s):
        @block.sync
        def _(sp):
            for c in range(k.c, k.c + 3):
                if c + SLOTS < len(k.chunks):
                    load_chunk(k, sp, c + SLOTS)
    k.c += 3


def rwkv_layer(k):
    nc = k.nc
    A, B, C, E = k.big
    flat = lambda buf: buf[:, :, :].rearrange("p a b -> p (a b)")
    feat = lambda buf: flat(buf).rearrange("p (a b) -> p a b", a=KD)
    modulated_norm(k, 0, B, feat(A), SEGS2)
    with ExitStack() as mem:
        sb = lambda n, shape: mem.enter_context(nc.sbuf_tensor(f"rw_{n}", shape, F32))
        R = sb("R", [P, KD, SEQ])
        twc, tac = sb("twc", [P, CH]), sb("tac", [P, CH])
        d_end = sb("d_end", [P, DIRS * PAIRS])
        bonus = sb("bonus", [P, SEQ // CH, PAIRS])
        low = k.X[:, LT:LT + CT, :].rearrange("p a b -> p (a b)")
        tw, ta, tg = low[:, 0:TOK2], low[:, TOK2:2 * TOK2], low[:, 2 * TOK2:2 * TOK2 + SEQ]
        V = flat(C).rearrange("p (c a i) -> p c a i", c=TOK2 // CH, a=PAIRS)
        rwkv_project(k, feat(A), feat(E), (feat(B), feat(C)), tw, ta, tg, R, V, feat(E))
        K, KK = feat(E), feat(A)
        rwkv_keys(k, K, KK, feat(B), tw, tg)
        Y = flat(B)[:, 0:SEQ // CH * PAIRS * CH].rearrange("p (c a i) -> p c a i", c=SEQ // CH, a=PAIRS)
        left = flat(B)[:, SEQ // CH * PAIRS * CH:]
        slot = lambda n: k.ring[:, (k.c + n) % SLOTS].rearrange("p a b -> p (a b)")
        room = [left[:, 0:D], left[:, D:2 * D], k.gates[:, 1, :], k.gates[:, 3, :]]
        room += [slot(n)[:, x * D:(x + 1) * D] for n in (1, 2) for x in range(4)]
        rwkv_scan(k, K, KK, R, V, tw, ta, Y, bonus, slot(0), room, (twc, tac, d_end),
                  k.X[:, 0:LT, :].rearrange("p a b -> p (a b)"))
        mixT = flat(C)[:, 0:KD * SEQ].rearrange("p (a b) -> p a b", a=KD)
        room = flat(A)
        n = SEQ // CH * PAIRS
        tables = (room[:, 0:4 * n].rearrange("p (a b) -> p a b", a=4), room[:, D:2 * D].rearrange("p (a b) -> p a b", a=2),
                  room[:, 2 * D:3 * D].rearrange("p (a b) -> p a b", a=2), room[:, 3 * D:4 * D])
        rwkv_readout(k, Y, V, bonus, tg, mixT, flat(E)[:, 0:n * CH], tables)
    hold(k)
    add_projection(k, mixT, TILES2[:LT], k.X, lambda t: k.gates[:, 0, :])



def weight_chunks(d, layers):
    chunks = []
    for l in range(DEPTH):
        if f"hybrid{l}" in layers:
            w = d["w_in"][l]
            chunks += [columns(w, n) for n in (0, 1, 4, 5, 2, 6, 3, 7)]
            chunks += [columns(d["w_out"][l], n) for n in range(2)]
    p = {n: d[n + "_2"] for n in ("ada_w", "na_w_qkv", "na_w_o")}
    for l in range(DEPTH):
        if f"ada{l}" in layers:
            chunks += [columns(p["ada_w"][l], n) for n in range(SECTIONS * D // CHUNK)]
        if l == 0 and "na" in layers:
            chunks += [columns(p["na_w_qkv"][0], n) for n in range(6)] + [columns(p["na_w_o"][0], n) for n in range(2)]
        if l == 1 and "rwkv" in layers:
            chunks += rwkv_chunks(d)
        if f"moe{l}" in layers:
            chunks += [[(lambda slot: slot, expert_chunk(d, l, e, j))] for e in range(EXPERTS) for j in range(W_CHUNKS)]
    return chunks


RESIDENT = {
    "ident": [P, P],
    "norm_cols": [P, DEPTH, KD],
}
SECOND_RESIDENT = {
    "cond": [P, KD, 2], "norm1_cols": [P, DEPTH, KD], "norm2_cols": [P, DEPTH, KD], "pick_row": [2, 2, P],
    "na_q_cols": [P, 1], "na_k_cols": [P, 1], "col_mask": [P, GRID],
    "router": [P, DEPTH, KD, EXPERTS], "iota": [P, CAP_L],
    "mix_cols": [P, 6, KD], "kk_cols": [P, KD], "ka_cols": [P, PAIRS], "rk_cols": [P, PAIRS],
    "a0_cols": [P, DIRS * PAIRS], "running": [P, DIRS, 2 * CH], "before_m": [P, DIRS, CH],
    "upto_m": [P, DIRS, CH], "eye2": [P, CH], "head_ones": [P, P],
}
HYBRID_RESIDENT = {
    "rope_cos": [P, TOK], "rope_sin": [P, TOK], "rope_mirror": [P, P], "causal": [P, P],
    "pick_head": [FOX_HEADS, FOX_HEADS, P], "b_forget": [FOX_HEADS, DEPTH],
    "subln_cols": [P, DEPTH, DIFF_HEADS], "lam_vec": [P, DEPTH, 4, HEAD], "w_forget": [P, DEPTH, KD, FOX_HEADS],
}


def resident(k, mem, shapes):
    tiles = {n: mem.enter_context(k.nc.sbuf_tensor(f"{n}_sb", s, F32)) for n, s in shapes.items()}
    k.update(tiles)
    return tiles


def load_resident(k, sp, tiles, here):
    total = 0
    for name, t in tiles.items():
        src = k.d[name]
        if name == "lam_vec":
            src = src.partition_broadcast(P)
        sp.dma_start(t[:], src).then_inc(here, 16)
        total += 16
    return total


def build(nc, d, out, layers, dump):
    k = Named(nc=nc, d=d, stage_no=0, c=0)
    k.chunks = weight_chunks(d, layers)
    k.bias_rows = nc.dram_tensor("bias_rows", [NA_HEADS * REL_ROWS, GRID, PAD], F32).ap()
    k.bias_stored = nc.alloc_semaphore("bias_stored")
    k.x_saved = nc.dram_tensor("x_saved", [P, LT, D], F32).ap()
    with ExitStack() as mem:
        k.psum = mem.enter_context(nc.psum_tensor("psum", [P, BANKS * BANK], F32))
        k.ring = mem.enter_context(nc.sbuf_tensor("ring", [P, SLOTS, KD, CHUNK], F32))
        k.X = mem.enter_context(nc.sbuf_tensor("X", [P, LT + CT, D], F32))
        k.chunk_loaded = [nc.alloc_semaphore(f"chunk_loaded{n}") for n in range(SLOTS)]
        always = resident(k, mem, RESIDENT)
        with ExitStack() as first:
            mine = resident(k, first, HYBRID_RESIDENT)
            with stage(k, "here scaled pad_cleared pad_here") as (block, s):
                pad = k.X[:, LT + CT - 1, 0:2 * PAD].rearrange("p (a c) -> p a c", a=2)

                @block.gpsimd
                def _(pool):
                    nc.gpsimd.memset(pad, 0.0).then_inc(s.pad_cleared, 1)

                @block.sync
                def _(sp):
                    total = load_resident(k, sp, {**always, **mine}, s.here)
                    sp.wait_ge(s.pad_cleared, 1)
                    load_bias(k, sp, pad, s.pad_here)
                    for t in range(LT):
                        sp.dma_start(k.X[:, t, :], d["x"][0, t * P:(t + 1) * P, :]).then_inc(s.here, 16)
                    sp.dma_start(k.X[0:NMETA, LT, :], d["meta_tokens"]).then_inc(s.here, 16)
                    for c in range(min(SLOTS, len(k.chunks))):
                        load_chunk(k, sp, c)
                    sp.wait_ge(s.pad_here, 16)
                    store_bias(k, sp, pad)
                    sp.wait_ge(s.here, total + 16 * (LT + 1))

                @block.vector
                def _(dve):
                    dve.wait_ge(s.here, 16 * (len(always) + len(mine) + LT + 1))
                    for l in range(DEPTH):
                        init = 0.8 - 0.6 * math.exp(-0.3 * l)
                        nc.vector.tensor_scalar(k.subln_cols[:, l, :], k.subln_cols[:, l, :], 1.0 - init, None,
                                                ALU.mult).then_inc(s.scaled, 1)
            for l in range(DEPTH):
                if f"hybrid{l}" in layers:
                    hybrid_layer(k, l)
        with ExitStack() as second:
            sb = lambda n, shape: second.enter_context(nc.sbuf_tensor(n, shape, F32))
            mine = resident(k, second, SECOND_RESIDENT)
            k.big = [sb(f"big{n}", [P, LT + CT, D]) for n in range(4)]
            k.gates = sb("gates", [P, 4, D])
            k.mod_cols = sb("mod_cols", [P, 4, KD, 2])
            k.cond_silu = sb("cond_silu", [P, KD, 2])
            second_start(k, mine, "final" in layers)
            for l in range(DEPTH):
                if f"ada{l}" in layers:
                    modulation(k, l)
                if l == 0 and "na" in layers:
                    neighbour_layer(k, 0)
                if l == 1 and "rwkv" in layers:
                    rwkv_layer(k)
                if f"moe{l}" in layers:
                    expert_layer(k, l, l < DEPTH - 1)
        with k.nc.Block() as block:
            stored = nc.alloc_semaphore("stored")

            @block.sync
            def _(sp):
                for t in range(LT):
                    sp.dma_start(out[0, t * P:(t + 1) * P, :], k.X[:, t, :]).then_inc(stored, 16)
                n = LT
                if dump is not None:
                    sp.dma_start(dump[:, 0:CT * D], k.X[:, LT:LT + CT, :]).then_inc(stored, 16)
                    n += 1
                sp.wait_ge(stored, 16 * n)



def host_arrays(inputs):
    a = {n: np.ascontiguousarray(np.asarray(v)) for n, v in inputs.items()}
    f = np.float32
    a["ident"] = np.eye(P, dtype=f)
    half = HEAD // 2
    inv = f(10000.0) ** (-np.arange(half, dtype=f) / f(half))
    pos = np.concatenate([np.arange(NMETA, TOK), np.arange(NMETA)]).astype(f)
    ang = inv[np.arange(P) % half][:, None] * pos[None, :]
    a["rope_cos"], a["rope_sin"] = np.cos(ang).astype(f), np.sin(ang).astype(f)
    mirror = np.zeros((P, P), f)
    for p in range(P):
        if p % HEAD < half:
            mirror[p + half, p] = -1
        else:
            mirror[p - half, p] = 1
    a["rope_mirror"] = mirror
    a["causal"] = np.where(np.arange(P)[None, :] <= np.arange(P)[:, None], f(0), f(NEG))
    a["pick_head"] = np.repeat(np.eye(FOX_HEADS, dtype=f)[:, :, None], P, axis=2)
    cols = lambda v: np.ascontiguousarray(np.moveaxis(v.reshape(v.shape[:-1] + (-1, P)), -1, 0))
    a["norm_cols"] = cols(a["norm_g"])
    a["subln_cols"] = cols(a["subln_g"])
    a["b_forget"] = np.ascontiguousarray(a["b_forget"].T)
    a["lam_vec"] = np.stack([a["lam_q1"], a["lam_k1"], a["lam_q2"], a["lam_k2"]], axis=1)
    a["w_forget"] = np.ascontiguousarray(a["w_in"][:, :, 4096:].reshape(DEPTH, KD, P, FOX_HEADS).transpose(2, 0, 1, 3))
    a["cond"] = cols(np.stack([a["c_2"][0], a["c_ctx_2"]], axis=0)).transpose(0, 2, 1).copy()
    a["norm1_cols"], a["norm2_cols"] = cols(a["norm1_g_2"]), cols(a["norm2_g_2"])
    a["pick_row"] = np.repeat(np.eye(2, dtype=f)[:, :, None], P, axis=2)
    a["na_q_cols"], a["na_k_cols"] = (np.tile(a[n].T, (2, 1)) for n in ("na_q_g_2", "na_k_g_2"))
    c = np.arange(GRID)
    start = np.clip(c - WIN_COLS // 2, 0, GRID - WIN_COLS)[:, None]
    inside = (c[None, :] >= start) & (c[None, :] < start + WIN_COLS)
    a["col_mask"] = np.tile(np.where(inside, f(0), f(NEG)), (2, 1))
    a["router"] = np.ascontiguousarray(a["moe_router_2"].reshape(DEPTH, KD, P, EXPERTS).transpose(2, 0, 1, 3))
    a["iota"] = np.tile(np.arange(CAP_L, dtype=f), (P, 1))
    s_, t_ = np.meshgrid(np.arange(CH), np.arange(CH), indexing="ij")
    both = lambda fwd, bwd: np.ascontiguousarray(np.tile(np.stack([fwd, bwd], axis=1), (2, 1, 1)).astype(f))
    a["running"] = both(np.hstack([s_ <= t_, s_ < t_]), np.hstack([s_ >= t_, s_ > t_]))
    a["before_m"], a["upto_m"] = both(t_ > s_, t_ < s_), both(t_ >= s_, t_ <= s_)
    a["eye2"] = np.tile(np.eye(CH, dtype=f), (2, 1))
    a["head_ones"] = np.kron(np.eye(2, dtype=f), np.ones((CH, CH), f))
    spread = np.zeros((P // 4, P), f)
    spread[0, :CH], spread[P // 8, CH:] = 1, 1
    a["head_spread"] = np.tile(spread, (4, 1))
    a["mix_cols"], a["kk_cols"] = cols(a["rw_mix_2"][0]), cols(a["rw_k_k_2"][0])
    a["ka_cols"] = cols(a["rw_k_a_2"][0])
    a["rk_cols"] = cols(a["rw_r_k_2"][0].reshape(-1))
    a["a0_cols"] = cols(a["rw_a0_2"][0]).reshape(P, DIRS * PAIRS)
    return a


_TABLES_OF = {
    "norm_g", "subln_g", "lam_q1", "lam_k1", "lam_q2", "lam_k2", "c_2", "c_ctx_2", "norm1_g_2", "norm2_g_2",
    "na_q_g_2", "na_k_g_2", "moe_router_2", "rw_mix_2", "rw_k_k_2", "rw_k_a_2", "rw_r_k_2", "rw_a0_2",
}
_LAYERS = ("hybrid0", "hybrid1", "final", "ada0", "na", "moe0", "ada1", "rwkv", "moe1")


def kernel(**inputs):
    import concourse.bacc as _bacc
    from concourse import mybir as _mybir
    from concourse.bass_utils import run_bass_kernel_spmd as _run

    arrays = {n: v for n, v in host_arrays(inputs).items()
              if n not in _TABLES_OF and not n.startswith(("mla_", "swa_"))}
    nc = _bacc.Bacc("TRN2", target_bir_lowering=False, num_devices=1)
    d = {n: nc.dram_tensor(n, a.shape, _mybir.dt.from_np(a.dtype), kind="ExternalInput").ap() for n, a in arrays.items()}
    out = nc.dram_tensor("out", (1, SEQ, D), F32, kind="ExternalOutput").ap()
    build(nc, d, out, _LAYERS, None)
    r = _run(nc, [arrays], core_ids=[0])
    return r.results[0]["out"]
```
